# Optimizing a Trainium2 kernel written in Bass

```python
import math
import jax, jax.numpy as jnp
from jax import lax
import numpy as np

D_MODEL = 1024
BATCH = 1
SEQ = 512
DEPTH = 1

D_MIX = D_MODEL
D_REC = D_MIX // 2
REC_BLOCKS = 8
REC_BLOCK_DIM = D_REC // REC_BLOCKS
CONV_WIDTH = 4
RG_C = 8.0
N_ATT_HEADS = 4
ATT_HALF_DIM = 64
ATT_V_DIM = 2 * ATT_HALF_DIM
D_ATT = N_ATT_HEADS * ATT_V_DIM
D_QK = N_ATT_HEADS * 2 * ATT_HALF_DIM
D_IN = 2 * D_REC + 2 * D_QK + D_ATT
ROPE_DIM = ATT_HALF_DIM // 4
ROPE_THETA = 500000.0
Q_BLOCK = 128
N_EXPERTS = 64
TOP_K = 8
N_GROUPS = 8
TOPK_GROUPS = 4
D_EXPERT = 256
D_SHARED = 256
ROUTE_SCALE = 2.5
MOE_BLOCK = 128
D_PLE = 256
EPS = 1e-6

kernel_name = "hymba_rglru_diffattn_moe_ple"

def rms_norm(x, g):
    xf = x.astype(jnp.float32)
    y = xf * lax.rsqrt(jnp.mean(xf * xf, axis=-1, keepdims=True) + EPS)
    return (y * g.astype(jnp.float32)).astype(x.dtype)

def rope_tables(positions):
    inv_freq = ROPE_THETA ** (-jnp.arange(0, ROPE_DIM, 2, dtype=jnp.float32) / ROPE_DIM)
    ang = positions.astype(jnp.float32)[..., None] * inv_freq
    return jnp.cos(ang), jnp.sin(ang)

def partial_rope(x, cos, sin):
    half = ROPE_DIM // 2
    c = cos[:, :, None, None, :]
    s = sin[:, :, None, None, :]
    xf = x.astype(jnp.float32)
    x1 = xf[..., :half]
    x2 = xf[..., half:ROPE_DIM]
    out = jnp.concatenate([x1 * c - x2 * s, x2 * c + x1 * s, xf[..., ROPE_DIM:]], axis=-1)
    return out.astype(x.dtype)

def rglru_mixer(xr, gate, conv_w, conv_b, w_a, b_a, w_i, b_i, rg_lambda):
    B, S, _ = xr.shape
    xc = lax.conv_general_dilated(
        xr, conv_w[:, None, :], window_strides=(1,), padding=[(CONV_WIDTH - 1, 0)],
        dimension_numbers=("NWC", "WIO", "NWC"), feature_group_count=D_REC) + conv_b
    xb = xc.reshape(B, S, REC_BLOCKS, REC_BLOCK_DIM)
    r = jax.nn.sigmoid(jnp.einsum("bsgi,gij->bsgj", xb, w_a) + b_a).reshape(B, S, D_REC)
    i = jax.nn.sigmoid(jnp.einsum("bsgi,gij->bsgj", xb, w_i) + b_i).reshape(B, S, D_REC)
    log_a = -RG_C * r.astype(jnp.float32) * jax.nn.softplus(-rg_lambda.astype(jnp.float32))
    a = jnp.exp(log_a)
    mult = jnp.sqrt(-jnp.expm1(2.0 * log_a))
    u = mult * i.astype(jnp.float32) * xc.astype(jnp.float32)

    def combine(left, right):
        a1, b1 = left
        a2, b2 = right
        return a1 * a2, a2 * b1 + b2

    _, h = lax.associative_scan(combine, (a, u), axis=1)
    y = h * jax.nn.gelu(gate.astype(jnp.float32))
    return y.astype(xr.dtype)

def diff_attention(q, k, v, cos, sin, lq1, lk1, lq2, lk2, g_sub, lam_init):
    B, S, _ = q.shape
    H, dh = N_ATT_HEADS, ATT_HALF_DIM
    q = partial_rope(q.reshape(B, S, H, 2, dh), cos, sin)
    k = partial_rope(k.reshape(B, S, H, 2, dh), cos, sin)
    v = v.reshape(B, S, H, ATT_V_DIM)
    f32 = jnp.float32
    lam = (jnp.exp(jnp.sum(lq1.astype(f32) * lk1.astype(f32)))
           - jnp.exp(jnp.sum(lq2.astype(f32) * lk2.astype(f32))) + lam_init)
    kh = k.transpose(0, 2, 3, 1, 4)
    vh = v.transpose(0, 2, 1, 3)
    nb = S // Q_BLOCK
    qb = q.transpose(0, 2, 3, 1, 4).reshape(B, H, 2, nb, Q_BLOCK, dh).transpose(3, 0, 1, 2, 4, 5)
    k_pos = jnp.arange(S)
    scale = dh ** -0.5

    def block(args):
        qblk, bi = args
        s = jnp.einsum("bhcqd,bhckd->bhcqk", qblk, kh).astype(f32) * scale
        q_pos = bi * Q_BLOCK + jnp.arange(Q_BLOCK)
        mask = k_pos[None, :] <= q_pos[:, None]
        s = jnp.where(mask, s, -jnp.inf)
        pr = jax.nn.softmax(s, axis=-1)
        w = pr[:, :, 0] - lam * pr[:, :, 1]
        return jnp.einsum("bhqk,bhkd->bhqd", w.astype(vh.dtype), vh)

    o = lax.map(block, (qb, jnp.arange(nb)))
    o = o.transpose(1, 0, 3, 2, 4).reshape(B, S, H, ATT_V_DIM)
    o = rms_norm(o, g_sub) * (1.0 - lam_init)
    return o.reshape(B, S, D_ATT)

def moe_ffn(h, w_router, e_bias, w1, w3, w2, ws1, ws3, ws2):
    B, S, D = h.shape
    T = B * S
    E, K, M = N_EXPERTS, TOP_K, MOE_BLOCK
    hf = h.reshape(T, D)
    scores = jax.nn.sigmoid((hf @ w_router).astype(jnp.float32))
    sel = scores + e_bias.astype(jnp.float32)
    grp = sel.reshape(T, N_GROUPS, E // N_GROUPS)
    grp_score = lax.top_k(grp, 2)[0].sum(-1)
    _, top_groups = lax.top_k(grp_score, TOPK_GROUPS)
    gmask = jax.nn.one_hot(top_groups, N_GROUPS).sum(1) > 0
    sel = jnp.where(jnp.repeat(gmask, E // N_GROUPS, axis=-1), sel, -jnp.inf)
    _, topi = lax.top_k(sel, K)
    topw = jnp.take_along_axis(scores, topi, axis=-1)
    topw = topw / jnp.sum(topw, axis=-1, keepdims=True) * ROUTE_SCALE
    N = T * K
    e_flat = topi.reshape(N).astype(jnp.int32)
    t_flat = jnp.repeat(jnp.arange(T, dtype=jnp.int32), K)
    w_flat = topw.reshape(N)
    order = jnp.argsort(e_flat)
    e_sorted = e_flat[order]
    t_sorted = t_flat[order]
    w_sorted = w_flat[order]
    counts = jnp.bincount(e_flat, length=E).astype(jnp.int32)
    padded = (counts + M - 1) // M * M
    pad_end = jnp.cumsum(padded)
    pad_start = pad_end - padded
    start = jnp.cumsum(counts) - counts
    dest = pad_start[e_sorted] + jnp.arange(N, dtype=jnp.int32) - start[e_sorted]
    P = N + E * M
    nblk = P // M
    row_token = jnp.zeros((P,), jnp.int32).at[dest].set(t_sorted)
    xbuf = hf[row_token].reshape(nblk, M, D)
    blk_expert = jnp.minimum(
        jnp.searchsorted(pad_end, jnp.arange(nblk, dtype=jnp.int32) * M, side="right"), E - 1)

    def expert_block(args):
        xb, e = args
        return (jax.nn.silu(xb @ w1[e]) * (xb @ w3[e])) @ w2[e]

    ybuf = lax.map(expert_block, (xbuf, blk_expert)).reshape(P, D)
    y_routed = jax.ops.segment_sum(ybuf[dest] * w_sorted[:, None].astype(ybuf.dtype),
                                   t_sorted, num_segments=T)
    y_shared = (jax.nn.silu(hf @ ws1) * (hf @ ws3)) @ ws2
    return (y_routed + y_shared).reshape(B, S, D)

def setup_inputs(seed: int = 0) -> dict:
    key = jax.random.key(seed)
    ks = jax.random.split(key, 32)
    L, D, E, F = DEPTH, D_MODEL, N_EXPERTS, D_EXPERT
    nrm = lambda k, shp, s: jax.random.normal(k, shp, jnp.float32) * s
    gain = lambda k, shp: 1.0 + 0.02 * jax.random.normal(k, shp, jnp.float32)
    a0 = jax.random.uniform(ks[9], (L, D_REC), jnp.float32, 0.9, 0.999)
    s0 = a0 ** (1.0 / RG_C)
    rg_lambda = jnp.log(s0) - jnp.log1p(-s0)
    return {
        "x": nrm(ks[0], (BATCH, SEQ, D), 1.0),
        "p": nrm(ks[1], (DEPTH, BATCH, SEQ, D_PLE), 1.0),
        "positions": jnp.broadcast_to(jnp.arange(SEQ, dtype=jnp.int32)[None, :], (BATCH, SEQ)),
        "ln_mix": gain(ks[2], (L, D)),
        "w_in": nrm(ks[3], (L, D, D_IN), D ** -0.5),
        "conv_w": nrm(ks[4], (L, CONV_WIDTH, D_REC), CONV_WIDTH ** -0.5),
        "conv_b": nrm(ks[5], (L, D_REC), 0.01),
        "w_a": nrm(ks[6], (L, REC_BLOCKS, REC_BLOCK_DIM, REC_BLOCK_DIM), REC_BLOCK_DIM ** -0.5),
        "b_a": nrm(ks[7], (L, REC_BLOCKS, REC_BLOCK_DIM), 0.01),
        "w_i": nrm(ks[8], (L, REC_BLOCKS, REC_BLOCK_DIM, REC_BLOCK_DIM), REC_BLOCK_DIM ** -0.5),
        "b_i": nrm(ks[10], (L, REC_BLOCKS, REC_BLOCK_DIM), 0.01),
        "rg_lambda": rg_lambda,
        "g_rec": gain(ks[11], (L, D_REC)),
        "lq1": nrm(ks[12], (L, ATT_HALF_DIM), 0.1),
        "lk1": nrm(ks[13], (L, ATT_HALF_DIM), 0.1),
        "lq2": nrm(ks[14], (L, ATT_HALF_DIM), 0.1),
        "lk2": nrm(ks[15], (L, ATT_HALF_DIM), 0.1),
        "g_sub": gain(ks[16], (L, ATT_V_DIM)),
        "w_out": nrm(ks[17], (L, D_MIX, D), D_MIX ** -0.5),
        "ln_moe": gain(ks[18], (L, D)),
        "w_router": nrm(ks[19], (L, D, E), D ** -0.5),
        "e_bias": nrm(ks[20], (L, E), 0.01),
        "w1": nrm(ks[21], (L, E, D, F), D ** -0.5),
        "w3": nrm(ks[22], (L, E, D, F), D ** -0.5),
        "w2": nrm(ks[23], (L, E, F, D), F ** -0.5),
        "ws1": nrm(ks[24], (L, D, D_SHARED), D ** -0.5),
        "ws3": nrm(ks[25], (L, D, D_SHARED), D ** -0.5),
        "ws2": nrm(ks[26], (L, D_SHARED, D), D_SHARED ** -0.5),
        "ln_ple": gain(ks[27], (L, D)),
        "w_ple_gate": nrm(ks[28], (L, D, D), D ** -0.5),
        "w_ple_proj": nrm(ks[29], (L, D_PLE, D), D_PLE ** -0.5),
        "ln_f": gain(ks[30], (D,)),
    }

def reference(x, p, positions, ln_mix, w_in, conv_w, conv_b, w_a, b_a, w_i, b_i, rg_lambda,
              g_rec, lq1, lk1, lq2, lk2, g_sub, w_out, ln_moe, w_router, e_bias, w1, w3, w2,
              ws1, ws3, ws2, ln_ple, w_ple_gate, w_ple_proj, ln_f):
    cos, sin = rope_tables(positions)
    h = x
    splits = [D_REC, 2 * D_REC, 2 * D_REC + D_QK, 2 * D_REC + 2 * D_QK]
    for l in range(DEPTH):
        lam_init = 0.8 - 0.6 * math.exp(-0.3 * l)
        hn = rms_norm(h, ln_mix[l])
        z = hn @ w_in[l]
        xr, gate, q, k, v = jnp.split(z, splits, axis=-1)
        y_rec = rms_norm(rglru_mixer(xr, gate, conv_w[l], conv_b[l], w_a[l], b_a[l],
                                     w_i[l], b_i[l], rg_lambda[l]), g_rec[l])
        y_att = diff_attention(q, k, v, cos, sin, lq1[l], lk1[l], lq2[l], lk2[l], g_sub[l], lam_init)
        h = h + jnp.concatenate([y_rec, y_att], axis=-1) @ w_out[l]
        h = h + moe_ffn(rms_norm(h, ln_moe[l]), w_router[l], e_bias[l], w1[l], w3[l], w2[l],
                        ws1[l], ws3[l], ws2[l])
        ple_gate = jax.nn.sigmoid(rms_norm(h, ln_ple[l]) @ w_ple_gate[l])
        h = h + ple_gate * (p[l] @ w_ple_proj[l])
    return rms_norm(h, ln_f)


_drawn_inputs = setup_inputs


def setup_inputs(seed=0):
    import zlib

    import numpy as np

    out = dict(_drawn_inputs(seed))
    spreads = {}
    factors = {'b_a': 4.89, 'b_i': 3.991, 'ln_ple': 166.429, 'ln_f': 21.282}
    for name, (base, spread) in spreads.items():
        noise = np.random.default_rng([zlib.crc32(name.encode()), seed]).standard_normal(out[name].shape)
        drawn = base * np.exp(spread * noise) if base else spread * noise
        out[name] = __import__('jax').numpy.asarray(drawn.astype(out[name].dtype))
    for name, factor in factors.items():
        out[name] = (out[name] * factor).astype(out[name].dtype)
    return out
```

```python
from contextlib import ExitStack

import numpy as np
import concourse.bass as bass
from concourse import mybir

F32 = mybir.dt.float32
BF16 = mybir.dt.bfloat16
U32 = mybir.dt.uint32
I32 = mybir.dt.int32
ALU = mybir.AluOpType
ACT = mybir.ActivationFunctionType
AX_X = mybir.AxisListType.X

P = 128
T = 512
NT = T // P
D = 1024
KC = D // P
BANK = 512
DR = 512
RC = DR // P
H = 4
HALF = 64
DV = 128
ROPE = 16
RH = ROPE // 2
NE = 64
TOPK = 8
NG = 8
GE = NE // NG
TOPG = 4
F = 256
FC = F // P
DPLE = 256
EPS = 1e-6
LAM_INIT = 0.2
ROUTE_SCALE = 2.5
RG_C = 8.0
NEG = -1.0e30
BIG = 1.0e30
NOWHERE = 8192
CHOICES = TOPK * T
MAXB = T // P
MAXX = 34
WSLOT = 2 * KC * F + FC * D
U = 4
GELU_A = 0.044715
GELU_B = 0.7978845608028654


class Chain:

    def __init__(self, eng, sem, base=0):
        self.eng, self.sem, self.base, self.n = eng, sem, base, 0

    def mark(self, ins):
        self.n += 1
        ins.then_inc(self.sem, 1)

    def sync(self):
        self.eng.wait_ge(self.sem, self.base + self.n)

    def link(self, ins):
        self.mark(ins)
        self.sync()


def build_layer(nc, x, p, positions, ln_mix, w_in, conv_w, conv_b, w_a, b_a, w_i, b_i, rg_lambda,
                g_rec, lq1, lk1, lq2, lk2, g_sub, w_out, ln_moe, w_router, e_bias, w1, w3, w2,
                ws1, ws3, ws2, ln_ple, w_ple_gate, w_ple_proj, ln_f, out):
    ctx = ExitStack()
    with ctx:
        def sb(name, shape, dt=F32):
            return ctx.enter_context(nc.sbuf_tensor(name, shape, dt))

        def sem(name):
            return ctx.enter_context(nc.semaphore(name))

        hf_rows = nc.dram_tensor("hf_rows", (T, D), F32, kind="Internal").ap()
        routed = nc.dram_tensor("routed", (CHOICES, D), F32, kind="Internal").ap()

        PS = ctx.enter_context(nc.psum_tensor("PS", [P, 8, BANK], F32))
        h = sb("h", [P, NT, D])
        hT = sb("hT", [P, KC, T])
        WB = sb("WB", [P, U * WSLOT])
        WK = sb("WK", [P, 16384])

        def region(base, at):
            def take(*shape):
                n = int(np.prod(shape))
                v = base[:, at[0]:at[0] + n]
                at[0] += n
                if len(shape) > 1:
                    names = " ".join(f"d{i}" for i in range(len(shape)))
                    v = v.rearrange(f"p ({names}) -> p {names}", **{f"d{i}": s for i, s in enumerate(shape) if i})
                return v
            return take

        wup = [WB[:, s * WSLOT:s * WSLOT + 2 * KC * F].rearrange("p (c w f) -> p c w f", w=2, f=F) for s in range(U)]
        wdn = [WB[:, s * WSLOT + 2 * KC * F:(s + 1) * WSLOT].rearrange("p (c n) -> p c n", n=D) for s in range(U)]

        pre = region(WB, [WSLOT])
        win = pre(2, KC, BANK)
        wab = pre(RC, P)
        wib = pre(RC, P)
        xr = pre(516)
        xc = pre(2, T)
        rg = pre(T)
        ig = pre(T)
        th = pre(T)
        aa = pre(T)
        gs = pre(T)
        gq = pre(T)
        gt = pre(T)
        qk = pre(2, BANK)
        rp = pre(4, 8, RH)
        vv = pre(NT, BANK)
        wk = region(WK, [0])
        qT = wk(H, T)
        kT = wk(H, T)
        ob = wk(4 * H, DV)
        yT = wk(2 * RC, T)
        pr = wk(2, 2, T)
        wb = wk(2, T)
        wT = wk(2, T)
        ysq = wk(RC, T)
        rowbuf = pr.rearrange("p a b t -> p a (b t)")
        lk = region(WK, [0])
        xg = lk(2, D)
        xgT = lk(2, KC, P)
        sgb = lk(2, F)
        hb = lk(2, F)
        hTe = lk(2, FC, P)
        yb = lk(2, D)
        onehot = lk(2, NT * P // 2)
        SL = lk(NT, NE)
        VVf = lk(NT * NE * 6 // 2)
        scores = lk(NT, NE)
        assert 2 * D * 3 <= 8192
        rt = region(WK, [12288])
        sel = rt(NT, NE)
        selm = rt(NT, NE)
        mk = rt(NT, NE)
        ww = rt(NT, NE)
        rr = rt(NT, NE)
        cr = rt(NT, NE)
        g8 = rt(NT, NG, 8)
        gsc = rt(NT, 16)
        gtop = rt(NT, 8)
        gthr = rt(NT, 8)
        grep = rt(NT, 16)
        gmask = rt(NT, NG)
        gpen = rt(NT, NG)
        top8 = rt(NT, 8)
        cnt = rt(NE)
        nxe = rt(MAXB - 1, NE)
        xpos = rt(MAXB - 1, NE)
        xeq = rt(MAXB - 1, NE)
        xev = rt(NE)
        xcol = rt(4)
        xsel = rt(MAXB - 1, NE)
        mkb = rt(NT * NE // 2).bitcast(BF16).rearrange("p (t e) -> p t e", e=NE)
        ohb = onehot.bitcast(BF16).rearrange("p r (c s) -> p r c s", s=P)
        VV = VVf.bitcast(BF16).rearrange("p (t e v) -> p t e v", t=NT, v=6)
        wpg = WB[:, 0:KC * D].rearrange("p (c n) -> p c n", n=D)
        planes = WB[:, KC * D:3 * KC * D].rearrange("p (r j n) -> p r j n", r=2, n=D)
        pk = region(WK, [0])
        prow = pk(NT, DPLE)
        pT = pk(DPLE // P, T)
        wpp = pk(DPLE // P, D)
        sg2 = pk(2, BANK)
        orow = pk(2, D)

        ident = sb("ident", [P, P])
        ones = sb("ones", [P, P])
        cmask = sb("cmask", [P, P])
        slots = sb("slots", [P, MAXB + 1, P])
        tri = sb("tri", [P, P], BF16)
        onesb = sb("onesb", [P, P], BF16)
        junk = WK[:, 15360:16384]
        ojunk = sb("ojunk", [P, DV])
        gain = sb("gain", [P, D])
        wr = sb("wr", [P, KC, NE])
        ebias = sb("ebias", [P, NE])
        posi = sb("posi", [P, NT], I32)
        posf = sb("posf", [P, NT])
        ang = sb("ang", [P, 2, NT, RH])
        kk = sb("kk", [P, 2, NT, RH])
        cs = sb("cs", [P, 2, NT, RH])
        cw = sb("cw", [P, 4, RC])
        cols = sb("cols", [P, 6, RC])
        spt = sb("spt", [P, 4, RC])
        lqk = sb("lqk", [P, 4, HALF])
        ljunk = sb("ljunk", [P, 2, HALF])
        lam = sb("lam", [P, 4])
        gsub = sb("gsub", [P, 1])
        ssq = sb("ssq", [P, 4, NT])
        rstd = sb("rstd", [P, 4, NT])
        oss = sb("oss", [P, 4 * H])
        ors = sb("ors", [P, 4 * H])
        mx = sb("mx", [P, 2, 2])
        nmx = sb("nmx", [P, 2, 2])
        sums = sb("sums", [P, 2, 2])
        rec = sb("rec", [P, 2, 2])
        den = sb("den", [P, NT])
        tlo = sb("tlo", [P, NT])
        pid = sb("pid", [P, 1])
        xtab = sb("xtab", [1, 2, P], I32)
        xnum = sb("xnum", [1, 1], I32)
        ixg = sb("ixg", [P, 2], U32)
        ixd = sb("ixd", [P, 2], U32)
        raw = sb("raw", [P, 4, 6])
        wgt = sb("wgt", [P, 2])
        CB, BA, BI, RL, GR, SP8 = range(6)

        x_in = [sem(f"x_in{t}") for t in range(NT)]
        gain_in = sem("gain_in")
        small_in = sem("small_in")
        bd_in = sem("bd_in")
        win_in = [sem("win_in0"), sem("win_in1")]
        consts = sem("consts")
        bd_zero = sem("bd_zero")
        ssq_done = sem("ssq_done")
        ms_done = sem("ms_done")
        root_done = sem("root_done")
        row_done = sem("row_done")
        row_T = sem("row_T")
        row_evac_a = sem("row_evac_a")
        row_evac_v = sem("row_evac_v")
        dve = sem("dve_steps")
        rope_in = sem("rope_in")
        rope_ready = sem("rope_ready")
        lam_v = sem("lam_v")
        lam_a = sem("lam_a")
        z_full = sem("z_full")
        z_free = sem("z_free")
        rope_done = sem("rope_done")
        qk_T = sem("qk_T")
        qk_evac = sem("qk_evac")
        att_s = sem("att_s")
        att_max = sem("att_max")
        att_exp = sem("att_exp")
        att_w = sem("att_w")
        att_t = sem("att_t")
        att_wt = sem("att_wt")
        att_pv = sem("att_pv")
        att_o = sem("att_o")
        rec_conv = sem("rec_conv")
        rec_la = sem("rec_la")
        rec_ta = sem("rec_ta")
        rec_q = sem("rec_q")
        rec_m = sem("rec_m")
        rec_h = sem("rec_h")
        gate_sq = sem("gate_sq")
        gate_t = sem("gate_t")
        gate_th = sem("gate_th")
        rec_y = sem("rec_y")
        rec_ss = sem("rec_ss")
        mixn_v = sem("mixn_v")
        mixn_a = sem("mixn_a")
        y_ready = sem("y_ready")
        o_norm = sem("o_norm")
        o_T = sem("o_T")
        mix_full = sem("mix_full")
        h1_done = sem("h1_done")
        hf_stored = [sem("hf_stored0"), sem("hf_stored1")]
        rt_full = sem("rt_full")
        rt_sig = sem("rt_sig")
        mk_done = sem("mk_done")
        rank_full = sem("rank_full")
        routes = sem("routes")
        xlist = sem("xlist")
        xrow = sem("xrow")
        wr_in = sem("wr_in")
        sw_in = sem("sw_in")
        sh_up = sem("sh_up")
        sh_sig = sem("sh_sig")
        sh_h = sem("sh_h")
        sh_T = sem("sh_T")
        sh_hT = sem("sh_hT")
        sh_dn = sem("sh_dn")
        sh_add = sem("sh_add")
        xg_zero = sem("xg_zero")
        up_in = [sem(f"up_in{s}") for s in range(U)]
        dn_in = [sem(f"dn_in{s}") for s in range(U)]
        pool_ready = sem("pool_ready")
        oh_done = sem("oh_done")
        ix_full = sem("ix_full")
        ix_done = sem("ix_done")
        dest_done = sem("dest_done")
        gathered = [sem("gathered0"), sem("gathered1")]
        tx_full = sem("tx_full")
        tx_evac = sem("tx_evac")
        up_full = sem("up_full")
        sg_done = sem("sg_done")
        ht_step = sem("ht_step")
        h_done = sem("h_done")
        ht_full = sem("ht_full")
        ht_evac = sem("ht_evac")
        dn_full = sem("dn_full")
        y_evac_a = sem("y_evac_a")
        y_evac_v = sem("y_evac_v")
        scattered = [sem("scattered0"), sem("scattered1")]
        experts_done_v = sem("experts_done_v")
        experts_done_a = sem("experts_done_a")
        experts_done_t = sem("experts_done_t")
        x_up_in = [sem("x_up_in0"), sem("x_up_in1")]
        x_dn_in = [sem("x_dn_in0"), sem("x_dn_in1")]
        x_oh = sem("x_oh")
        x_ix = sem("x_ix")
        x_ixd = sem("x_ixd")
        x_gathered = [sem("x_gathered0"), sem("x_gathered1")]
        x_tx = sem("x_tx")
        x_txe = sem("x_txe")
        x_up = sem("x_up")
        x_sg = sem("x_sg")
        x_step = sem("x_step")
        x_h = sem("x_h")
        x_ht = sem("x_ht")
        x_hte = sem("x_hte")
        x_dn = sem("x_dn")
        x_ya = sem("x_ya")
        x_yv = sem("x_yv")
        x_scattered = [sem("x_scattered0"), sem("x_scattered1")]
        routed_done = sem("routed_done")
        wpg_in = sem("wpg_in")
        pw_in = sem("pw_in")
        plane_in = [sem("plane_in0"), sem("plane_in1")]
        plane_used = sem("plane_used")
        p_T = sem("p_T")
        p_evac = sem("p_evac")
        pg_full = sem("pg_full")
        pg_sig = sem("pg_sig")
        pp_full = sem("pp_full")
        ple_mul = sem("ple_mul")
        ple_done = sem("ple_done")
        orow_done = sem("orow_done")
        stored = [sem("stored0"), sem("stored1")]

        block = ctx.enter_context(nc.Block())

        ring = [("qkv", n) for n in range(3 * NT)]
        for k in range(2 * RC):
            ring.append(("Z", k))
            if 1 <= k <= RC:
                ring += [("R", k - 1), ("I", k - 1)]
        ring_at = {u: n for n, u in enumerate(ring)}
        NSLOT = 2 * RC + 1
        NS = 4 * H
        HALVES = 2

        w_in_v = w_in[0].rearrange("(p c) n -> p c n", c=KC)
        w_out_v = w_out[0].rearrange("(c p) n -> p c n", p=P)
        x_v = x[0].rearrange("(t p) n -> t p n", p=P)
        out_v = out[0].rearrange("(t p) n -> t p n", p=P)
        p_v = p[0, 0].rearrange("(t p) n -> t p n", p=P)
        hf_v = hf_rows.rearrange("(t p) n -> t p n", p=P)
        routed_v = routed.rearrange("(j t p) n -> t p j n", j=TOPK, p=P)
        WIN_COLS = [2 * DR, 2 * DR + 512, 2 * DR + 1024, 0, DR]
        WIN_UNITS = [NT, 2 * NT, 3 * NT, ring_at[("Z", RC - 1)] + 1, ring_at[("Z", 2 * RC - 1)] + 1]

        def expert_up(e):
            return (w1[0, bass.ds(e, 1)].rearrange("a (p c) f -> p (a c) f", c=KC),
                    w3[0, bass.ds(e, 1)].rearrange("a (p c) f -> p (a c) f", c=KC))

        def expert_dn(e):
            return w2[0, bass.ds(e, 1)].rearrange("a (p c) n -> p (a c) n", c=FC)

        def scatters_before(e, s):
            return 16 * (e // 2) if isinstance(e, int) else (e - s) * 8 + 16 * (s // 2)

        def main_done(eng):
            for done, n in ((up_full, NE), (dn_full, HALVES * NE), (h_done, NE), (ix_full, NE), (ix_done, 2 * NE), (dest_done, 2 * NE),
                            (tx_full, HALVES * NE), (tx_evac, HALVES * NE), (ht_full, NE), (ht_evac, NE),
                            (y_evac_a, NE), (y_evac_v, NE), (scattered[0], 8 * NE), (scattered[1], 8 * NE)):
                eng.wait_ge(done, n)

        @block.sync
        def _(eng):
            for t in range(NT):
                eng.dma_start(h[:, t, :], x_v[t]).then_inc(x_in[t], 16)

            def load_win(n):
                if n >= 2:
                    eng.wait_ge(z_full, WIN_UNITS[n - 2])
                src = w_in_v[:, :, WIN_COLS[n]:WIN_COLS[n] + BANK] if n < 5 else \
                    w_out_v[:, :, (n - 5) * BANK:(n - 4) * BANK]
                eng.dma_start(win[:, n % 2], src).then_inc(win_in[n % 2], 16)

            load_win(0)
            load_win(1)

            def load_up(e, s):
                for j, src in enumerate(expert_up(e)):
                    eng.dma_start(wup[s][:, :, j, :], src).then_inc(up_in[s], 16)

            def load_dn(e, s):
                eng.dma_start(wdn[s], expert_dn(e)).then_inc(dn_in[s], 16)

            load_up(0, 0)
            load_dn(0, 0)
            for n in range(2, 7):
                load_win(n)
            def store_row(t):
                eng.wait_ge(row_done, NT + t + 1)
                eng.dma_start(hf_v[t], rowbuf[:, t % 2, :]).then_inc(hf_stored[t % 2], 16)
            eng.wait_ge(mix_full, NT * HALVES)
            eng.dma_start(wup[3][:, :, 0, :], ws1[0].rearrange("(p c) f -> p c f", c=KC)).then_inc(sw_in, 16)
            eng.dma_start(wup[3][:, :, 1, :], ws3[0].rearrange("(p c) f -> p c f", c=KC)).then_inc(sw_in, 16)
            eng.dma_start(wdn[3], ws2[0].rearrange("(p c) n -> p c n", c=FC)).then_inc(sw_in, 16)
            for t in range(NT):
                store_row(t)
            for s in (1, 2):
                load_up(s, s)
                load_dn(s, s)
            eng.wait_ge(sh_dn, NT * HALVES)
            load_up(3, 3)
            load_dn(3, 3)

            def refill(e, s, read_before):
                up_src, dn_src = expert_up(e), expert_dn(e)
                dn_read = eng.snap(read_before * HALVES)
                eng.wait_ge(up_full, read_before)
                for j, src in enumerate(up_src):
                    eng.dma_start(wup[s][:, :, j, :], src).then_inc(up_in[s], 16)
                eng.wait_ge(dn_full, dn_read)
                eng.dma_start(wdn[s], dn_src).then_inc(dn_in[s], 16)

            with eng.Fori(1, NE // U) as i:
                for s in range(U):
                    e = eng.snap(i * U + s)
                    read_before = eng.snap(e - (U - 1))
                    refill(e, s, read_before)

            main_done(eng)
            pairs = eng.value_load(xnum[0:1, 0:1], min_val=0, max_val=MAXX // 2)
            with eng.If(pairs > 0):
                with eng.Fori(0, pairs) as i:
                    for j in range(2):
                        e = eng.value_load(xtab[0:1, 0, bass.ds(i * 2 + j, 1)], min_val=0, max_val=NE - 1)
                        up_src, dn_src = expert_up(e), expert_dn(e)
                        up_read, dn_read = eng.snap(i * 2), eng.snap(i * 4)
                        eng.wait_ge(x_up, up_read)
                        for w, src in enumerate(up_src):
                            eng.dma_start(wup[j][:, :, w, :], src).then_inc(x_up_in[j], 16)
                        eng.wait_ge(x_dn, dn_read)
                        eng.dma_start(wdn[j], dn_src).then_inc(x_dn_in[j], 16)
            with eng.Else():
                eng.nop()
            eng.wait_ge(experts_done_t, 1)

            eng.dma_start(wpg, w_ple_gate[0].rearrange("(p c) n -> p c n", c=KC)).then_inc(wpg_in, 16)
            eng.wait_ge(experts_done_v, 1)
            eng.wait_ge(experts_done_a, 1)
            eng.wait_ge(routed_done, 2)
            eng.dma_start(wpp, w_ple_proj[0].rearrange("(p c) n -> p c n", c=DPLE // P)).then_inc(pw_in, 16)
            eng.dma_start(prow, p_v.rearrange("t p n -> p t n")).then_inc(pw_in, 16)
            for t in range(NT):
                if t >= 2:
                    eng.wait_ge(plane_used, t - 1)
                eng.dma_start(planes[:, t % 2], routed_v[t]).then_inc(plane_in[t % 2], 16)
            for t in range(NT):
                eng.wait_ge(orow_done, t + 1)
                eng.dma_start(out_v[t], orow[:, t % 2, :]).then_inc(stored[t % 2], 16)
            for r in range(2):
                eng.wait_ge(stored[r], 16 * NT // 2)

        @block.scalar
        def _(eng):
            act = nc.scalar

            def small(dst, src):
                with nc.allow_non_contiguous_dma(reason="small columns"):
                    eng.dma_start(dst, src).then_inc(small_in, 16)

            def rows(dst, src):
                eng.dma_start(dst, src.to_broadcast([P, src.shape[1]])).then_inc(small_in, 16)

            def load_gain(src):
                eng.dma_start(gain[:, :], src.to_broadcast([P, D])).then_inc(gain_in, 16)

            load_gain(ln_mix)
            with nc.allow_non_contiguous_dma(reason="a number for each token"):
                eng.dma_start(posi[:, :], positions[0].rearrange("(t p) -> p t", p=P)).then_inc(rope_in, 16)
            for j, v in enumerate((lq1, lk1, lq2, lk2)):
                rows(lqk[:, j, :], v)
            small(cw[:, :, :], conv_w[0].rearrange("w (c p) -> p w c", p=P))
            small(cols[:, CB, :], conv_b[0].rearrange("(c p) -> p c", p=P))
            small(cols[:, BA, :], b_a[0].rearrange("(c b) j -> (b j) c", b=2))
            small(cols[:, BI, :], b_i[0].rearrange("(c b) j -> (b j) c", b=2))
            small(cols[:, RL, :], rg_lambda[0].rearrange("(c p) -> p c", p=P))
            small(cols[:, GR, :], g_rec[0].rearrange("(c p) -> p c", p=P))
            small(gsub[:, :], g_sub[0].rearrange("(d a) -> d a", a=1))
            rows(ebias[:, :], e_bias)
            eng.wait_ge(bd_zero, 2)
            for b in range(2):
                for dst, src in ((wab, w_a), (wib, w_i)):
                    eng.dma_start(dst[b * HALF:(b + 1) * HALF, :, b * HALF:(b + 1) * HALF],
                                  src[0].rearrange("(c b) i j -> b i c j", b=2)[b]).then_inc(bd_in, 16)
            eng.dma_start(wr[:, :, :], w_router[0].rearrange("(p c) e -> p c e", c=KC)).then_inc(wr_in, 16)

            def squares(n, t):
                if n or t:
                    eng.wait_ge(ssq_done, NT * n + t)
                act.activation(junk, h[:, t, :], ACT.Square, accum_out=ssq[:, n, t:t + 1]).then_inc(ssq_done, 1)

            def root(n, t):
                eng.wait_ge(ms_done, NT * n + t + 1)
                act.activation(rstd[:, n, t:t + 1], rstd[:, n, t:t + 1], ACT.Sqrt).then_inc(root_done, 1)

            def row_evac(n, t):
                eng.wait_ge(row_T, HALVES * (NT * n + t) + 1)
                act.activation(hT[:, 0:4, t * P:(t + 1) * P],
                               PS[:, (2 * t) % 4, :].rearrange("p (c n) -> p c n", n=P), ACT.Copy).then_inc(row_evac_a, 1)

            for t in range(NT):
                eng.wait_ge(x_in[t], 16)
                squares(0, t)
            for t in range(NT):
                root(0, t)
                row_evac(0, t)
            eng.wait_ge(rope_ready, 1)
            act.activation(cs[:, :, :, :], ang[:, :, :, :], ACT.Sin).then_inc(rope_ready, 1)
            eng.wait_ge(lam_v, 3)
            act.activation(lam[:, 2:4], lam[:, 0:2], ACT.Exp).then_inc(lam_a, 1)
            act.activation(spt[:, 1, :], spt[:, 0, :], ACT.Exp).then_inc(lam_a, 1)

            for n in range(3 * NT):
                eng.wait_ge(z_full, n + 1)
                if n < 2 * NT:
                    if n >= 2:
                        eng.wait_ge(qk_T, n - 1)
                    dst = qk[:, n % 2, :]
                else:
                    dst = vv[:, n - 2 * NT, :]
                act.activation(dst, PS[:, n % 2, :], ACT.Copy).then_inc(z_free, 1)

            def evac_z(k):
                n = ring_at[("Z", k)]
                eng.wait_ge(z_full, n + 1)
                if k < RC:
                    if k == 0:
                        eng.wait_ge(bd_zero, 3)
                    else:
                        eng.wait_ge(rec_conv, k)
                    act.activation(xr[:, 3:3 + T], PS[:, n % 2, :], ACT.Copy).then_inc(z_free, 1)
                else:
                    if k > RC:
                        eng.wait_ge(rec_y, k - RC)
                    act.activation(gs, PS[:, n % 2, :], ACT.Copy).then_inc(z_free, 1)
                    eng.wait_ge(z_free, n + 1)
                    act.activation(gq, gs, ACT.Square).then_inc(gate_sq, 1)

            def gates(c):
                for what, dst, bias in (("R", rg, BA), ("I", ig, BI)):
                    n = ring_at[(what, c)]
                    eng.wait_ge(z_full, n + 1)
                    if c:
                        eng.wait_ge(rec_h, c)
                    act.activation(dst, PS[:, n % 2, :], ACT.Sigmoid, bias=cols[:, bias, c:c + 1]).then_inc(z_free, 1)

            def exps(s):
                i = s // H
                nk = (i + 1) * P
                eng.wait_ge(att_max, s + 1)
                if s >= 2:
                    eng.wait_ge(att_w, s - 1)
                for c in range(2):
                    act.activation(pr[:, s % 2, c, 0:nk], PS[:, 2 + 2 * (s % 2) + c, 0:nk], ACT.Exp,
                                   bias=nmx[:, s % 2, c:c + 1], scale=HALF ** -0.5,
                                   accum_out=sums[:, s % 2, c:c + 1]).then_inc(att_exp, 1)

            def evac_wT(s):
                nk = (s // H + 1) * P
                eng.wait_ge(att_t, s + 1)
                if s >= 2:
                    eng.wait_ge(att_pv, s - 1)
                act.activation(wT[:, s % 2, 0:nk], PS[:, 6 + s % 2, 0:nk], ACT.Copy).then_inc(att_wt, 1)

            def evac_o(s):
                eng.wait_ge(att_pv, s + 1)
                act.activation(ob[:, s, :], PS[:, 6 + s % 2, 0:DV], ACT.Copy).then_inc(att_o, 1)
                if s:
                    eng.wait_ge(att_o, 2 * s)
                act.activation(ojunk[:, :], PS[:, 6 + s % 2, 0:DV], ACT.Square,
                               accum_out=oss[:, s:s + 1]).then_inc(att_o, 1)

            eng.wait_ge(ssq_done, NT)
            for k in range(NSLOT):
                if k < 2 * RC:
                    evac_z(k)
                if 1 <= k <= RC:
                    gates(k - 1)
                if k < 8:
                    exps(2 * k)
                    exps(2 * k + 1)
                if 1 <= k <= RC:
                    c = k - 1
                    eng.wait_ge(rec_la, c + 1)
                    act.activation(th, rg, ACT.Tanh).then_inc(rec_ta, 1)
                    act.activation(aa, rg, ACT.Exp, scale=-1.0).then_inc(rec_ta, 1)
                if k >= 1:
                    evac_wT(2 * k - 2)
                    evac_wT(2 * k - 1)
                    evac_o(2 * k - 2)
                    evac_o(2 * k - 1)
                if 1 <= k <= RC:
                    eng.wait_ge(rec_q, k)
                    act.activation(th, th, ACT.Sqrt, scale=2.0).then_inc(rec_m, 1)
                if RC <= k < 2 * RC:
                    eng.wait_ge(gate_t, k - RC + 1)
                    act.activation(gq, gt, ACT.Tanh, scale=GELU_B).then_inc(gate_th, 1)
            eng.wait_ge(mixn_v, 1)
            act.activation(ors[:, :], ors[:, :], ACT.Sqrt).then_inc(mixn_a, 1)
            eng.wait_ge(mixn_v, 2)
            act.activation(gs, gs, ACT.Sqrt).then_inc(mixn_a, 1)

            load_after = [ln_moe, ln_ple, ln_f]
            eng.wait_ge(row_done, NT)
            load_gain(load_after[0])
            for t in range(NT):
                eng.wait_ge(h1_done, HALVES * (t + 1))
                squares(1, t)
                root(1, t)
                if t:
                    row_evac(1, t - 1)
            row_evac(1, NT - 1)
            eng.wait_ge(row_done, 2 * NT)
            load_gain(load_after[1])
            eng.wait_ge(rt_full, NT)
            act.activation(scores, PS[:, 4, 0:NT * NE].rearrange("p (t e) -> p t e", e=NE), ACT.Sigmoid).then_inc(rt_sig, 1)

            for t in range(NT + 1):
                if t < NT:
                    eng.wait_ge(sh_up, t + 1)
                    if t >= 2:
                        eng.wait_ge(sh_h, t - 1)
                    act.activation(sgb[:, t % 2, :], PS[:, 6 + t % 2, 0:F], ACT.Sigmoid).then_inc(sh_sig, 1)
                if t:
                    eng.wait_ge(sh_T, t)
                    if t >= 3:
                        eng.wait_ge(sh_dn, HALVES * (t - 2))
                    act.activation(hTe[:, (t - 1) % 2], PS[:, 2 + (t - 1) % 2, 0:F].rearrange("p (c n) -> p c n", n=P),
                                   ACT.Copy).then_inc(sh_hT, 1)

            def tx(e, s):
                for j in range(HALVES):
                    eng.wait_ge(tx_full, HALVES * e + j + 1)
                    if not isinstance(e, int) or e >= 2:
                        eng.wait_ge(up_full, e - 1)
                    act.activation(xgT[:, s % 2, 4 * j:4 * j + 4, :],
                                   PS[:, 2 + j, :].rearrange("p (c n) -> p c n", n=P), ACT.Copy).then_inc(tx_evac, 1)

            def sig(e, s):
                eng.wait_ge(up_full, e + 1)
                if not isinstance(e, int) or e >= 2:
                    eng.wait_ge(h_done, e - 1)
                act.activation(sgb[:, s % 2, :], PS[:, s % 2, 0:F], ACT.Sigmoid).then_inc(sg_done, 1)

            def down_evacs(e, s):
                eng.wait_ge(ht_full, e + 1)
                if not isinstance(e, int) or e >= 2:
                    eng.wait_ge(dn_full, HALVES * (e - 1))
                act.activation(hTe[:, s % 2], PS[:, 4, 0:F].rearrange("p (c n) -> p c n", n=P), ACT.Copy).then_inc(ht_evac, 1)
                eng.wait_ge(dn_full, HALVES * e + 1)
                if not isinstance(e, int) or e >= 2:
                    eng.wait_ge(scattered[s % 2], scatters_before(e, s))
                eng.wait_ge(dest_done, 2 * e + 2)
                act.activation(yb[:, s % 2, 0:BANK], PS[:, 6, :], ACT.Copy, scale=wgt[:, s % 2:s % 2 + 1]).then_inc(y_evac_a, 1)

            def turn(e, s, first=False, last=False):
                if not last:
                    tx(e + 1, (s + 1) % U)
                sig(e, s)
                if not first:
                    down_evacs(e - 1, (s - 1) % U)

            eng.wait_ge(sh_h, NT)
            eng.wait_ge(sh_dn, NT * HALVES)
            tx(0, 0)
            for s in range(U):
                turn(s, s, first=(s == 0))
            with eng.Fori(1, NE // U - 1) as i:
                for s in range(U):
                    turn(i * U + s, s)
            for s in range(U):
                turn(NE - U + s, s, last=(s == U - 1))
            down_evacs(NE - 1, U - 1)
            main_done(eng)

            pairs = eng.value_load(xnum[0:1, 0:1], min_val=0, max_val=MAXX // 2)
            with eng.If(pairs > 0):
                with eng.Fori(0, pairs) as i:
                    for j in range(2):
                        for n in range(HALVES):
                            eng.wait_ge(x_tx, i * 4 + (2 * j + n + 1))
                            eng.wait_ge(x_up, i * 2)
                            act.activation(xgT[:, j, 4 * n:4 * n + 4, :],
                                           PS[:, 4 * j + 2 + n, :].rearrange("p (c n) -> p c n", n=P), ACT.Copy).then_inc(x_txe, 1)
                    for j in range(2):
                        eng.wait_ge(x_up, i * 2 + (j + 1))
                        eng.wait_ge(x_h, i * 2)
                        act.activation(sgb[:, j, :], PS[:, j, 0:F], ACT.Sigmoid).then_inc(x_sg, 1)
                    for j in range(2):
                        eng.wait_ge(x_ht, i * 2 + (j + 1))
                        eng.wait_ge(x_dn, i * 4)
                        act.activation(hTe[:, j], PS[:, 4, 0:F].rearrange("p (c n) -> p c n", n=P), ACT.Copy).then_inc(x_hte, 1)
                        eng.wait_ge(x_dn, i * 4 + (2 * j + 1))
                        eng.wait_ge(x_scattered[j], i * 16)
                        act.activation(yb[:, j, 0:BANK], PS[:, 6, :], ACT.Copy, scale=wgt[:, j:j + 1]).then_inc(x_ya, 1)
                eng.wait_ge(x_ya, pairs * 2)
                eng.sem_inc(experts_done_a, 1)
            with eng.Else():
                eng.sem_inc(experts_done_a, 1)

            for t in range(NT):
                eng.wait_ge(plane_used, t + 1)
                squares(2, t)
                root(2, t)
                if t:
                    row_evac(2, t - 1)
            row_evac(2, NT - 1)
            eng.wait_ge(row_done, 3 * NT)
            load_gain(load_after[2])
            for u in range(NT * HALVES):
                eng.wait_ge(pg_full, u + 1)
                if u >= 2:
                    eng.wait_ge(ple_mul, u - 1)
                act.activation(sg2[:, u % 2, :], PS[:, 4 + u % 2, :], ACT.Sigmoid).then_inc(pg_sig, 1)
                if u % 2 == 1:
                    t = u // 2
                    eng.wait_ge(ple_done, u + 1)
                    squares(3, t)
                    root(3, t)

        @block.vector
        def _(eng):
            v = nc.vector
            ch = Chain(eng, dve)

            def mean_square(n, t):
                eng.wait_ge(ssq_done, NT * n + t + 1)
                v.tensor_scalar(rstd[:, n, t:t + 1], ssq[:, n, t:t + 1], 1.0 / D, EPS, ALU.mult, ALU.add).then_inc(ms_done, 1)

            def row(n, t, dst):
                eng.wait_ge(root_done, NT * n + t + 1)
                ch.link(v.reciprocal(rstd[:, n, t:t + 1], rstd[:, n, t:t + 1]))
                eng.wait_ge(gain_in, 16 * (n + 1))
                return v.scalar_tensor_tensor(out=dst, in0=h[:, t, :], scalar=rstd[:, n, t:t + 1], in1=gain[:, :],
                                              op0=ALU.mult, op1=ALU.mult)

            def row_evac(n, t):
                eng.wait_ge(row_T, HALVES * (NT * n + t) + 2)
                v.tensor_copy(hT[:, 4:8, t * P:(t + 1) * P],
                              PS[:, (2 * t + 1) % 4, :].rearrange("p (c n) -> p c n", n=P)).then_inc(row_evac_v, 1)

            for t in range(NT):
                mean_square(0, t)
            for t in range(NT):
                if t >= 2:
                    eng.wait_ge(row_T, HALVES * (t - 1))
                row(0, t, rowbuf[:, t % 2, :]).then_inc(row_done, 1)
                if t:
                    row_evac(0, t - 1)
            row_evac(0, NT - 1)

            inv = [float(np.float32(500000.0) ** np.float32(-2 * j / ROPE)) for j in range(RH)]
            eng.wait_ge(rope_in, 16)
            ch.link(v.tensor_copy(posf[:, :], posi[:, :]))
            for j in range(RH):
                ch.mark(v.tensor_scalar(ang[:, 0, :, j], posf[:, :], inv[j], None, ALU.mult))
            ch.sync()
            ch.mark(v.tensor_scalar(kk[:, 0], ang[:, 0], float(1 / (2 * np.pi)), 12582912.0, ALU.mult, ALU.add))
            ch.link(v.tensor_scalar(ang[:, 1], ang[:, 0], float(1 / (2 * np.pi)), 0.25, ALU.mult, ALU.add))
            ch.link(v.tensor_scalar(kk[:, 1], ang[:, 1], 12582912.0, None, ALU.add))
            ch.link(v.tensor_scalar(kk[:, :], kk[:, :], 12582912.0, None, ALU.subtract))
            ch.link(v.tensor_copy(ang[:, 1], ang[:, 0]))
            c1, c2 = 6.28125, float(np.float32(2 * np.pi - 6.28125))
            for c in (c1, c2):
                ch.link(v.scalar_tensor_tensor(out=ang[:, :, :, :].rearrange("p a t j -> p (a t j)"),
                                               in0=kk[:, :, :, :].rearrange("p a t j -> p (a t j)"), scalar=-c,
                                               in1=ang[:, :, :, :].rearrange("p a t j -> p (a t j)"), op0=ALU.mult, op1=ALU.add))
            ch.link(v.tensor_scalar(ang[:, 1], ang[:, 1], float(np.pi / 2), None, ALU.add))
            v.tensor_scalar(ang[:, :], ang[:, :], 3.1415925, -3.1415925, ALU.min, ALU.max).then_inc(rope_ready, 1)

            eng.wait_ge(small_in, 16 * 12)
            for j in range(2):
                v.tensor_tensor_reduce(ljunk[:, j, :], lqk[:, 2 * j, :], lqk[:, 2 * j + 1, :], 1.0, 0.0, ALU.mult, ALU.add,
                                       lam[:, j:j + 1]).then_inc(lam_v, 1)
            L = cols[:, RL, :]
            ch.link(v.tensor_scalar(spt[:, 1, :], L, -1.0, None, ALU.mult))
            ch.link(v.tensor_tensor(spt[:, 0, :], L, spt[:, 1, :], ALU.min))
            ch.link(v.tensor_scalar(cols[:, SP8, :], spt[:, 1, :], 0.0, None, ALU.max))
            eng.sem_inc(lam_v, 1)
            eng.wait_ge(lam_a, 2)
            ch.link(v.tensor_tensor(lam[:, 0:1], lam[:, 3:4], lam[:, 2:3], ALU.subtract))
            ch.link(v.tensor_scalar(lam[:, 0:1], lam[:, 0:1], LAM_INIT, None, ALU.subtract))
            y0, s0, s2, acc = spt[:, 1, :], spt[:, 0, :], spt[:, 2, :], spt[:, 3, :]
            ch.link(v.tensor_scalar(s0, y0, 2.0, None, ALU.add))
            ch.link(v.reciprocal(s0, s0))
            ch.link(v.tensor_tensor(s0, s0, y0, ALU.mult))
            ch.link(v.tensor_tensor(s2, s0, s0, ALU.mult))
            ch.link(v.tensor_scalar(acc, s2, 1.0 / 17, 1.0 / 15, ALU.mult, ALU.add))
            for d in (13, 11, 9, 7, 5, 3, 1):
                ch.link(v.tensor_tensor(acc, acc, s2, ALU.mult))
                ch.link(v.tensor_scalar(acc, acc, 1.0 / d, None, ALU.add))
            ch.link(v.tensor_tensor(acc, acc, s0, ALU.mult))
            ch.link(v.scalar_tensor_tensor(out=cols[:, SP8, :], in0=acc, scalar=2.0, in1=cols[:, SP8, :],
                                           op0=ALU.mult, op1=ALU.add))
            ch.link(v.tensor_scalar(cols[:, SP8, :], cols[:, SP8, :], RG_C, None, ALU.mult))

            def rope(n):
                t = n % NT
                eng.wait_ge(z_free, n + 1)
                g = qk[:, n % 2, :].rearrange("p (g d) -> p g d", d=HALF)
                x1, x2 = g[:, :, 0:RH], g[:, :, RH:ROPE]
                sn = cs[:, 0, t, :].unsqueeze(1).to_broadcast([P, 8, RH])
                cn = cs[:, 1, t, :].unsqueeze(1).to_broadcast([P, 8, RH])
                if n:
                    eng.wait_ge(rope_done, 2 * n)
                ch.mark(v.tensor_tensor(rp[:, 0], x1, cn, ALU.mult))
                ch.mark(v.tensor_tensor(rp[:, 1], x2, sn, ALU.mult))
                ch.mark(v.tensor_tensor(rp[:, 2], x2, cn, ALU.mult))
                ch.link(v.tensor_tensor(rp[:, 3], x1, sn, ALU.mult))
                v.tensor_tensor(x1, rp[:, 0], rp[:, 1], ALU.subtract).then_inc(rope_done, 1)
                v.tensor_tensor(x2, rp[:, 2], rp[:, 3], ALU.add).then_inc(rope_done, 1)

            def evac_qk(n):
                t = n % NT
                eng.wait_ge(qk_T, n + 1)
                dst = qT if n < NT else kT
                v.tensor_copy(dst[:, :, t * P:(t + 1) * P],
                              PS[:, 2 + n % 2, :].rearrange("p (h n) -> p h n", n=P)).then_inc(qk_evac, 1)

            eng.wait_ge(rope_ready, 2)
            for n in range(2 * NT + 1):
                if n < 2 * NT:
                    rope(n)
                if n:
                    evac_qk(n - 1)

            def conv(k):
                eng.wait_ge(z_free, ring_at[("Z", k)] + 1)
                o = xc[:, k % 2, :]
                ch.link(v.tensor_scalar(o, xr[:, 0:T], cw[:, 0, k:k + 1], cols[:, CB, k:k + 1], ALU.mult, ALU.add))
                for j in (1, 2):
                    ch.link(v.scalar_tensor_tensor(out=o, in0=xr[:, j:j + T], scalar=cw[:, j, k:k + 1], in1=o,
                                                   op0=ALU.mult, op1=ALU.add))
                v.scalar_tensor_tensor(out=o, in0=xr[:, 3:3 + T], scalar=cw[:, 3, k:k + 1], in1=o,
                                       op0=ALU.mult, op1=ALU.add).then_inc(rec_conv, 1)

            def smax(s):
                i = s // H
                nk = (i + 1) * P
                b = 2 + 2 * (s % 2)
                eng.wait_ge(att_s, 2 * s + 2)
                diag = PS[:, b:b + 2, i * P:nk]
                ch.link(v.tensor_tensor(diag, diag, cmask[:, :].unsqueeze(1).to_broadcast([P, 2, P]), ALU.add))
                ch.link(v.tensor_reduce(mx[:, s % 2, :], PS[:, b:b + 2, 0:nk], AX_X, ALU.max))
                if s >= 2:
                    eng.wait_ge(att_exp, 2 * (s - 1))
                v.tensor_scalar(nmx[:, s % 2, :], mx[:, s % 2, :], -HALF ** -0.5, None, ALU.mult).then_inc(att_max, 1)

            def combine(s):
                nk = (s // H + 1) * P
                eng.wait_ge(att_exp, 2 * (s + 1))
                ch.link(v.reciprocal(rec[:, s % 2, :], sums[:, s % 2, :]))
                ch.link(v.tensor_tensor(rec[:, s % 2, 1:2], rec[:, s % 2, 1:2], lam[:, 0:1], ALU.mult))
                if s >= 2:
                    eng.wait_ge(att_t, s - 1)
                w = wb[:, s % 2, 0:nk]
                ch.link(v.tensor_scalar(w, pr[:, s % 2, 0, 0:nk], rec[:, s % 2, 0:1], None, ALU.mult))
                v.scalar_tensor_tensor(out=w, in0=pr[:, s % 2, 1, 0:nk], scalar=rec[:, s % 2, 1:2], in1=w,
                                       op0=ALU.mult, op1=ALU.add).then_inc(att_w, 1)

            for k in range(NSLOT):
                if k < RC:
                    conv(k)
                if k < 8:
                    smax(2 * k)
                    smax(2 * k + 1)
                if 1 <= k <= RC:
                    c = k - 1
                    eng.wait_ge(z_free, ring_at[("I", c)] + 1)
                    v.tensor_scalar(rg, rg, cols[:, SP8, c:c + 1], None, ALU.mult).then_inc(rec_la, 1)
                if k < 8:
                    combine(2 * k)
                    combine(2 * k + 1)
                if 1 <= k <= RC:
                    c = k - 1
                    eng.wait_ge(rec_ta, 2 * k)
                    ch.link(v.tensor_scalar(rg, th, 1.0, None, ALU.add))
                    ch.link(v.reciprocal(rg, rg))
                    v.tensor_tensor(th, th, rg, ALU.mult).then_inc(rec_q, 1)
                    ch.link(v.tensor_tensor(ig, ig, xc[:, c % 2, :], ALU.mult))
                    eng.wait_ge(rec_m, k)
                    ch.link(v.tensor_tensor(ig, ig, th, ALU.mult))
                    v.tensor_tensor_scan(yT[:, c, :], aa, ig, 0.0, ALU.mult, ALU.add).then_inc(rec_h, 1)
                if RC <= k < 2 * RC:
                    c = k - RC
                    eng.wait_ge(gate_sq, c + 1)
                    ch.link(v.tensor_scalar(gt, gq, GELU_A, 1.0, ALU.mult, ALU.add))
                    v.tensor_tensor(gt, gt, gs, ALU.mult).then_inc(gate_t, 1)
                    eng.wait_ge(gate_th, c + 1)
                    ch.link(v.scalar_tensor_tensor(out=gq, in0=gq, scalar=1.0, in1=gs, op0=ALU.add, op1=ALU.mult))
                    eng.wait_ge(rec_h, RC)
                    ch.link(v.scalar_tensor_tensor(out=yT[:, c, :], in0=gq, scalar=0.5, in1=yT[:, c, :],
                                                   op0=ALU.mult, op1=ALU.mult))
                    v.tensor_tensor(ysq[:, c, :], yT[:, c, :], yT[:, c, :], ALU.mult).then_inc(rec_y, 1)
            eng.wait_ge(att_o, 2 * NS)
            v.tensor_scalar(ors[:, :], oss[:, :], 1.0 / DV, EPS, ALU.mult, ALU.add).then_inc(mixn_v, 1)
            eng.wait_ge(rec_ss, 1)
            eng.wait_ge(rec_y, RC)
            v.tensor_scalar(gs, PS[:, 0, :], 1.0 / DR, EPS, ALU.mult, ALU.add).then_inc(mixn_v, 1)
            eng.wait_ge(mixn_a, 1)
            ch.link(v.reciprocal(ors[:, :], ors[:, :]))
            v.tensor_tensor(ob, ob, ors[:, :].unsqueeze(2).to_broadcast([P, NS, DV]), ALU.mult).then_inc(o_norm, 1)
            eng.wait_ge(mixn_a, 2)
            ch.link(v.reciprocal(gs, gs))
            for c in range(RC):
                v.scalar_tensor_tensor(out=yT[:, c, :], in0=yT[:, c, :], scalar=cols[:, GR, c:c + 1], in1=gs,
                                       op0=ALU.mult, op1=ALU.mult).then_inc(y_ready, 1)
            for i in range(NT):
                eng.wait_ge(o_T, i + 1)
                v.tensor_scalar(yT[:, RC:2 * RC, i * P:(i + 1) * P], PS[:, 2 + i, :].rearrange("p (h n) -> p h n", n=P),
                                gsub[:, :], 1.0 - LAM_INIT, ALU.mult, ALU.mult).then_inc(y_ready, 1)

            for t in range(NT):
                for n in range(HALVES):
                    u = HALVES * t + n
                    eng.wait_ge(mix_full, u + 1)
                    hh = h[:, t, n * BANK:(n + 1) * BANK]
                    v.tensor_tensor(hh, hh, PS[:, u, :], ALU.add).then_inc(h1_done, 1)
                mean_square(1, t)
                if t >= 2:
                    eng.wait_ge(row_T, HALVES * (NT + t - 1))
                    eng.wait_ge(hf_stored[t % 2], 16 * (t // 2))
                row(1, t, rowbuf[:, t % 2, :]).then_inc(row_done, 1)
                if t:
                    row_evac(1, t - 1)
            row_evac(1, NT - 1)

            ch.mark(v.memset(gsc[:, :, :], NEG))
            ch.mark(v.memset(gthr[:, :, :], NEG))
            eng.wait_ge(rt_sig, 1)
            ch.link(v.tensor_tensor(sel, scores, ebias[:, :].unsqueeze(1).to_broadcast([P, NT, NE]), ALU.add))
            for t in range(NT):
                for g in range(NG):
                    ch.mark(v.max(g8[:, t, g, :], sel[:, t, g * GE:(g + 1) * GE]))
            ch.sync()
            ch.link(v.tensor_tensor(gsc[:, :, 0:NG], g8[:, :, :, 0], g8[:, :, :, 1], ALU.add))
            for t in range(NT):
                ch.mark(v.max(gtop[:, t, :], gsc[:, t, :]))
            ch.sync()
            ch.link(v.tensor_copy(gthr[:, :, 0:TOPG], gtop[:, :, 0:TOPG]))
            for t in range(NT):
                ch.mark(v.match_replace(grep[:, t, :], gthr[:, t, :], gsc[:, t, :], BIG))
            ch.sync()
            ch.link(v.tensor_scalar(gmask[:, :, :], grep[:, :, 0:NG], BIG / 10, None, ALU.is_ge))
            ch.link(v.tensor_scalar(gpen[:, :, :], gmask[:, :, :], BIG, BIG, ALU.mult, ALU.subtract))
            selg = sel.rearrange("p t (g e) -> p (t g) e", e=GE)
            selmg = selm.rearrange("p t (g e) -> p (t g) e", e=GE)
            ch.link(v.tensor_tensor(selmg, selg, gmask[:, :, :].rearrange("p t g -> p (t g)").unsqueeze(2).to_broadcast([P, NT * NG, GE]), ALU.mult))
            ch.link(v.tensor_tensor(selmg, selmg, gpen[:, :, :].rearrange("p t g -> p (t g)").unsqueeze(2).to_broadcast([P, NT * NG, GE]), ALU.add))
            for t in range(NT):
                ch.mark(v.max(top8[:, t, :], selm[:, t, :]))
            ch.sync()
            for t in range(NT):
                ch.mark(v.match_replace(mk[:, t, :], top8[:, t, :], selm[:, t, :], BIG))
            ch.sync()
            ch.link(v.tensor_scalar(mk, mk, BIG / 10, None, ALU.is_ge))
            v.tensor_copy(mkb, mk).then_inc(mk_done, 1)
            ch.link(v.tensor_tensor(ww, mk, scores, ALU.mult))
            ch.link(v.tensor_reduce(den[:, :], ww, AX_X, ALU.add))
            ch.link(v.reciprocal(den[:, :], den[:, :]))
            ch.link(v.tensor_tensor(ww, ww, den[:, :].unsqueeze(2).to_broadcast([P, NT, NE]), ALU.mult))
            ch.link(v.tensor_scalar(ww, ww, ROUTE_SCALE, None, ALU.mult))
            ch.link(v.tensor_copy(VV[:, :, :, 3], ww))
            ch.link(v.tensor_tensor(rr, ww, VV[:, :, :, 3], ALU.subtract))
            ch.link(v.tensor_copy(VV[:, :, :, 4], rr))
            ch.link(v.tensor_tensor(VV[:, :, :, 5], rr, VV[:, :, :, 4], ALU.subtract))
            for t in range(NT):
                ch.mark(v.tensor_tensor_scan(cr[:, t, :], ones[:, 0:NE], mk[:, t, :], 0.0, ALU.mult, ALU.add))
            ch.sync()
            ch.link(v.tensor_tensor(cr, cr, mk, ALU.subtract))
            eng.wait_ge(consts, 3)
            for t in range(NT):
                hi = float(256 * (t // 2) - NOWHERE)
                ch.mark(v.tensor_scalar(VV[:, t, :, 0], ones[:, 0:NE], tlo[:, t:t + 1], None, ALU.mult))
                ch.mark(v.memset(VV[:, t, :, 1], hi))
                ch.mark(v.tensor_scalar(VV[:, t, :, 2], cr[:, t, :], float(T), hi, ALU.mult, ALU.add))
            eng.wait_ge(rank_full, NT + 1)
            R = PS[:, 5, 0:NT * NE].rearrange("p (t e) -> p t e", e=NE)
            ch.link(v.scalar_tensor_tensor(out=SL.rearrange("p t e -> p (t e)"), in0=PS[:, 5, 0:NT * NE], scalar=1.0,
                                           in1=mk.rearrange("p t e -> p (t e)"), op0=ALU.add, op1=ALU.mult))
            ch.link(v.tensor_scalar(SL, SL, -1.0, None, ALU.add))
            ch.link(v.tensor_copy(cnt, PS[:, 5, NT * NE:NT * NE + NE]))
            for b in range(1, MAXB):
                ch.mark(v.tensor_scalar(nxe[:, b - 1, :], cnt, b * P + 0.5, None, ALU.is_ge))
            ch.sync()
            ch.link(v.tensor_tensor(cnt, nxe[:, 0, :], nxe[:, 1, :], ALU.add))
            ch.link(v.tensor_tensor(cnt, cnt, nxe[:, 2, :], ALU.add))
            ch.link(v.tensor_tensor_scan(xev, ones[:, 0:NE], cnt, 0.0, ALU.mult, ALU.add))
            ch.link(v.tensor_tensor(cnt, xev, cnt, ALU.subtract))
            ch.mark(v.tensor_scalar(xcol[:, 2:3], xev[:, NE - 1:NE], 0.5, 0.25, ALU.mult, ALU.add))
            for b in range(1, MAXB):
                ch.mark(v.tensor_scalar(xpos[:, b - 1, :], cnt, float(b - 1), None, ALU.add))
            ch.sync()
            ch.link(v.tensor_scalar(xeq, xpos, pid[:, :], None, ALU.is_equal))
            ch.link(v.tensor_tensor(xeq, xeq, nxe, ALU.mult))
            ch.link(v.tensor_tensor(xsel, xeq, slots[:, 0, 0:NE].unsqueeze(1).to_broadcast([P, MAXB - 1, NE]), ALU.mult))
            ch.link(v.tensor_reduce(xcol[:, 0:1], xsel.rearrange("p b e -> p (b e)"), AX_X, ALU.add))
            for b in range(1, MAXB):
                ch.mark(v.tensor_scalar(xsel[:, b - 1, :], xeq[:, b - 1, :], float(b - MAXB), None, ALU.mult))
            ch.sync()
            ch.link(v.tensor_reduce(xcol[:, 1:2], xsel.rearrange("p b e -> p (b e)"), AX_X, ALU.add))
            v.tensor_scalar(xcol[:, 1:2], xcol[:, 1:2], float(MAXB), None, ALU.add).then_inc(xlist, 1)
            ch.link(v.tensor_copy(xnum[:, :], xcol[0:1, 2:3]))

            for t in range(NT + 1):
                if t < NT:
                    eng.wait_ge(sh_sig, t + 1)
                    ch.link(v.tensor_tensor(sgb[:, t % 2, :], sgb[:, t % 2, :], PS[:, 6 + t % 2, 0:F], ALU.mult))
                    if t >= 2:
                        eng.wait_ge(sh_T, t - 1)
                    v.tensor_tensor(hb[:, t % 2, :], sgb[:, t % 2, :], PS[:, 6 + t % 2, F:2 * F], ALU.mult).then_inc(sh_h, 1)
                if t:
                    for n in range(HALVES):
                        eng.wait_ge(sh_dn, HALVES * (t - 1) + n + 1)
                        hh = h[:, t - 1, n * BANK:(n + 1) * BANK]
                        v.tensor_tensor(hh, hh, PS[:, n, :], ALU.add).then_inc(sh_add, 1)

            def one_hot(e, s):
                if not isinstance(e, int) or e >= 2:
                    eng.wait_ge(ix_full, e - 1)
                v.tensor_tensor(ohb[:, s % 2], slots[:, 0, :].unsqueeze(1).to_broadcast([P, NT, P]),
                                SL[:, :, bass.ds(e, 1)].to_broadcast([P, NT, P]), ALU.is_equal).then_inc(oh_done, 1)

            def indices(e, s):
                eng.wait_ge(ix_full, e + 1)
                b = PS[:, 5, 0:6]
                if not isinstance(e, int) or e >= 2:
                    eng.wait_ge(tx_full, HALVES * (e - 1))
                v.tensor_scalar(ixg[:, s % 2:s % 2 + 1], b[:, 1:2], b[:, 0:1], float(NOWHERE), ALU.add, ALU.add).then_inc(ix_done, 1)
                if not isinstance(e, int) or e >= 4:
                    eng.wait_ge(dest_done, 2 * e - 6)
                v.tensor_copy(raw[:, s % 4, :], b).then_inc(ix_done, 1)

            def dest(e, s):
                eng.wait_ge(ix_done, 2 * e + 2)
                if not isinstance(e, int) or e >= 2:
                    eng.wait_ge(y_evac_a, e - 1)
                    eng.wait_ge(y_evac_v, e - 1)
                    eng.wait_ge(scattered[s % 2], scatters_before(e, s))
                r = raw[:, s % 4, :]
                v.tensor_scalar(ixd[:, s % 2:s % 2 + 1], r[:, 2:3], r[:, 0:1], float(NOWHERE), ALU.add, ALU.add).then_inc(dest_done, 1)
                v.tensor_reduce(wgt[:, s % 2:s % 2 + 1], r[:, 3:6], AX_X, ALU.add).then_inc(dest_done, 1)

            def act_mul(e, s):
                eng.wait_ge(sg_done, e + 1)
                if not isinstance(e, int) or e >= 2:
                    eng.wait_ge(ht_full, e - 1)
                v.tensor_tensor(hb[:, s % 2, :], sgb[:, s % 2, :], PS[:, s % 2, 0:F], ALU.mult).then_inc(ht_step, 1)
                eng.wait_ge(ht_step, e + 1)
                v.tensor_tensor(hb[:, s % 2, :], hb[:, s % 2, :], PS[:, s % 2, F:2 * F], ALU.mult).then_inc(h_done, 1)

            def down_evac(e, s):
                eng.wait_ge(dn_full, HALVES * e + 2)
                eng.wait_ge(dest_done, 2 * e + 2)
                if not isinstance(e, int) or e >= 2:
                    eng.wait_ge(scattered[s % 2], scatters_before(e, s))
                v.tensor_scalar(yb[:, s % 2, BANK:D], PS[:, 7, :], wgt[:, s % 2:s % 2 + 1], None, ALU.mult).then_inc(y_evac_v, 1)

            eng.wait_ge(xrow, 1)
            v.tensor_copy(xtab[:, :, :], PS[0:1, 5, 0:2 * P].rearrange("p (a x) -> p a x", a=2)).then_inc(routes, 1)
            ch.sync()
            one_hot(0, 0)
            one_hot(1, 1)
            indices(0, 0)
            one_hot(2, 2)
            indices(1, 1)
            def turn(e, s, first=False, left=U):
                if left > 3:
                    one_hot(e + 3, (s + 3) % U)
                if left > 2:
                    indices(e + 2, (s + 2) % U)
                act_mul(e, s)
                if not first:
                    dest(e - 1, (s - 1) % U)
                    down_evac(e - 1, (s - 1) % U)

            for s in range(U):
                turn(s, s, first=(s == 0))
            with eng.Fori(1, NE // U - 1) as i:
                for s in range(U):
                    turn(i * U + s, s)
            for s in range(U):
                turn(NE - U + s, s, left=U - s)
            dest(NE - 1, U - 1)
            down_evac(NE - 1, U - 1)
            eng.wait_ge(sh_add, HALVES * NT)
            main_done(eng)

            pairs = eng.value_load(xnum[0:1, 0:1], min_val=0, max_val=MAXX // 2)
            with eng.If(pairs > 0):
                with eng.Fori(0, pairs) as i:
                    for j in range(2):
                        e = eng.value_load(xtab[0:1, 0, bass.ds(i * 2 + j, 1)], min_val=0, max_val=NE - 1)
                        b = eng.value_load(xtab[0:1, 1, bass.ds(i * 2 + j, 1)], min_val=0, max_val=MAXB)
                        eng.wait_ge(x_ix, i * 2)
                        v.tensor_tensor(ohb[:, j], slots[:, bass.ds(b, 1), :].to_broadcast([P, NT, P]),
                                        SL[:, :, bass.ds(e, 1)].to_broadcast([P, NT, P]), ALU.is_equal).then_inc(x_oh, 1)
                    for j in range(2):
                        eng.wait_ge(x_ix, i * 2 + (j + 1))
                        eng.wait_ge(x_ya, i * 2)
                        eng.wait_ge(x_yv, i * 2)
                        eng.wait_ge(x_scattered[j], i * 16)
                        for dst, k in ((ixg, 1), (ixd, 2)):
                            v.tensor_scalar(dst[:, j:j + 1], PS[:, 5, k:k + 1], PS[:, 5, 0:1], float(NOWHERE), ALU.add, ALU.add).then_inc(x_ixd, 1)
                        v.tensor_reduce(wgt[:, j:j + 1], PS[:, 5, 3:6], AX_X, ALU.add).then_inc(x_ixd, 1)
                    for j in range(2):
                        eng.wait_ge(x_sg, i * 2 + (j + 1))
                        eng.wait_ge(x_ht, i * 2)
                        v.tensor_tensor(hb[:, j, :], sgb[:, j, :], PS[:, j, 0:F], ALU.mult).then_inc(x_step, 1)
                        eng.wait_ge(x_step, i * 2 + (j + 1))
                        v.tensor_tensor(hb[:, j, :], hb[:, j, :], PS[:, j, F:2 * F], ALU.mult).then_inc(x_h, 1)
                    for j in range(2):
                        eng.wait_ge(x_dn, i * 4 + (2 * j + 2))
                        v.tensor_scalar(yb[:, j, BANK:D], PS[:, 7, :], wgt[:, j:j + 1], None, ALU.mult).then_inc(x_yv, 1)
                eng.wait_ge(x_yv, pairs * 2)
                eng.sem_inc(experts_done_v, 1)
            with eng.Else():
                eng.sem_inc(experts_done_v, 1)

            for t in range(NT):
                eng.wait_ge(plane_in[t % 2], 16 * (t // 2 + 1))
                for j in range(TOPK):
                    ins = v.tensor_tensor(h[:, t, :], h[:, t, :], planes[:, t % 2, j, :], ALU.add)
                    if j < TOPK - 1:
                        ch.link(ins)
                    else:
                        ins.then_inc(plane_used, 1)
                if t == 1:
                    for u in range(2):
                        eng.wait_ge(p_T, u + 1)
                        v.tensor_copy(pT[:, u, :], PS[:, 6 + u, :]).then_inc(p_evac, 1)
                mean_square(2, t)
                eng.wait_ge(plane_used, t + 1)
                if t >= 2:
                    eng.wait_ge(row_T, HALVES * (2 * NT + t - 1))
                row(2, t, orow[:, t % 2, :]).then_inc(row_done, 1)
                if t:
                    row_evac(2, t - 1)
            row_evac(2, NT - 1)

            for u in range(NT * HALVES):
                t, n = divmod(u, HALVES)
                eng.wait_ge(pg_sig, u + 1)
                eng.wait_ge(pp_full, u + 1)
                v.tensor_tensor(sg2[:, u % 2, :], sg2[:, u % 2, :], PS[:, 6 + u % 2, :], ALU.mult).then_inc(ple_mul, 1)
                eng.wait_ge(ple_mul, u + 1)
                hh = h[:, t, n * BANK:(n + 1) * BANK]
                v.tensor_tensor(hh, hh, sg2[:, u % 2, :], ALU.add).then_inc(ple_done, 1)
                if n == 1:
                    mean_square(3, t)
                    if t >= 2:
                        eng.wait_ge(stored[t % 2], 16 * (t // 2))
                    elif t == 0:
                        eng.wait_ge(row_T, HALVES * 3 * NT)
                    row(3, t, orow[:, t % 2, :]).then_inc(orow_done, 1)

        @block.gpsimd
        def _(eng):
            g = nc.gpsimd
            g.memset(ident[:, :], 0.0).then_inc(bd_zero, 1)
            eng.wait_ge(bd_zero, 1)
            g.memset(wab, 0.0)
            g.memset(wib, 0.0).then_inc(bd_zero, 1)
            g.memset(xr[:, 0:3], 0.0).then_inc(bd_zero, 1)
            g.affine_select(out=ident[:, :], in_=ident[:, :], compare_op=ALU.not_equal, fill=1.0, base=0,
                            pattern=[[-1, P]], channel_multiplier=1).then_inc(consts, 1)
            g.memset(ones[:, :], 1.0)
            g.memset(onesb[:, :], 1.0)
            g.memset(tri[:, :], 1.0)
            g.memset(cmask[:, :], 0.0)
            g.iota(slots[:, :, :], [[P, MAXB + 1], [1, P]], base=0, channel_multiplier=0, allow_small_or_imprecise_dtypes=True)
            g.iota(pid[:, :], [[0, 1]], base=0, channel_multiplier=1, allow_small_or_imprecise_dtypes=True)
            g.iota(tlo[:, :], [[0, 2], [P, 2]], base=0, channel_multiplier=1,
                   allow_small_or_imprecise_dtypes=True).then_inc(consts, 1)
            eng.wait_ge(consts, 2)
            g.affine_select(out=cmask[:, :], in_=cmask[:, :], compare_op=ALU.is_ge, fill=NEG, base=0,
                            pattern=[[-1, P]], channel_multiplier=1)
            g.affine_select(out=tri[:, :], in_=tri[:, :], compare_op=ALU.is_gt, fill=0.0, base=0,
                            pattern=[[1, P]], channel_multiplier=-1).then_inc(consts, 1)
            eng.wait_ge(mix_full, NT * HALVES)
            g.memset(xg, 0.0).then_inc(xg_zero, 1)

            def gather(e, s):
                eng.wait_ge(ix_done, 2 * e + 2)
                if not isinstance(e, int) or e >= 2:
                    eng.wait_ge(tx_full, HALVES * (e - 1))
                eng.sem_inc(pool_ready, 1)
                g.indirect_dma_start(xg[:, s % 2, :], None, hf_rows,
                                     bass.IndirectOffsetOnAxis(ap=ixg[:, s % 2:s % 2 + 1], axis=0),
                                     bounds_check=T - 1, oob_is_err=False).then_inc(gathered[s % 2], 16)

            def scatter(e, s):
                eng.wait_ge(y_evac_a, e + 1)
                eng.wait_ge(y_evac_v, e + 1)
                eng.sem_inc(pool_ready, 1)
                g.indirect_dma_start(routed, bass.IndirectOffsetOnAxis(ap=ixd[:, s % 2:s % 2 + 1], axis=0),
                                     yb[:, s % 2, :], None,
                                     bounds_check=CHOICES - 1, oob_is_err=False).then_inc(scattered[s % 2], 16)

            eng.wait_ge(xg_zero, 1)
            for r in range(2):
                eng.wait_ge(hf_stored[r], 16 * NT // 2)
            gather(0, 0)
            gather(1, 1)
            def turn(e, s, first=False, left=U):
                if left > 2:
                    gather(e + 2, (s + 2) % U)
                if not first:
                    scatter(e - 1, (s - 1) % U)

            for s in range(U):
                turn(s, s, first=(s == 0))
            with eng.Fori(1, NE // U - 1) as i:
                for s in range(U):
                    turn(i * U + s, s)
            for s in range(U):
                turn(NE - U + s, s, left=U - s)
            scatter(NE - 1, U - 1)
            main_done(eng)

            pairs = eng.value_load(xnum[0:1, 0:1], min_val=0, max_val=MAXX // 2)
            with eng.If(pairs > 0):
                with eng.Fori(0, pairs) as i:
                    for j in range(2):
                        eng.wait_ge(x_ixd, i * 6 + (3 * j + 3))
                        eng.wait_ge(x_tx, i * 4)
                        eng.sem_inc(pool_ready, 1)
                        g.indirect_dma_start(xg[:, j, :], None, hf_rows,
                                             bass.IndirectOffsetOnAxis(ap=ixg[:, j:j + 1], axis=0),
                                             bounds_check=T - 1, oob_is_err=False).then_inc(x_gathered[j], 16)
                    for j in range(2):
                        eng.wait_ge(x_ya, i * 2 + (j + 1))
                        eng.wait_ge(x_yv, i * 2 + (j + 1))
                        eng.sem_inc(pool_ready, 1)
                        g.indirect_dma_start(routed, bass.IndirectOffsetOnAxis(ap=ixd[:, j:j + 1], axis=0),
                                             yb[:, j, :], None,
                                             bounds_check=CHOICES - 1, oob_is_err=False).then_inc(x_scattered[j], 16)
                for j in range(2):
                    eng.wait_ge(x_scattered[j], pairs * 16)
                    eng.sem_inc(routed_done, 1)
            with eng.Else():
                eng.sem_inc(routed_done, 2)

        @block.tensor
        def _(eng):
            pe = nc.tensor
            eng.wait_ge(consts, 3)

            def row_T_(n, t, src):
                for j in range(HALVES):
                    b = (2 * t + j) % 4
                    if t >= 2:
                        eng.wait_ge((row_evac_a, row_evac_v)[j], NT * n + t - 1)
                    for c in range(4):
                        mm = pe.transpose(PS[:, b, c * P:(c + 1) * P],
                                          src.rearrange("p (q c) -> p c q", c=KC)[:, 4 * j + c, :], ident[:, :])
                    mm.then_inc(row_T, 1)

            for t in range(NT):
                eng.wait_ge(row_done, t + 1)
                row_T_(0, t, rowbuf[:, t % 2, :])
            eng.wait_ge(row_evac_a, NT)
            eng.wait_ge(row_evac_v, NT)

            def unit(n, pairs):
                if n >= 2:
                    eng.wait_ge(z_free, n - 1)
                for j, (a, b) in enumerate(pairs):
                    mm = pe.matmul(PS[:, n % 2, :], a, b, start=(j == 0), stop=(j == len(pairs) - 1))
                mm.then_inc(z_full, 1)

            def qk_T_(n):
                eng.wait_ge(rope_done, 2 * n + 2)
                if n >= 2:
                    eng.wait_ge(qk_evac, n - 1)
                for hh in range(H):
                    mm = pe.transpose(PS[:, 2 + n % 2, hh * P:(hh + 1) * P], qk[:, n % 2, hh * P:(hh + 1) * P], ident[:, :])
                mm.then_inc(qk_T, 1)

            for n in range(3 * NT):
                j, t = divmod(n, NT)
                if t == 0:
                    eng.wait_ge(win_in[j % 2], 16 * (j // 2 + 1))
                unit(n, [(hT[:, c, t * P:(t + 1) * P], win[:, j % 2, c, :]) for c in range(KC)])
                if 1 <= n <= 2 * NT:
                    qk_T_(n - 1)

            def z_unit(k):
                j = 3 + k // RC
                if k % RC == 0:
                    eng.wait_ge(win_in[j % 2], 16 * (j // 2 + 1))
                c0 = (k % RC) * P
                unit(ring_at[("Z", k)], [(win[:, j % 2, c, c0:c0 + P], hT[:, c, :]) for c in range(KC)])

            def scores_(s):
                i, hh = divmod(s, H)
                nk = (i + 1) * P
                if s >= 2:
                    eng.wait_ge(att_exp, 2 * (s - 1))
                for c in range(2):
                    a, b = c * HALF, (c + 1) * HALF
                    pe.matmul(PS[:, 2 + 2 * (s % 2) + c, 0:nk], qT[a:b, hh, i * P:(i + 1) * P], kT[a:b, hh, 0:nk],
                              start=True, stop=True).then_inc(att_s, 1)

            def w_T(s):
                eng.wait_ge(att_w, s + 1)
                if s >= 2:
                    eng.wait_ge(att_o, 2 * (s - 1))
                for kb in range(s // H + 1):
                    mm = pe.transpose(PS[:, 6 + s % 2, kb * P:(kb + 1) * P], wb[:, s % 2, kb * P:(kb + 1) * P], ident[:, :])
                mm.then_inc(att_t, 1)

            def pv(s):
                i, hh = divmod(s, H)
                eng.wait_ge(att_wt, s + 1)
                for kb in range(i + 1):
                    mm = pe.matmul(PS[:, 6 + s % 2, 0:DV], wT[:, s % 2, kb * P:(kb + 1) * P],
                                   vv[:, kb, hh * DV:(hh + 1) * DV], start=(kb == 0), stop=(kb == i))
                mm.then_inc(att_pv, 1)

            eng.wait_ge(qk_evac, 2 * NT)
            eng.wait_ge(bd_in, 64)
            for k in range(NSLOT):
                if k < 2 * RC:
                    z_unit(k)
                if 1 <= k <= RC:
                    eng.wait_ge(rec_conv, k)
                    unit(ring_at[("R", k - 1)], [(wab[:, k - 1, :], xc[:, (k - 1) % 2, :])])
                    unit(ring_at[("I", k - 1)], [(wib[:, k - 1, :], xc[:, (k - 1) % 2, :])])
                if k < 8:
                    scores_(2 * k)
                    scores_(2 * k + 1)
                if k >= 1:
                    for f in (w_T, pv):
                        f(2 * k - 2)
                        f(2 * k - 1)
            eng.wait_ge(z_free, len(ring))
            eng.wait_ge(rec_y, RC)
            for c in range(RC):
                mm = pe.matmul(PS[:, 0, :], ones[:, :], ysq[:, c, :], start=(c == 0), stop=(c == RC - 1))
            mm.then_inc(rec_ss, 1)
            eng.wait_ge(o_norm, 1)
            eng.wait_ge(att_exp, 2 * NS)
            for i in range(NT):
                for hh in range(H):
                    mm = pe.transpose(PS[:, 2 + i, hh * P:(hh + 1) * P], ob[:, H * i + hh, :], ident[:, :])
                mm.then_inc(o_T, 1)

            eng.wait_ge(y_ready, RC + NT)
            eng.wait_ge(win_in[1], 16 * 3)
            eng.wait_ge(win_in[0], 16 * 4)
            for t in range(NT):
                for n in range(HALVES):
                    for c in range(KC):
                        mm = pe.matmul(PS[:, HALVES * t + n, :], yT[:, c, t * P:(t + 1) * P], win[:, (5 + n) % 2, c, :],
                                       start=(c == 0), stop=(c == KC - 1))
                    mm.then_inc(mix_full, 1)

            eng.wait_ge(wr_in, 16)

            def router(t):
                eng.wait_ge(row_evac_a, NT + t + 1)
                eng.wait_ge(row_evac_v, NT + t + 1)
                eng.wait_ge(h1_done, 5)
                for c in range(KC):
                    mm = pe.matmul(PS[:, 4, t * NE:(t + 1) * NE], hT[:, c, t * P:(t + 1) * P], wr[:, c, :],
                                   start=(c == 0), stop=(c == KC - 1))
                mm.then_inc(rt_full, 1)

            for t in range(NT):
                eng.wait_ge(row_done, NT + t + 1)
                row_T_(1, t, rowbuf[:, t % 2, :])
                if t:
                    router(t - 1)
            router(NT - 1)

            def ranks():
                eng.wait_ge(mk_done, 1)
                for t in range(NT):
                    for i in range(t + 1):
                        mm = pe.matmul(PS[:, 5, t * NE:(t + 1) * NE], tri[:, :] if i == t else onesb[:, :], mkb[:, i, :],
                                       start=(i == 0), stop=(i == t))
                    mm.then_inc(rank_full, 1)
                for i in range(NT):
                    mm = pe.matmul(PS[:, 5, NT * NE:NT * NE + NE], onesb[:, :], mkb[:, i, :], start=(i == 0), stop=(i == NT - 1))
                mm.then_inc(rank_full, 1)

            eng.wait_ge(sw_in, 48)
            for t in range(NT + 1):
                if t < NT:
                    if t >= 2:
                        eng.wait_ge(sh_h, t - 1)
                    for c in range(KC):
                        mm = pe.matmul(PS[:, 6 + t % 2, :], hT[:, c, t * P:(t + 1) * P],
                                       wup[3][:, c].rearrange("p w f -> p (w f)"), start=(c == 0), stop=(c == KC - 1))
                    mm.then_inc(sh_up, 1)
                if t == 1:
                    ranks()
                if t:
                    eng.wait_ge(sh_h, t)
                    if t >= 3:
                        eng.wait_ge(sh_hT, t - 2)
                    for c in range(FC):
                        mm = pe.transpose(PS[:, 2 + (t - 1) % 2, c * P:(c + 1) * P],
                                          hb[:, (t - 1) % 2, :].rearrange("p (q c) -> p c q", c=FC)[:, c, :], ident[:, :])
                    mm.then_inc(sh_T, 1)
                    eng.wait_ge(sh_hT, t)
                    for n in range(HALVES):
                        if t >= 2:
                            eng.wait_ge(sh_add, HALVES * (t - 2) + n + 1)
                        for c in range(FC):
                            mm = pe.matmul(PS[:, n, :], hTe[:, (t - 1) % 2, c, :], wdn[3][:, c, n * BANK:(n + 1) * BANK],
                                           start=(c == 0), stop=(c == FC - 1))
                        mm.then_inc(sh_dn, 1)

            def index_sums(e, s):
                eng.wait_ge(oh_done, e + 1)
                if not isinstance(e, int) or e >= 1:
                    eng.wait_ge(ix_done, 2 * e)
                for c in range(NT):
                    mm = pe.matmul(PS[:, 5, 0:6], ohb[:, s % 2, c, :],
                                   VV[:, c, bass.ds(e, 1), :].rearrange("p a v -> p (a v)"), start=(c == 0), stop=(c == NT - 1))
                mm.then_inc(ix_full, 1)

            def gathered_T(e, s):
                eng.wait_ge(gathered[s % 2], 16 * (e // 2 + 1) if isinstance(e, int) else (e - s) * 8 + 16 * (s // 2 + 1))
                for j in range(HALVES):
                    if not isinstance(e, int) or e >= 1:
                        eng.wait_ge(tx_evac, HALVES * (e - 1) + j + 1)
                    for c in range(4):
                        mm = pe.transpose(PS[:, 2 + j, c * P:(c + 1) * P],
                                          xg[:, s % 2, :].rearrange("p (q c) -> p c q", c=KC)[:, 4 * j + c, :], ident[:, :])
                    mm.then_inc(tx_full, 1)

            def up(e, s):
                eng.wait_ge(tx_evac, HALVES * (e + 1))
                eng.wait_ge(up_in[s], 32 * (e // U + 1) if isinstance(e, int) else (e - s) * 8 + 32)
                if not isinstance(e, int) or e >= 2:
                    eng.wait_ge(h_done, e - 1)
                for c in range(KC):
                    mm = pe.matmul(PS[:, s % 2, :], xgT[:, s % 2, c, :], wup[s][:, c].rearrange("p w f -> p (w f)"),
                                   start=(c == 0), stop=(c == KC - 1))
                mm.then_inc(up_full, 1)

            def down(e, s):
                eng.wait_ge(h_done, e + 1)
                if not isinstance(e, int) or e >= 1:
                    eng.wait_ge(ht_evac, e)
                for c in range(FC):
                    mm = pe.transpose(PS[:, 4, c * P:(c + 1) * P],
                                      hb[:, s % 2, :].rearrange("p (q c) -> p c q", c=FC)[:, c, :], ident[:, :])
                mm.then_inc(ht_full, 1)
                eng.wait_ge(ht_evac, e + 1)
                eng.wait_ge(dn_in[s], 16 * (e // U + 1) if isinstance(e, int) else (e - s) * 4 + 16)
                for n in range(HALVES):
                    if not isinstance(e, int) or e >= 1:
                        eng.wait_ge((y_evac_a, y_evac_v)[n], e)
                    for c in range(FC):
                        mm = pe.matmul(PS[:, 6 + n, :], hTe[:, s % 2, c, :], wdn[s][:, c, n * BANK:(n + 1) * BANK],
                                       start=(c == 0), stop=(c == FC - 1))
                    mm.then_inc(dn_full, 1)

            eng.wait_ge(xlist, 1)
            for a in range(2):
                mm = pe.matmul(PS[0:1, 5, a * P:(a + 1) * P], xcol[:, a:a + 1], ident[:, :], start=True, stop=True)
            mm.then_inc(xrow, 1)
            eng.wait_ge(routes, 1)
            eng.wait_ge(sh_add, HALVES * NT)
            eng.wait_ge(sh_h, NT)
            index_sums(0, 0)
            index_sums(1, 1)
            gathered_T(0, 0)
            def turn(e, s, first=False, left=U):
                if left > 2:
                    index_sums(e + 2, (s + 2) % U)
                if left > 1:
                    gathered_T(e + 1, (s + 1) % U)
                up(e, s)
                if not first:
                    down(e - 1, (s - 1) % U)

            for s in range(U):
                turn(s, s, first=(s == 0))
            with eng.Fori(1, NE // U - 1) as i:
                for s in range(U):
                    turn(i * U + s, s)
            for s in range(U):
                turn(NE - U + s, s, left=U - s)
            down(NE - 1, U - 1)
            main_done(eng)

            pairs = eng.value_load(xnum[0:1, 0:1], min_val=0, max_val=MAXX // 2)
            with eng.If(pairs > 0):
                with eng.Fori(0, pairs) as i:
                    for j in range(2):
                        e = eng.value_load(xtab[0:1, 0, bass.ds(i * 2 + j, 1)], min_val=0, max_val=NE - 1)
                        eng.wait_ge(x_oh, i * 2 + (j + 1))
                        eng.wait_ge(x_ixd, i * 6 + 3 * j)
                        for c in range(NT):
                            mm = pe.matmul(PS[:, 5, 0:6], ohb[:, j, c, :], VV[:, c, bass.ds(e, 1), :].rearrange("p a v -> p (a v)"),
                                           start=(c == 0), stop=(c == NT - 1))
                        mm.then_inc(x_ix, 1)
                    for j in range(2):
                        eng.wait_ge(x_gathered[j], i * 16 + 16)
                        eng.wait_ge(x_txe, i * 4)
                        eng.wait_ge(x_ya, i * 2)
                        eng.wait_ge(x_yv, i * 2)
                        for n in range(HALVES):
                            for c in range(4):
                                mm = pe.transpose(PS[:, 4 * j + 2 + n, c * P:(c + 1) * P],
                                                  xg[:, j, :].rearrange("p (q c) -> p c q", c=KC)[:, 4 * n + c, :], ident[:, :])
                            mm.then_inc(x_tx, 1)
                    for j in range(2):
                        eng.wait_ge(x_txe, i * 4 + (2 * j + 2))
                        eng.wait_ge(x_up_in[j], i * 32 + 32)
                        eng.wait_ge(x_h, i * 2)
                        for c in range(KC):
                            mm = pe.matmul(PS[:, j, :], xgT[:, j, c, :], wup[j][:, c].rearrange("p w f -> p (w f)"),
                                           start=(c == 0), stop=(c == KC - 1))
                        mm.then_inc(x_up, 1)
                    for j in range(2):
                        eng.wait_ge(x_h, i * 2 + (j + 1))
                        eng.wait_ge(x_hte, i * 2 + j)
                        for c in range(FC):
                            mm = pe.transpose(PS[:, 4, c * P:(c + 1) * P],
                                              hb[:, j, :].rearrange("p (q c) -> p c q", c=FC)[:, c, :], ident[:, :])
                        mm.then_inc(x_ht, 1)
                        eng.wait_ge(x_hte, i * 2 + (j + 1))
                        eng.wait_ge(x_dn_in[j], i * 16 + 16)
                        for n in range(HALVES):
                            eng.wait_ge((x_ya, x_yv)[n], i * 2 + j)
                            for c in range(FC):
                                mm = pe.matmul(PS[:, 6 + n, :], hTe[:, j, c, :], wdn[j][:, c, n * BANK:(n + 1) * BANK],
                                               start=(c == 0), stop=(c == FC - 1))
                            mm.then_inc(x_dn, 1)
                eng.wait_ge(x_dn, pairs * 4)
                eng.sem_inc(experts_done_t, 1)
            with eng.Else():
                eng.sem_inc(experts_done_t, 1)

            eng.wait_ge(experts_done_v, 1)
            eng.wait_ge(experts_done_a, 1)
            eng.wait_ge(pw_in, 32)
            for u in range(DPLE // P):
                for t in range(NT):
                    mm = pe.transpose(PS[:, 6 + u, t * P:(t + 1) * P],
                                      prow[:, t, :].rearrange("p (q c) -> p c q", c=DPLE // P)[:, u, :], ident[:, :])
                mm.then_inc(p_T, 1)
            for t in range(NT):
                eng.wait_ge(row_done, 2 * NT + t + 1)
                row_T_(2, t, orow[:, t % 2, :])
            eng.wait_ge(wpg_in, 16)
            eng.wait_ge(p_evac, 2)
            eng.wait_ge(row_evac_a, 3 * NT)
            eng.wait_ge(row_evac_v, 3 * NT)
            for u in range(NT * HALVES):
                t, n = divmod(u, HALVES)
                if u >= 2:
                    eng.wait_ge(pg_sig, u - 1)
                for c in range(KC):
                    mm = pe.matmul(PS[:, 4 + u % 2, :], hT[:, c, t * P:(t + 1) * P], wpg[:, c, n * BANK:(n + 1) * BANK],
                                   start=(c == 0), stop=(c == KC - 1))
                mm.then_inc(pg_full, 1)
                if u >= 2:
                    eng.wait_ge(ple_mul, u - 1)
                for c in range(DPLE // P):
                    mm = pe.matmul(PS[:, 6 + u % 2, :], pT[:, c, t * P:(t + 1) * P], wpp[:, c, n * BANK:(n + 1) * BANK],
                                   start=(c == 0), stop=(c == DPLE // P - 1))
                mm.then_inc(pp_full, 1)


_INS = ["x", "p", "positions", "ln_mix", "w_in", "conv_w", "conv_b", "w_a", "b_a", "w_i", "b_i", "rg_lambda",
        "g_rec", "lq1", "lk1", "lq2", "lk2", "g_sub", "w_out", "ln_moe", "w_router", "e_bias", "w1", "w3", "w2",
        "ws1", "ws3", "ws2", "ln_ple", "w_ple_gate", "w_ple_proj", "ln_f"]


def kernel(**inputs):
    import numpy as _np
    import concourse.bacc as _bacc
    from concourse import mybir as _mybir
    from concourse.bass_utils import run_bass_kernel_spmd as _run

    nc = _bacc.Bacc("TRN2", target_bir_lowering=False, num_devices=1)
    arrays, args = {}, []
    for name in _INS:
        a = _np.ascontiguousarray(inputs[name])
        if name == "ln_f":
            a = a.reshape(1, D)
        arrays[f"in_{name}_dram"] = a
        args.append(nc.dram_tensor(f"in_{name}_dram", a.shape, _mybir.dt.from_np(a.dtype), kind="ExternalInput").ap())
    args.append(nc.dram_tensor("out_0_dram", (1, T, D), _mybir.dt.float32, kind="ExternalOutput").ap())
    build_layer(nc, *args)
    r = _run(nc, [arrays], core_ids=[0])
    return r.results[0]["out_0_dram"]
```

```python
from contextlib import ExitStack

import numpy as np
import concourse.bass as bass
from concourse import mybir

F32 = mybir.dt.float32
BF16 = mybir.dt.bfloat16
U32 = mybir.dt.uint32
I32 = mybir.dt.int32
ALU = mybir.AluOpType
ACT = mybir.ActivationFunctionType
AX_X = mybir.AxisListType.X

P = 128
T = 512
NT = T // P
D = 1024
KC = D // P
BANK = 512
DR = 512
RC = DR // P
H = 4
HALF = 64
DV = 128
ROPE = 16
RH = ROPE // 2
NE = 64
TOPK = 8
NG = 8
GE = NE // NG
TOPG = 4
F = 256
FC = F // P
DPLE = 256
EPS = 1e-6
LAM_INIT = 0.2
ROUTE_SCALE = 2.5
RG_C = 8.0
NEG = -1.0e30
BIG = 1.0e30
NOWHERE = 8192
CHOICES = TOPK * T
MAXB = T // P
MAXX = 34
WSLOT = 2 * KC * F + FC * D
U = 4
STEPS = NE + 2
GELU_A = 0.044715
GELU_B = 0.7978845608028654


class Chain:

    def __init__(self, eng, sem, base=0):
        self.eng, self.sem, self.base, self.n = eng, sem, base, 0

    def mark(self, ins):
        self.n += 1
        ins.then_inc(self.sem, 1)

    def sync(self):
        self.eng.wait_ge(self.sem, self.base + self.n)

    def link(self, ins):
        self.mark(ins)
        self.sync()


def build_layer(nc, x, p, positions, ln_mix, w_in, conv_w, conv_b, w_a, b_a, w_i, b_i, rg_lambda,
                g_rec, lq1, lk1, lq2, lk2, g_sub, w_out, ln_moe, w_router, e_bias, w1, w3, w2,
                ws1, ws3, ws2, ln_ple, w_ple_gate, w_ple_proj, ln_f, out):
    ctx = ExitStack()
    with ctx:
        def sb(name, shape, dt=F32):
            return ctx.enter_context(nc.sbuf_tensor(name, shape, dt))

        def sem(name):
            return ctx.enter_context(nc.semaphore(name))

        hf_rows = nc.dram_tensor("hf_rows", (T, D), F32, kind="Internal").ap()
        routed = nc.dram_tensor("routed", (CHOICES, D), F32, kind="Internal").ap()

        PS = ctx.enter_context(nc.psum_tensor("PS", [P, 8, BANK], F32))
        h = sb("h", [P, NT, D])
        hT = sb("hT", [P, KC, T])
        WB = sb("WB", [P, U * WSLOT])
        WK = sb("WK", [P, 16384])

        def region(base, at):
            def take(*shape):
                n = int(np.prod(shape))
                v = base[:, at[0]:at[0] + n]
                at[0] += n
                if len(shape) > 1:
                    names = " ".join(f"d{i}" for i in range(len(shape)))
                    v = v.rearrange(f"p ({names}) -> p {names}", **{f"d{i}": s for i, s in enumerate(shape) if i})
                return v
            return take

        wup = [WB[:, s * WSLOT:s * WSLOT + 2 * KC * F].rearrange("p (c w f) -> p c w f", w=2, f=F) for s in range(U)]
        wdn = [WB[:, s * WSLOT + 2 * KC * F:(s + 1) * WSLOT].rearrange("p (c n) -> p c n", n=D) for s in range(U)]

        pre = region(WB, [WSLOT])
        win = pre(2, KC, BANK)
        wab = pre(RC, P)
        wib = pre(RC, P)
        xr = pre(516)
        xc = pre(2, T)
        rg = pre(T)
        ig = pre(T)
        th = pre(T)
        aa = pre(T)
        gs = pre(T)
        gq = pre(T)
        gt = pre(T)
        qk = pre(2, BANK)
        rp = pre(4, 8, RH)
        vv = pre(NT, BANK)
        wk = region(WK, [0])
        qT = wk(H, T)
        kT = wk(H, T)
        ob = wk(4 * H, DV)
        yT = wk(2 * RC, T)
        pr = wk(2, 2, T)
        wb = wk(2, T)
        wT = wk(2, T)
        ysq = wk(RC, T)
        rowbuf = pr.rearrange("p a b t -> p a (b t)")
        lk = region(WK, [0])
        xg = lk(2, D)
        xgT = lk(2, KC, P)
        sgb = lk(2, F)
        hb = lk(2, F)
        hTe = lk(2, FC, P)
        yb = lk(2, D)
        onehot = lk(2, NT * P // 2)
        SL = lk(NT, NE)
        VVf = lk(NT * NE * 6 // 2)
        scores = lk(NT, NE)
        assert 2 * D * 3 <= 8192
        rt = region(WK, [12288])
        sel = rt(NT, NE)
        selm = rt(NT, NE)
        mk = rt(NT, NE)
        ww = rt(NT, NE)
        rr = rt(NT, NE)
        cr = rt(NT, NE)
        g8 = rt(NT, NG, 8)
        gsc = rt(NT, 16)
        gtop = rt(NT, 8)
        gthr = rt(NT, 8)
        grep = rt(NT, 16)
        gmask = rt(NT, NG)
        gpen = rt(NT, NG)
        top8 = rt(NT, 8)
        cnt = rt(NE)
        nxe = rt(MAXB - 1, NE)
        xpos = rt(MAXB - 1, NE)
        xeq = rt(MAXB - 1, NE)
        xev = rt(NE)
        xcol = rt(4)
        xsel = rt(MAXB - 1, NE)
        mkb = rt(NT * NE // 2).bitcast(BF16).rearrange("p (t e) -> p t e", e=NE)
        ohb = onehot.bitcast(BF16).rearrange("p r (c s) -> p r c s", s=P)
        VV = VVf.bitcast(BF16).rearrange("p (t e v) -> p t e v", t=NT, v=6)
        planes = WB[:, 0:2 * KC * D].rearrange("p (r j n) -> p r j n", r=2, n=D)
        wpg = WB[:, 2 * KC * D:3 * KC * D].rearrange("p (c n) -> p c n", n=D)
        pk = region(WK, [0])
        pproj = pk(NT, D)
        sg2 = pk(2, BANK)
        orow = pk(2, D)
        gain_f = pk(D)
        pk2 = region(WK, [9472])
        prow = pk2(NT, DPLE)
        pT = pk2(DPLE // P, T)
        wpp = pk2(DPLE // P, D)

        ident = sb("ident", [P, P])
        ones = sb("ones", [P, P])
        cmask = sb("cmask", [P, P])
        slots = sb("slots", [P, MAXB + 1, P])
        tri = sb("tri", [P, P], BF16)
        onesb = sb("onesb", [P, P], BF16)
        junk = WK[:, 15360:16384]
        ojunk = sb("ojunk", [P, DV])
        gain = sb("gain", [P, D])
        wr = sb("wr", [P, KC, NE])
        ebias = sb("ebias", [P, NE])
        posi = sb("posi", [P, NT], I32)
        posf = sb("posf", [P, NT])
        ang = sb("ang", [P, 2, NT, RH])
        kk = sb("kk", [P, 2, NT, RH])
        cs = sb("cs", [P, 2, NT, RH])
        cw = sb("cw", [P, 4, RC])
        cols = sb("cols", [P, 6, RC])
        spt = sb("spt", [P, 4, RC])
        lqk = sb("lqk", [P, 4, HALF])
        ljunk = sb("ljunk", [P, 2, HALF])
        lam = sb("lam", [P, 4])
        gsub = sb("gsub", [P, 1])
        ssq = sb("ssq", [P, 4, NT])
        rstd = sb("rstd", [P, 4, NT])
        oss = sb("oss", [P, 4 * H])
        ors = sb("ors", [P, 4 * H])
        mx = sb("mx", [P, 2, 2])
        nmx = sb("nmx", [P, 2, 2])
        sums = sb("sums", [P, 2, 2])
        rec = sb("rec", [P, 2, 2])
        den = sb("den", [P, NT])
        tlo = sb("tlo", [P, NT])
        pid = sb("pid", [P, 1])
        xtab = sb("xtab", [1, 2, P], I32)
        xnum = sb("xnum", [1, 1], I32)
        ixg = sb("ixg", [P, 2], U32)
        ixd = sb("ixd", [P, 4], U32)
        raw = sb("raw", [P, 4, 6])
        wgt = sb("wgt", [P, 4])
        CB, BA, BI, RL, GR, SP8 = range(6)

        x_in = [sem(f"x_in{t}") for t in range(NT)]
        gain_in = sem("gain_in")
        gain_f_in = sem("gain_f_in")
        small_in = sem("small_in")
        bd_in = sem("bd_in")
        win_in = [sem("win_in0"), sem("win_in1")]
        consts = sem("consts")
        bd_zero = sem("bd_zero")
        ssq_done = sem("ssq_done")
        ms_done = sem("ms_done")
        root_done = sem("root_done")
        row_done = sem("row_done")
        row_T = sem("row_T")
        row_evac_a = sem("row_evac_a")
        row_evac_v = sem("row_evac_v")
        dve = sem("dve_steps")
        rope_in = sem("rope_in")
        rope_ready = sem("rope_ready")
        lam_v = sem("lam_v")
        lam_a = sem("lam_a")
        z_full = sem("z_full")
        z_free = sem("z_free")
        rope_done = sem("rope_done")
        qk_T = sem("qk_T")
        qk_evac = sem("qk_evac")
        att_s = sem("att_s")
        att_max = sem("att_max")
        att_exp = sem("att_exp")
        att_w = sem("att_w")
        att_t = sem("att_t")
        att_wt = sem("att_wt")
        att_pv = sem("att_pv")
        att_o = sem("att_o")
        rec_conv = sem("rec_conv")
        rec_la = sem("rec_la")
        rec_ta = sem("rec_ta")
        rec_q = sem("rec_q")
        rec_m = sem("rec_m")
        rec_h = sem("rec_h")
        gate_sq = sem("gate_sq")
        gate_t = sem("gate_t")
        gate_th = sem("gate_th")
        rec_y = sem("rec_y")
        rec_ss = sem("rec_ss")
        mixn_v = sem("mixn_v")
        mixn_a = sem("mixn_a")
        y_ready = sem("y_ready")
        o_norm = sem("o_norm")
        o_T = sem("o_T")
        mix_full = sem("mix_full")
        h1_done = sem("h1_done")
        hf_stored = [sem("hf_stored0"), sem("hf_stored1")]
        rt_full = sem("rt_full")
        rt_sig = sem("rt_sig")
        mk_done = sem("mk_done")
        rank_full = sem("rank_full")
        routes = sem("routes")
        xlist = sem("xlist")
        xrow = sem("xrow")
        wr_in = sem("wr_in")
        sw_in = sem("sw_in")
        sh_up = sem("sh_up")
        sh_sig = sem("sh_sig")
        sh_h = sem("sh_h")
        sh_T = sem("sh_T")
        sh_hT = sem("sh_hT")
        sh_dn = sem("sh_dn")
        sh_add = sem("sh_add")
        xg_zero = sem("xg_zero")
        up_in = [sem(f"up_in{s}") for s in range(U)]
        dn_in = [sem(f"dn_in{s}") for s in range(U)]
        pool_ready = sem("pool_ready")
        oh_done = sem("oh_done")
        ix_full = sem("ix_full")
        ix_done = sem("ix_done")
        dest_done = sem("dest_done")
        gathered = [sem("gathered0"), sem("gathered1")]
        tx_full = sem("tx_full")
        tx_evac = sem("tx_evac")
        up_full = sem("up_full")
        sg_done = sem("sg_done")
        ht_step = sem("ht_step")
        h_done = sem("h_done")
        ht_full = sem("ht_full")
        ht_evac = sem("ht_evac")
        dn_full = sem("dn_full")
        y_evac_a = sem("y_evac_a")
        y_evac_v = sem("y_evac_v")
        scattered = [sem("scattered0"), sem("scattered1")]
        experts_done_v = sem("experts_done_v")
        experts_done_a = sem("experts_done_a")
        experts_done_t = sem("experts_done_t")
        routed_done = sem("routed_done")
        wpg_in = sem("wpg_in")
        pw_in = sem("pw_in")
        plane_in = [[sem(f"plane_in{r}_{g}") for g in range(4)] for r in range(2)]
        pair_added = sem("pair_added")
        sums_done = sem("sums_done")
        pproj_done = sem("pproj_done")
        plane_used = sem("plane_used")
        p_T = sem("p_T")
        p_evac = sem("p_evac")
        pg_full = sem("pg_full")
        pg_sig = sem("pg_sig")
        pp_full = sem("pp_full")
        ple_mul = sem("ple_mul")
        ple_done = sem("ple_done")
        orow_done = sem("orow_done")
        stored = [sem("stored0"), sem("stored1")]

        block = ctx.enter_context(nc.Block())

        ring = [("qkv", n) for n in range(3 * NT)]
        for k in range(2 * RC):
            ring.append(("Z", k))
            if 1 <= k <= RC:
                ring += [("R", k - 1), ("I", k - 1)]
        ring_at = {u: n for n, u in enumerate(ring)}
        NSLOT = 2 * RC + 1
        NS = 4 * H
        HALVES = 2

        w_in_v = w_in[0].rearrange("(p c) n -> p c n", c=KC)
        w_out_v = w_out[0].rearrange("(c p) n -> p c n", p=P)
        x_v = x[0].rearrange("(t p) n -> t p n", p=P)
        out_v = out[0].rearrange("(t p) n -> t p n", p=P)
        p_v = p[0, 0].rearrange("(t p) n -> t p n", p=P)
        hf_v = hf_rows.rearrange("(t p) n -> t p n", p=P)
        routed_v = routed.rearrange("(j t p) n -> t p j n", j=TOPK, p=P)
        WIN_COLS = [2 * DR, 2 * DR + 512, 2 * DR + 1024, 0, DR]
        WIN_UNITS = [NT, 2 * NT, 3 * NT, ring_at[("Z", RC - 1)] + 1, ring_at[("Z", 2 * RC - 1)] + 1]

        def expert_up(e):
            return (w1[0, bass.ds(e, 1)].rearrange("a (p c) f -> p (a c) f", c=KC),
                    w3[0, bass.ds(e, 1)].rearrange("a (p c) f -> p (a c) f", c=KC))

        def expert_dn(e):
            return w2[0, bass.ds(e, 1)].rearrange("a (p c) n -> p (a c) n", c=FC)

        def scatters_before(e, s):
            return 16 * (e // 2) if isinstance(e, int) else (e - s) * 8 + 16 * (s // 2)

        late = [(2, 0), (2, 1), (2, 2)] + [nt for t in range(3, NT) for nt in ((2, t), (3, t - 3))] + \
            [(3, t) for t in range(NT - 3, NT)]

        def norm_count(n, t):
            return NT * n + t if n < 2 else 2 * NT + late.index((n, t))

        def loads(e, s, dmas, extra):
            if isinstance(e, int):
                return 16 * dmas * (e // U + 1)
            if not extra:
                return (e - s) * (4 * dmas) + 16 * dmas
            return (e - s) * (8 * dmas) + 16 * dmas * (1 - NE // U)

        def extra_steps(eng, stages, finish, tail):
            pairs = eng.value_load(xnum[0:1, 0:1], min_val=0, max_val=MAXX // 2)
            with eng.If(pairs > 1):
                with eng.Fori(1, pairs) as i:
                    stages(i)
                finish(pairs * 2 + NE)
                tail()
            with eng.Else():
                finish(STEPS)
                tail()

        @block.sync
        def _(eng):
            for t in range(NT):
                eng.dma_start(h[:, t, :], x_v[t]).then_inc(x_in[t], 16)

            def load_win(n):
                if n >= 2:
                    eng.wait_ge(z_full, WIN_UNITS[n - 2])
                src = w_in_v[:, :, WIN_COLS[n]:WIN_COLS[n] + BANK] if n < 5 else \
                    w_out_v[:, :, (n - 5) * BANK:(n - 4) * BANK]
                eng.dma_start(win[:, n % 2], src).then_inc(win_in[n % 2], 16)

            load_win(0)
            load_win(1)

            def small(dst, src):
                with nc.allow_non_contiguous_dma(reason="small columns"):
                    eng.dma_start(dst, src).then_inc(small_in, 16)

            def rows(dst, src):
                eng.dma_start(dst, src.to_broadcast([P, src.shape[1]])).then_inc(small_in, 16)

            with nc.allow_non_contiguous_dma(reason="a number for each token"):
                eng.dma_start(posi[:, :], positions[0].rearrange("(t p) -> p t", p=P)).then_inc(rope_in, 16)
            for j, v in enumerate((lq1, lk1, lq2, lk2)):
                rows(lqk[:, j, :], v)
            small(cw[:, :, :], conv_w[0].rearrange("w (c p) -> p w c", p=P))
            small(cols[:, CB, :], conv_b[0].rearrange("(c p) -> p c", p=P))
            small(cols[:, BA, :], b_a[0].rearrange("(c b) j -> (b j) c", b=2))
            small(cols[:, BI, :], b_i[0].rearrange("(c b) j -> (b j) c", b=2))
            small(cols[:, RL, :], rg_lambda[0].rearrange("(c p) -> p c", p=P))
            small(cols[:, GR, :], g_rec[0].rearrange("(c p) -> p c", p=P))
            small(gsub[:, :], g_sub[0].rearrange("(d a) -> d a", a=1))
            rows(ebias[:, :], e_bias)
            eng.wait_ge(bd_zero, 2)
            for b in range(2):
                for dst, src in ((wab, w_a), (wib, w_i)):
                    eng.dma_start(dst[b * HALF:(b + 1) * HALF, :, b * HALF:(b + 1) * HALF],
                                  src[0].rearrange("(c b) i j -> b i c j", b=2)[b]).then_inc(bd_in, 16)
            eng.dma_start(wr[:, :, :], w_router[0].rearrange("(p c) e -> p c e", c=KC)).then_inc(wr_in, 16)


            def load_up(e, s):
                for j, src in enumerate(expert_up(e)):
                    eng.dma_start(wup[s][:, :, j, :], src).then_inc(up_in[s], 16)

            def load_dn(e, s):
                eng.dma_start(wdn[s], expert_dn(e)).then_inc(dn_in[s], 16)

            load_up(0, 0)
            load_dn(0, 0)
            for n in range(2, 7):
                load_win(n)
            def store_row(t):
                eng.wait_ge(row_done, NT + t + 1)
                eng.dma_start(hf_v[t], rowbuf[:, t % 2, :]).then_inc(hf_stored[t % 2], 16)
            eng.wait_ge(mix_full, NT * HALVES)
            eng.dma_start(wup[3][:, :, 0, :], ws1[0].rearrange("(p c) f -> p c f", c=KC)).then_inc(sw_in, 16)
            eng.dma_start(wup[3][:, :, 1, :], ws3[0].rearrange("(p c) f -> p c f", c=KC)).then_inc(sw_in, 16)
            eng.dma_start(wdn[3], ws2[0].rearrange("(p c) n -> p c n", c=FC)).then_inc(sw_in, 16)
            for t in range(NT):
                store_row(t)
            for s in (1, 2):
                load_up(s, s)
                load_dn(s, s)
            eng.wait_ge(sh_dn, NT * HALVES)
            load_up(3, 3)
            load_dn(3, 3)

            def refill_up(e, s, step):
                up_src = expert_up(e)
                up_read = step - (U - 1) if isinstance(step, int) else eng.snap(step - (U - 1))
                eng.wait_ge(up_full, up_read)
                for j, src in enumerate(up_src):
                    eng.dma_start(wup[s][:, :, j, :], src).then_inc(up_in[s], 16)

            def refill_dn(e, s, step):
                dn_src = expert_dn(e)
                dn_read = (step - (U - 1)) * HALVES if isinstance(step, int) else eng.snap((step - (U - 1)) * HALVES)
                eng.wait_ge(dn_full, dn_read)
                eng.dma_start(wdn[s], dn_src).then_inc(dn_in[s], 16)

            refill_up(U, 0, U)
            with eng.Fori(1, NE // U - 1) as i:
                for s in range(U):
                    e = eng.snap(i * U + s)
                    e_next = eng.snap(e + 1)
                    refill_up(e_next, (s + 1) % U, e_next)
                    refill_dn(e, s, e)
            eng.wait_ge(routes, 1)
            expert_of = list(range(NE)) + [eng.value_load(xtab[0:1, 0, j:j + 1], min_val=0, max_val=NE - 1) for j in range(2)]
            for e in range(NE - U, STEPS):
                if e + 1 < STEPS:
                    refill_up(expert_of[e + 1], (e + 1) % U, e + 1)
                refill_dn(expert_of[e], e % U, e)
            eng.dma_start(wpp, w_ple_proj[0].rearrange("(p c) n -> p c n", c=DPLE // P)).then_inc(pw_in, 16)
            eng.dma_start(prow, p_v.rearrange("t p n -> p t n")).then_inc(pw_in, 16)
            eng.wait_ge(dn_full, HALVES * NE)
            eng.dma_start(wpg, w_ple_gate[0].rearrange("(p c) n -> p c n", c=KC)).then_inc(wpg_in, 16)
            pairs = eng.value_load(xnum[0:1, 0:1], min_val=0, max_val=MAXX // 2)
            with eng.If(pairs > 1):
                with eng.Fori(1, pairs) as i:
                    for j in range(2):
                        e = eng.value_load(xtab[0:1, 0, bass.ds(i * 2 + j, 1)], min_val=0, max_val=NE - 1)
                        up_src, dn_src = expert_up(e), expert_dn(e)
                        up_read = eng.snap(i * 2 + (NE + j - 1))
                        dn_read = eng.snap(up_read * HALVES)
                        eng.wait_ge(up_full, up_read)
                        for w, src in enumerate(up_src):
                            eng.dma_start(wup[j][:, :, w, :], src).then_inc(up_in[j], 16)
                        eng.wait_ge(dn_full, dn_read)
                        eng.dma_start(wdn[j], dn_src).then_inc(dn_in[j], 16)
            with eng.Else():
                eng.nop()

            eng.wait_ge(experts_done_t, 1)
            eng.wait_ge(routed_done, 2)
            for t in range(NT):
                if t >= 2:
                    eng.wait_ge(plane_used, t - 1)
                for g in range(4):
                    eng.dma_start(planes[:, t % 2, 2 * g:2 * g + 2], routed_v[t][:, 2 * g:2 * g + 2]).then_inc(plane_in[t % 2][g], 16)
            for t in range(NT):
                eng.wait_ge(orow_done, t + 1)
                eng.dma_start(out_v[t], pproj[:, t, :]).then_inc(stored[t % 2], 16)
            for r in range(2):
                eng.wait_ge(stored[r], 16 * NT // 2)

        @block.scalar
        def _(eng):
            act = nc.scalar

            def load_gain(src):
                eng.dma_start(gain[:, :], src.to_broadcast([P, D])).then_inc(gain_in, 16)

            load_gain(ln_mix)
            def squares(n, t):
                if n or t:
                    eng.wait_ge(ssq_done, norm_count(n, t))
                act.activation(junk, h[:, t, :], ACT.Square, accum_out=ssq[:, n, t:t + 1]).then_inc(ssq_done, 1)

            def root(n, t):
                eng.wait_ge(ms_done, norm_count(n, t) + 1)
                act.activation(rstd[:, n, t:t + 1], rstd[:, n, t:t + 1], ACT.Sqrt).then_inc(root_done, 1)

            def row_evac(n, t):
                eng.wait_ge(row_T, HALVES * (NT * n + t) + 1)
                act.activation(hT[:, 0:4, t * P:(t + 1) * P],
                               PS[:, (2 * t) % 4, :].rearrange("p (c n) -> p c n", n=P), ACT.Copy).then_inc(row_evac_a, 1)

            for t in range(NT):
                eng.wait_ge(x_in[t], 16)
                squares(0, t)
            for t in range(NT):
                root(0, t)
                row_evac(0, t)
            eng.wait_ge(rope_ready, 1)
            act.activation(cs[:, :, :, :], ang[:, :, :, :], ACT.Sin).then_inc(rope_ready, 1)
            eng.wait_ge(lam_v, 3)
            act.activation(lam[:, 2:4], lam[:, 0:2], ACT.Exp).then_inc(lam_a, 1)
            act.activation(spt[:, 1, :], spt[:, 0, :], ACT.Exp).then_inc(lam_a, 1)

            for n in range(3 * NT):
                eng.wait_ge(z_full, n + 1)
                if n < 2 * NT:
                    if n >= 2:
                        eng.wait_ge(qk_T, n - 1)
                    dst = qk[:, n % 2, :]
                else:
                    dst = vv[:, n - 2 * NT, :]
                act.activation(dst, PS[:, n % 2, :], ACT.Copy).then_inc(z_free, 1)

            def evac_z(k):
                n = ring_at[("Z", k)]
                eng.wait_ge(z_full, n + 1)
                if k < RC:
                    if k == 0:
                        eng.wait_ge(bd_zero, 3)
                    else:
                        eng.wait_ge(rec_conv, k)
                    act.activation(xr[:, 3:3 + T], PS[:, n % 2, :], ACT.Copy).then_inc(z_free, 1)
                else:
                    if k > RC:
                        eng.wait_ge(rec_y, k - RC)
                    act.activation(gs, PS[:, n % 2, :], ACT.Copy).then_inc(z_free, 1)
                    eng.wait_ge(z_free, n + 1)
                    act.activation(gq, gs, ACT.Square).then_inc(gate_sq, 1)

            def gates(c):
                for what, dst, bias in (("R", rg, BA), ("I", ig, BI)):
                    n = ring_at[(what, c)]
                    eng.wait_ge(z_full, n + 1)
                    if c:
                        eng.wait_ge(rec_h, c)
                    act.activation(dst, PS[:, n % 2, :], ACT.Sigmoid, bias=cols[:, bias, c:c + 1]).then_inc(z_free, 1)

            def exps(s):
                i = s // H
                nk = (i + 1) * P
                eng.wait_ge(att_max, s + 1)
                if s >= 2:
                    eng.wait_ge(att_w, s - 1)
                for c in range(2):
                    act.activation(pr[:, s % 2, c, 0:nk], PS[:, 2 + 2 * (s % 2) + c, 0:nk], ACT.Exp,
                                   bias=nmx[:, s % 2, c:c + 1], scale=HALF ** -0.5,
                                   accum_out=sums[:, s % 2, c:c + 1]).then_inc(att_exp, 1)

            def evac_wT(s):
                nk = (s // H + 1) * P
                eng.wait_ge(att_t, s + 1)
                if s >= 2:
                    eng.wait_ge(att_pv, s - 1)
                act.activation(wT[:, s % 2, 0:nk], PS[:, 6 + s % 2, 0:nk], ACT.Copy).then_inc(att_wt, 1)

            def evac_o(s):
                eng.wait_ge(att_pv, s + 1)
                act.activation(ob[:, s, :], PS[:, 6 + s % 2, 0:DV], ACT.Copy).then_inc(att_o, 1)
                if s:
                    eng.wait_ge(att_o, 2 * s)
                act.activation(ojunk[:, :], PS[:, 6 + s % 2, 0:DV], ACT.Square,
                               accum_out=oss[:, s:s + 1]).then_inc(att_o, 1)

            eng.wait_ge(ssq_done, NT)
            for k in range(NSLOT):
                if k < 2 * RC:
                    evac_z(k)
                if 1 <= k <= RC:
                    gates(k - 1)
                if k < 8:
                    exps(2 * k)
                    exps(2 * k + 1)
                if 1 <= k <= RC:
                    c = k - 1
                    eng.wait_ge(rec_la, c + 1)
                    act.activation(th, rg, ACT.Tanh).then_inc(rec_ta, 1)
                    act.activation(aa, rg, ACT.Exp, scale=-1.0).then_inc(rec_ta, 1)
                if k >= 1:
                    evac_wT(2 * k - 2)
                    evac_wT(2 * k - 1)
                    evac_o(2 * k - 2)
                    evac_o(2 * k - 1)
                if 1 <= k <= RC:
                    eng.wait_ge(rec_q, k)
                    act.activation(th, th, ACT.Sqrt, scale=2.0).then_inc(rec_m, 1)
                if RC <= k < 2 * RC:
                    eng.wait_ge(gate_t, k - RC + 1)
                    act.activation(gq, gt, ACT.Tanh, scale=GELU_B).then_inc(gate_th, 1)
            eng.wait_ge(mixn_v, 1)
            act.activation(ors[:, :], ors[:, :], ACT.Sqrt).then_inc(mixn_a, 1)
            eng.wait_ge(mixn_v, 2)
            act.activation(gs, gs, ACT.Sqrt).then_inc(mixn_a, 1)

            eng.wait_ge(row_done, NT)
            load_gain(ln_moe)
            for t in range(NT):
                eng.wait_ge(h1_done, HALVES * (t + 1))
                squares(1, t)
                root(1, t)
                if t:
                    row_evac(1, t - 1)
            row_evac(1, NT - 1)
            eng.wait_ge(row_done, 2 * NT)
            load_gain(ln_ple)
            eng.wait_ge(rt_full, NT)
            act.activation(scores, PS[:, 4, 0:NT * NE].rearrange("p (t e) -> p t e", e=NE), ACT.Sigmoid).then_inc(rt_sig, 1)

            for t in range(NT + 1):
                if t < NT:
                    eng.wait_ge(sh_up, t + 1)
                    if t >= 2:
                        eng.wait_ge(sh_h, t - 1)
                    act.activation(sgb[:, t % 2, :], PS[:, 6 + t % 2, 0:F], ACT.Sigmoid).then_inc(sh_sig, 1)
                if t:
                    eng.wait_ge(sh_T, t)
                    if t >= 3:
                        eng.wait_ge(sh_dn, HALVES * (t - 2))
                    act.activation(hTe[:, (t - 1) % 2], PS[:, 2 + (t - 1) % 2, 0:F].rearrange("p (c n) -> p c n", n=P),
                                   ACT.Copy).then_inc(sh_hT, 1)

            def tx(e, s):
                for j in range(HALVES):
                    eng.wait_ge(tx_full, HALVES * e + j + 1)
                    if not isinstance(e, int) or e >= 2:
                        eng.wait_ge(up_full, e - 1)
                    act.activation(xgT[:, s % 2, 4 * j:4 * j + 4, :],
                                   PS[:, 2 + j, :].rearrange("p (c n) -> p c n", n=P), ACT.Copy).then_inc(tx_evac, 1)

            def sig(e, s):
                eng.wait_ge(up_full, e + 1)
                if not isinstance(e, int) or e >= 2:
                    eng.wait_ge(h_done, e - 1)
                act.activation(sgb[:, s % 2, :], PS[:, s % 2, 0:F], ACT.Sigmoid).then_inc(sg_done, 1)

            def hidden_evac(e, s):
                eng.wait_ge(ht_full, e + 1)
                if not isinstance(e, int) or e >= 2:
                    eng.wait_ge(dn_full, HALVES * (e - 1))
                act.activation(hTe[:, s % 2], PS[:, 4, 0:F].rearrange("p (c n) -> p c n", n=P), ACT.Copy).then_inc(ht_evac, 1)

            def down_evac(e, s):
                eng.wait_ge(dn_full, HALVES * e + 1)
                if not isinstance(e, int) or e >= 2:
                    eng.wait_ge(scattered[s % 2], scatters_before(e, s))
                eng.wait_ge(dest_done, 2 * e + 2)
                act.activation(yb[:, s % 2, 0:BANK], PS[:, 6, :], ACT.Copy, scale=wgt[:, s:s + 1]).then_inc(y_evac_a, 1)

            def turn(e, s, first=False, last=False):
                if not last:
                    tx(e + 1, (s + 1) % U)
                if not first:
                    hidden_evac(e - 1, (s - 1) % U)
                sig(e, s)
                if not first:
                    down_evac(e - 1, (s - 1) % U)

            eng.wait_ge(sh_h, NT)
            eng.wait_ge(sh_dn, NT * HALVES)
            tx(0, 0)
            for s in range(U):
                turn(s, s, first=(s == 0))
            with eng.Fori(1, NE // U - 1) as i:
                for s in range(U):
                    turn(i * U + s, s)
            for s in range(U):
                turn(NE - U + s, s)
            for e in range(NE, STEPS):
                turn(e, e % U, last=(e == STEPS - 1))
            hidden_evac(STEPS - 1, (STEPS - 1) % U)
            down_evac(STEPS - 1, (STEPS - 1) % U)

            def pair(i):
                for stages in ((tx,), (sig,), (hidden_evac, down_evac)):
                    for j in range(2):
                        for stage in stages:
                            stage(i * 2 + (NE + j), j)

            extra_steps(eng, pair, lambda steps: eng.wait_ge(y_evac_a, steps), lambda: eng.sem_inc(experts_done_a, 1))

            eng.wait_ge(experts_done_t, 1)
            eng.wait_ge(experts_done_v, 1)
            eng.wait_ge(routed_done, 2)
            eng.dma_start(gain_f, ln_f.to_broadcast([P, D])).then_inc(gain_f_in, 16)
            for u in range(NT * HALVES):
                t, n = divmod(u, HALVES)
                eng.wait_ge(pp_full, u + 1)
                act.activation(pproj[:, t, n * BANK:(n + 1) * BANK], PS[:, 6 + u % 2, :], ACT.Copy).then_inc(pproj_done, 1)

            def gate(u):
                eng.wait_ge(pg_full, u + 1)
                if u >= 2:
                    eng.wait_ge(ple_done, u - 1)
                act.activation(sg2[:, u % 2, :], PS[:, 4 + u % 2, :], ACT.Sigmoid).then_inc(pg_sig, 1)

            def last_norm(t):
                eng.wait_ge(ple_done, HALVES * (t + 1))
                squares(3, t)
                root(3, t)

            eng.wait_ge(sums_done, 1)
            squares(2, 0)
            root(2, 0)
            row_evac(2, 0)
            eng.wait_ge(sums_done, 2)
            squares(2, 1)
            root(2, 1)
            for t in range(NT):
                gate(HALVES * t)
                if t + 1 < NT:
                    row_evac(2, t + 1)
                if t + 2 < NT:
                    eng.wait_ge(sums_done, t + 3)
                    squares(2, t + 2)
                    root(2, t + 2)
                gate(HALVES * t + 1)
                if t:
                    last_norm(t - 1)
            last_norm(NT - 1)

        @block.vector
        def _(eng):
            v = nc.vector
            ch = Chain(eng, dve)

            def mean_square(n, t):
                eng.wait_ge(ssq_done, norm_count(n, t) + 1)
                v.tensor_scalar(rstd[:, n, t:t + 1], ssq[:, n, t:t + 1], 1.0 / D, EPS, ALU.mult, ALU.add).then_inc(ms_done, 1)

            def row(n, t, dst):
                eng.wait_ge(root_done, norm_count(n, t) + 1)
                ch.link(v.reciprocal(rstd[:, n, t:t + 1], rstd[:, n, t:t + 1]))
                if n == 3:
                    eng.wait_ge(gain_f_in, 16)
                else:
                    eng.wait_ge(gain_in, 16 * (n + 1))
                return v.scalar_tensor_tensor(out=dst, in0=h[:, t, :], scalar=rstd[:, n, t:t + 1],
                                              in1=gain_f if n == 3 else gain[:, :], op0=ALU.mult, op1=ALU.mult)

            def row_evac(n, t):
                eng.wait_ge(row_T, HALVES * (NT * n + t) + 2)
                v.tensor_copy(hT[:, 4:8, t * P:(t + 1) * P],
                              PS[:, (2 * t + 1) % 4, :].rearrange("p (c n) -> p c n", n=P)).then_inc(row_evac_v, 1)

            for t in range(NT):
                mean_square(0, t)
            for t in range(NT):
                if t >= 2:
                    eng.wait_ge(row_T, HALVES * (t - 1))
                row(0, t, rowbuf[:, t % 2, :]).then_inc(row_done, 1)
                if t:
                    row_evac(0, t - 1)
            row_evac(0, NT - 1)

            inv = [float(np.float32(500000.0) ** np.float32(-2 * j / ROPE)) for j in range(RH)]
            eng.wait_ge(rope_in, 16)
            ch.link(v.tensor_copy(posf[:, :], posi[:, :]))
            for j in range(RH):
                ch.mark(v.tensor_scalar(ang[:, 0, :, j], posf[:, :], inv[j], None, ALU.mult))
            ch.sync()
            ch.mark(v.tensor_scalar(kk[:, 0], ang[:, 0], float(1 / (2 * np.pi)), 12582912.0, ALU.mult, ALU.add))
            ch.link(v.tensor_scalar(ang[:, 1], ang[:, 0], float(1 / (2 * np.pi)), 0.25, ALU.mult, ALU.add))
            ch.link(v.tensor_scalar(kk[:, 1], ang[:, 1], 12582912.0, None, ALU.add))
            ch.link(v.tensor_scalar(kk[:, :], kk[:, :], 12582912.0, None, ALU.subtract))
            ch.link(v.tensor_copy(ang[:, 1], ang[:, 0]))
            c1, c2 = 6.28125, float(np.float32(2 * np.pi - 6.28125))
            for c in (c1, c2):
                ch.link(v.scalar_tensor_tensor(out=ang[:, :, :, :].rearrange("p a t j -> p (a t j)"),
                                               in0=kk[:, :, :, :].rearrange("p a t j -> p (a t j)"), scalar=-c,
                                               in1=ang[:, :, :, :].rearrange("p a t j -> p (a t j)"), op0=ALU.mult, op1=ALU.add))
            ch.link(v.tensor_scalar(ang[:, 1], ang[:, 1], float(np.pi / 2), None, ALU.add))
            v.tensor_scalar(ang[:, :], ang[:, :], 3.1415925, -3.1415925, ALU.min, ALU.max).then_inc(rope_ready, 1)

            eng.wait_ge(small_in, 16 * 12)
            for j in range(2):
                v.tensor_tensor_reduce(ljunk[:, j, :], lqk[:, 2 * j, :], lqk[:, 2 * j + 1, :], 1.0, 0.0, ALU.mult, ALU.add,
                                       lam[:, j:j + 1]).then_inc(lam_v, 1)
            L = cols[:, RL, :]
            ch.link(v.tensor_scalar(spt[:, 1, :], L, -1.0, None, ALU.mult))
            ch.link(v.tensor_tensor(spt[:, 0, :], L, spt[:, 1, :], ALU.min))
            ch.link(v.tensor_scalar(cols[:, SP8, :], spt[:, 1, :], 0.0, None, ALU.max))
            eng.sem_inc(lam_v, 1)
            eng.wait_ge(lam_a, 2)
            ch.link(v.tensor_tensor(lam[:, 0:1], lam[:, 3:4], lam[:, 2:3], ALU.subtract))
            ch.link(v.tensor_scalar(lam[:, 0:1], lam[:, 0:1], LAM_INIT, None, ALU.subtract))
            y0, s0, s2, acc = spt[:, 1, :], spt[:, 0, :], spt[:, 2, :], spt[:, 3, :]
            ch.link(v.tensor_scalar(s0, y0, 2.0, None, ALU.add))
            ch.link(v.reciprocal(s0, s0))
            ch.link(v.tensor_tensor(s0, s0, y0, ALU.mult))
            ch.link(v.tensor_tensor(s2, s0, s0, ALU.mult))
            ch.link(v.tensor_scalar(acc, s2, 1.0 / 17, 1.0 / 15, ALU.mult, ALU.add))
            for d in (13, 11, 9, 7, 5, 3, 1):
                ch.link(v.tensor_tensor(acc, acc, s2, ALU.mult))
                ch.link(v.tensor_scalar(acc, acc, 1.0 / d, None, ALU.add))
            ch.link(v.tensor_tensor(acc, acc, s0, ALU.mult))
            ch.link(v.scalar_tensor_tensor(out=cols[:, SP8, :], in0=acc, scalar=2.0, in1=cols[:, SP8, :],
                                           op0=ALU.mult, op1=ALU.add))
            ch.link(v.tensor_scalar(cols[:, SP8, :], cols[:, SP8, :], RG_C, None, ALU.mult))

            def rope(n):
                t = n % NT
                eng.wait_ge(z_free, n + 1)
                g = qk[:, n % 2, :].rearrange("p (g d) -> p g d", d=HALF)
                x1, x2 = g[:, :, 0:RH], g[:, :, RH:ROPE]
                sn = cs[:, 0, t, :].unsqueeze(1).to_broadcast([P, 8, RH])
                cn = cs[:, 1, t, :].unsqueeze(1).to_broadcast([P, 8, RH])
                if n:
                    eng.wait_ge(rope_done, 2 * n)
                ch.mark(v.tensor_tensor(rp[:, 0], x1, cn, ALU.mult))
                ch.mark(v.tensor_tensor(rp[:, 1], x2, sn, ALU.mult))
                ch.mark(v.tensor_tensor(rp[:, 2], x2, cn, ALU.mult))
                ch.link(v.tensor_tensor(rp[:, 3], x1, sn, ALU.mult))
                v.tensor_tensor(x1, rp[:, 0], rp[:, 1], ALU.subtract).then_inc(rope_done, 1)
                v.tensor_tensor(x2, rp[:, 2], rp[:, 3], ALU.add).then_inc(rope_done, 1)

            def evac_qk(n):
                t = n % NT
                eng.wait_ge(qk_T, n + 1)
                dst = qT if n < NT else kT
                v.tensor_copy(dst[:, :, t * P:(t + 1) * P],
                              PS[:, 2 + n % 2, :].rearrange("p (h n) -> p h n", n=P)).then_inc(qk_evac, 1)

            eng.wait_ge(rope_ready, 2)
            for n in range(2 * NT + 1):
                if n < 2 * NT:
                    rope(n)
                if n:
                    evac_qk(n - 1)

            def conv(k):
                eng.wait_ge(z_free, ring_at[("Z", k)] + 1)
                o = xc[:, k % 2, :]
                ch.link(v.tensor_scalar(o, xr[:, 0:T], cw[:, 0, k:k + 1], cols[:, CB, k:k + 1], ALU.mult, ALU.add))
                for j in (1, 2):
                    ch.link(v.scalar_tensor_tensor(out=o, in0=xr[:, j:j + T], scalar=cw[:, j, k:k + 1], in1=o,
                                                   op0=ALU.mult, op1=ALU.add))
                v.scalar_tensor_tensor(out=o, in0=xr[:, 3:3 + T], scalar=cw[:, 3, k:k + 1], in1=o,
                                       op0=ALU.mult, op1=ALU.add).then_inc(rec_conv, 1)

            def smax(s):
                i = s // H
                nk = (i + 1) * P
                b = 2 + 2 * (s % 2)
                eng.wait_ge(att_s, 2 * s + 2)
                diag = PS[:, b:b + 2, i * P:nk]
                ch.link(v.tensor_tensor(diag, diag, cmask[:, :].unsqueeze(1).to_broadcast([P, 2, P]), ALU.add))
                ch.link(v.tensor_reduce(mx[:, s % 2, :], PS[:, b:b + 2, 0:nk], AX_X, ALU.max))
                if s >= 2:
                    eng.wait_ge(att_exp, 2 * (s - 1))
                v.tensor_scalar(nmx[:, s % 2, :], mx[:, s % 2, :], -HALF ** -0.5, None, ALU.mult).then_inc(att_max, 1)

            def combine(s):
                nk = (s // H + 1) * P
                eng.wait_ge(att_exp, 2 * (s + 1))
                ch.link(v.reciprocal(rec[:, s % 2, :], sums[:, s % 2, :]))
                ch.link(v.tensor_tensor(rec[:, s % 2, 1:2], rec[:, s % 2, 1:2], lam[:, 0:1], ALU.mult))
                if s >= 2:
                    eng.wait_ge(att_t, s - 1)
                w = wb[:, s % 2, 0:nk]
                ch.link(v.tensor_scalar(w, pr[:, s % 2, 0, 0:nk], rec[:, s % 2, 0:1], None, ALU.mult))
                v.scalar_tensor_tensor(out=w, in0=pr[:, s % 2, 1, 0:nk], scalar=rec[:, s % 2, 1:2], in1=w,
                                       op0=ALU.mult, op1=ALU.add).then_inc(att_w, 1)

            for k in range(NSLOT):
                if k < RC:
                    conv(k)
                if k < 8:
                    smax(2 * k)
                    smax(2 * k + 1)
                if 1 <= k <= RC:
                    c = k - 1
                    eng.wait_ge(z_free, ring_at[("I", c)] + 1)
                    v.tensor_scalar(rg, rg, cols[:, SP8, c:c + 1], None, ALU.mult).then_inc(rec_la, 1)
                if k < 8:
                    combine(2 * k)
                    combine(2 * k + 1)
                if 1 <= k <= RC:
                    c = k - 1
                    eng.wait_ge(rec_ta, 2 * k)
                    ch.link(v.tensor_scalar(rg, th, 1.0, None, ALU.add))
                    ch.link(v.reciprocal(rg, rg))
                    v.tensor_tensor(th, th, rg, ALU.mult).then_inc(rec_q, 1)
                    ch.link(v.tensor_tensor(ig, ig, xc[:, c % 2, :], ALU.mult))
                    eng.wait_ge(rec_m, k)
                    ch.link(v.tensor_tensor(ig, ig, th, ALU.mult))
                    v.tensor_tensor_scan(yT[:, c, :], aa, ig, 0.0, ALU.mult, ALU.add).then_inc(rec_h, 1)
                if RC <= k < 2 * RC:
                    c = k - RC
                    eng.wait_ge(gate_sq, c + 1)
                    ch.link(v.tensor_scalar(gt, gq, GELU_A, 1.0, ALU.mult, ALU.add))
                    v.tensor_tensor(gt, gt, gs, ALU.mult).then_inc(gate_t, 1)
                    eng.wait_ge(gate_th, c + 1)
                    ch.link(v.scalar_tensor_tensor(out=gq, in0=gq, scalar=1.0, in1=gs, op0=ALU.add, op1=ALU.mult))
                    eng.wait_ge(rec_h, RC)
                    ch.link(v.scalar_tensor_tensor(out=yT[:, c, :], in0=gq, scalar=0.5, in1=yT[:, c, :],
                                                   op0=ALU.mult, op1=ALU.mult))
                    v.tensor_tensor(ysq[:, c, :], yT[:, c, :], yT[:, c, :], ALU.mult).then_inc(rec_y, 1)
            eng.wait_ge(att_o, 2 * NS)
            v.tensor_scalar(ors[:, :], oss[:, :], 1.0 / DV, EPS, ALU.mult, ALU.add).then_inc(mixn_v, 1)
            eng.wait_ge(rec_ss, 1)
            eng.wait_ge(rec_y, RC)
            v.tensor_scalar(gs, PS[:, 0, :], 1.0 / DR, EPS, ALU.mult, ALU.add).then_inc(mixn_v, 1)
            eng.wait_ge(mixn_a, 1)
            ch.link(v.reciprocal(ors[:, :], ors[:, :]))
            v.tensor_tensor(ob, ob, ors[:, :].unsqueeze(2).to_broadcast([P, NS, DV]), ALU.mult).then_inc(o_norm, 1)
            eng.wait_ge(mixn_a, 2)
            ch.link(v.reciprocal(gs, gs))
            for c in range(RC):
                v.scalar_tensor_tensor(out=yT[:, c, :], in0=yT[:, c, :], scalar=cols[:, GR, c:c + 1], in1=gs,
                                       op0=ALU.mult, op1=ALU.mult).then_inc(y_ready, 1)
            for i in range(NT):
                eng.wait_ge(o_T, i + 1)
                v.tensor_scalar(yT[:, RC:2 * RC, i * P:(i + 1) * P], PS[:, 2 + i, :].rearrange("p (h n) -> p h n", n=P),
                                gsub[:, :], 1.0 - LAM_INIT, ALU.mult, ALU.mult).then_inc(y_ready, 1)

            for t in range(NT):
                for n in range(HALVES):
                    u = HALVES * t + n
                    eng.wait_ge(mix_full, u + 1)
                    hh = h[:, t, n * BANK:(n + 1) * BANK]
                    v.tensor_tensor(hh, hh, PS[:, u, :], ALU.add).then_inc(h1_done, 1)
                mean_square(1, t)
                if t >= 2:
                    eng.wait_ge(row_T, HALVES * (NT + t - 1))
                    eng.wait_ge(hf_stored[t % 2], 16 * (t // 2))
                row(1, t, rowbuf[:, t % 2, :]).then_inc(row_done, 1)
                if t:
                    row_evac(1, t - 1)
            row_evac(1, NT - 1)

            ch.mark(v.memset(gsc[:, :, :], NEG))
            ch.mark(v.memset(gthr[:, :, :], NEG))
            eng.wait_ge(rt_sig, 1)
            ch.link(v.tensor_tensor(sel, scores, ebias[:, :].unsqueeze(1).to_broadcast([P, NT, NE]), ALU.add))
            for t in range(NT):
                for g in range(NG):
                    ch.mark(v.max(g8[:, t, g, :], sel[:, t, g * GE:(g + 1) * GE]))
            ch.sync()
            ch.link(v.tensor_tensor(gsc[:, :, 0:NG], g8[:, :, :, 0], g8[:, :, :, 1], ALU.add))
            for t in range(NT):
                ch.mark(v.max(gtop[:, t, :], gsc[:, t, :]))
            ch.sync()
            ch.link(v.tensor_copy(gthr[:, :, 0:TOPG], gtop[:, :, 0:TOPG]))
            for t in range(NT):
                ch.mark(v.match_replace(grep[:, t, :], gthr[:, t, :], gsc[:, t, :], BIG))
            ch.sync()
            ch.link(v.tensor_scalar(gmask[:, :, :], grep[:, :, 0:NG], BIG / 10, None, ALU.is_ge))
            ch.link(v.tensor_scalar(gpen[:, :, :], gmask[:, :, :], BIG, BIG, ALU.mult, ALU.subtract))
            selg = sel.rearrange("p t (g e) -> p (t g) e", e=GE)
            selmg = selm.rearrange("p t (g e) -> p (t g) e", e=GE)
            ch.link(v.tensor_tensor(selmg, selg, gmask[:, :, :].rearrange("p t g -> p (t g)").unsqueeze(2).to_broadcast([P, NT * NG, GE]), ALU.mult))
            ch.link(v.tensor_tensor(selmg, selmg, gpen[:, :, :].rearrange("p t g -> p (t g)").unsqueeze(2).to_broadcast([P, NT * NG, GE]), ALU.add))
            for t in range(NT):
                ch.mark(v.max(top8[:, t, :], selm[:, t, :]))
            ch.sync()
            for t in range(NT):
                ch.mark(v.match_replace(mk[:, t, :], top8[:, t, :], selm[:, t, :], BIG))
            ch.sync()
            ch.link(v.tensor_scalar(mk, mk, BIG / 10, None, ALU.is_ge))
            v.tensor_copy(mkb, mk).then_inc(mk_done, 1)
            ch.link(v.tensor_tensor(ww, mk, scores, ALU.mult))
            ch.link(v.tensor_reduce(den[:, :], ww, AX_X, ALU.add))
            ch.link(v.reciprocal(den[:, :], den[:, :]))
            ch.link(v.tensor_tensor(ww, ww, den[:, :].unsqueeze(2).to_broadcast([P, NT, NE]), ALU.mult))
            ch.link(v.tensor_scalar(ww, ww, ROUTE_SCALE, None, ALU.mult))
            ch.link(v.tensor_copy(VV[:, :, :, 3], ww))
            ch.link(v.tensor_tensor(rr, ww, VV[:, :, :, 3], ALU.subtract))
            ch.link(v.tensor_copy(VV[:, :, :, 4], rr))
            ch.link(v.tensor_tensor(VV[:, :, :, 5], rr, VV[:, :, :, 4], ALU.subtract))
            for t in range(NT):
                ch.mark(v.tensor_tensor_scan(cr[:, t, :], ones[:, 0:NE], mk[:, t, :], 0.0, ALU.mult, ALU.add))
            ch.sync()
            ch.link(v.tensor_tensor(cr, cr, mk, ALU.subtract))
            eng.wait_ge(consts, 3)
            for t in range(NT):
                hi = float(256 * (t // 2) - NOWHERE)
                ch.mark(v.tensor_scalar(VV[:, t, :, 0], ones[:, 0:NE], tlo[:, t:t + 1], None, ALU.mult))
                ch.mark(v.memset(VV[:, t, :, 1], hi))
                ch.mark(v.tensor_scalar(VV[:, t, :, 2], cr[:, t, :], float(T), hi, ALU.mult, ALU.add))
            eng.wait_ge(rank_full, NT + 1)
            R = PS[:, 5, 0:NT * NE].rearrange("p (t e) -> p t e", e=NE)
            ch.link(v.scalar_tensor_tensor(out=SL.rearrange("p t e -> p (t e)"), in0=PS[:, 5, 0:NT * NE], scalar=1.0,
                                           in1=mk.rearrange("p t e -> p (t e)"), op0=ALU.add, op1=ALU.mult))
            ch.link(v.tensor_scalar(SL, SL, -1.0, None, ALU.add))
            ch.link(v.tensor_copy(cnt, PS[:, 5, NT * NE:NT * NE + NE]))
            for b in range(1, MAXB):
                ch.mark(v.tensor_scalar(nxe[:, b - 1, :], cnt, b * P + 0.5, None, ALU.is_ge))
            ch.sync()
            ch.link(v.tensor_tensor(cnt, nxe[:, 0, :], nxe[:, 1, :], ALU.add))
            ch.link(v.tensor_tensor(cnt, cnt, nxe[:, 2, :], ALU.add))
            ch.link(v.tensor_tensor_scan(xev, ones[:, 0:NE], cnt, 0.0, ALU.mult, ALU.add))
            ch.link(v.tensor_tensor(cnt, xev, cnt, ALU.subtract))
            ch.mark(v.tensor_scalar(xcol[:, 2:3], xev[:, NE - 1:NE], 0.5, 0.25, ALU.mult, ALU.add))
            for b in range(1, MAXB):
                ch.mark(v.tensor_scalar(xpos[:, b - 1, :], cnt, float(b - 1), None, ALU.add))
            ch.sync()
            ch.link(v.tensor_scalar(xeq, xpos, pid[:, :], None, ALU.is_equal))
            ch.link(v.tensor_tensor(xeq, xeq, nxe, ALU.mult))
            ch.link(v.tensor_tensor(xsel, xeq, slots[:, 0, 0:NE].unsqueeze(1).to_broadcast([P, MAXB - 1, NE]), ALU.mult))
            ch.link(v.tensor_reduce(xcol[:, 0:1], xsel.rearrange("p b e -> p (b e)"), AX_X, ALU.add))
            for b in range(1, MAXB):
                ch.mark(v.tensor_scalar(xsel[:, b - 1, :], xeq[:, b - 1, :], float(b - MAXB), None, ALU.mult))
            ch.sync()
            ch.link(v.tensor_reduce(xcol[:, 1:2], xsel.rearrange("p b e -> p (b e)"), AX_X, ALU.add))
            v.tensor_scalar(xcol[:, 1:2], xcol[:, 1:2], float(MAXB), None, ALU.add).then_inc(xlist, 1)
            ch.link(v.tensor_copy(xnum[:, :], xcol[0:1, 2:3]))

            for t in range(NT + 1):
                if t < NT:
                    eng.wait_ge(sh_sig, t + 1)
                    ch.link(v.tensor_tensor(sgb[:, t % 2, :], sgb[:, t % 2, :], PS[:, 6 + t % 2, 0:F], ALU.mult))
                    if t >= 2:
                        eng.wait_ge(sh_T, t - 1)
                    v.tensor_tensor(hb[:, t % 2, :], sgb[:, t % 2, :], PS[:, 6 + t % 2, F:2 * F], ALU.mult).then_inc(sh_h, 1)
                if t:
                    for n in range(HALVES):
                        eng.wait_ge(sh_dn, HALVES * (t - 1) + n + 1)
                        hh = h[:, t - 1, n * BANK:(n + 1) * BANK]
                        v.tensor_tensor(hh, hh, PS[:, n, :], ALU.add).then_inc(sh_add, 1)

            def one_hot(e, s, expert=None, block=0):
                expert = e if expert is None else expert
                if not isinstance(e, int) or e >= 2:
                    eng.wait_ge(ix_full, e - 1)
                v.tensor_tensor(ohb[:, s % 2], slots[:, bass.ds(block, 1), :].to_broadcast([P, NT, P]),
                                SL[:, :, bass.ds(expert, 1)].to_broadcast([P, NT, P]), ALU.is_equal).then_inc(oh_done, 1)

            def indices(e, s, extra=False):
                eng.wait_ge(ix_full, e + 1)
                b = PS[:, 5, 0:6]
                if not isinstance(e, int) or e >= 2:
                    eng.wait_ge(tx_full, HALVES * (e - 1))
                v.tensor_scalar(ixg[:, s % 2:s % 2 + 1], b[:, 1:2], b[:, 0:1], float(NOWHERE), ALU.add, ALU.add).then_inc(ix_done, 1)
                if extra:
                    eng.wait_ge(dest_done, 2 * e - 2)
                elif not isinstance(e, int) or e >= U:
                    eng.wait_ge(dest_done, 2 * e - 2 * (U - 1))
                v.tensor_copy(raw[:, s, :], b).then_inc(ix_done, 1)

            def dest(e, s, extra=False):
                eng.wait_ge(ix_done, 2 * e + 2)
                if extra:
                    eng.wait_ge(y_evac_a, e - 1)
                    eng.wait_ge(y_evac_v, e - 1)
                    eng.wait_ge(scattered[s % 2], scatters_before(e, s))
                elif not isinstance(e, int) or e >= U:
                    eng.wait_ge(y_evac_a, e - (U - 1))
                    eng.wait_ge(y_evac_v, e - (U - 1))
                    eng.wait_ge(scattered[s % 2], scatters_before(e, s) - 16)
                r = raw[:, s, :]
                v.tensor_scalar(ixd[:, s:s + 1], r[:, 2:3], r[:, 0:1], float(NOWHERE), ALU.add, ALU.add).then_inc(dest_done, 1)
                v.tensor_reduce(wgt[:, s:s + 1], r[:, 3:6], AX_X, ALU.add).then_inc(dest_done, 1)

            def act_mul(e, s):
                eng.wait_ge(sg_done, e + 1)
                if not isinstance(e, int) or e >= 2:
                    eng.wait_ge(ht_full, e - 1)
                v.tensor_tensor(hb[:, s % 2, :], sgb[:, s % 2, :], PS[:, s % 2, 0:F], ALU.mult).then_inc(ht_step, 1)
                eng.wait_ge(ht_step, e + 1)
                v.tensor_tensor(hb[:, s % 2, :], hb[:, s % 2, :], PS[:, s % 2, F:2 * F], ALU.mult).then_inc(h_done, 1)

            def down_evac(e, s):
                eng.wait_ge(dn_full, HALVES * e + 2)
                eng.wait_ge(dest_done, 2 * e + 2)
                if not isinstance(e, int) or e >= 2:
                    eng.wait_ge(scattered[s % 2], scatters_before(e, s))
                v.tensor_scalar(yb[:, s % 2, BANK:D], PS[:, 7, :], wgt[:, s:s + 1], None, ALU.mult).then_inc(y_evac_v, 1)

            eng.wait_ge(xrow, 1)
            v.tensor_copy(xtab[:, :, :], PS[0:1, 5, 0:2 * P].rearrange("p (a x) -> p a x", a=2)).then_inc(routes, 1)
            ch.sync()
            one_hot(0, 0)
            one_hot(1, 1)
            indices(0, 0)
            one_hot(2, 2)
            indices(1, 1)
            one_hot(3, 3)
            indices(2, 2)

            def turn(e, s, first=False, left=U + 1, listed=None):
                if left > 4:
                    if isinstance(e, int) and e + 4 >= NE:
                        one_hot(e + 4, s, *listed[e + 4 - NE])
                    else:
                        one_hot(e + 4, s)
                if not first:
                    dest(e - 1, (s - 1) % U)
                if left > 3:
                    indices(e + 3, (s + 3) % U)
                act_mul(e, s)
                if not first:
                    down_evac(e - 1, (s - 1) % U)

            for s in range(U):
                turn(s, s, first=(s == 0))
            with eng.Fori(1, NE // U - 1) as i:
                for s in range(U):
                    turn(i * U + s, s)
            listed = [[eng.value_load(xtab[0:1, a, j:j + 1], min_val=0, max_val=(NE - 1, MAXB)[a]) for a in range(2)]
                      for j in range(2)]
            for e in range(NE - U, STEPS):
                turn(e, e % U, left=STEPS - e, listed=listed)
            dest(STEPS - 1, (STEPS - 1) % U)
            down_evac(STEPS - 1, (STEPS - 1) % U)
            eng.wait_ge(sh_add, HALVES * NT)

            def pair(i):
                for j in range(2):
                    e = eng.value_load(xtab[0:1, 0, bass.ds(i * 2 + j, 1)], min_val=0, max_val=NE - 1)
                    b = eng.value_load(xtab[0:1, 1, bass.ds(i * 2 + j, 1)], min_val=0, max_val=MAXB)
                    one_hot(i * 2 + (NE + j), j, e, b)
                for j in range(2):
                    indices(i * 2 + (NE + j), j, extra=True)
                for j in range(2):
                    act_mul(i * 2 + (NE + j), j)
                for j in range(2):
                    dest(i * 2 + (NE + j), j, extra=True)
                    down_evac(i * 2 + (NE + j), j)

            extra_steps(eng, pair, lambda steps: eng.wait_ge(y_evac_v, steps), lambda: eng.sem_inc(experts_done_v, 1))

            for u in range(DPLE // P):
                eng.wait_ge(p_T, u + 1)
                v.tensor_copy(pT[:, u, :], PS[:, u, :]).then_inc(p_evac, 1)

            def choice_sum(t):
                for j in (0, 2, 4, 6, 7):
                    if j < 6:
                        eng.wait_ge(pair_added, 3 * t + j // 2 + 1)
                    elif j == 6:
                        eng.wait_ge(plane_in[t % 2][3], 16 * (t // 2 + 1))
                    ins = v.tensor_tensor(h[:, t, :], h[:, t, :], planes[:, t % 2, j, :], ALU.add)
                    if j < TOPK - 1:
                        ch.link(ins)
                    else:
                        ins.then_inc(plane_used, 1)
                eng.wait_ge(plane_used, t + 1)
                eng.sem_inc(sums_done, 1)

            def ple_norm(t):
                mean_square(2, t)
                if t >= 2:
                    eng.wait_ge(row_T, HALVES * (2 * NT + t - 1))
                row(2, t, orow[:, t % 2, :]).then_inc(row_done, 1)

            def ple(u):
                t, n = divmod(u, HALVES)
                cols_ = slice(n * BANK, (n + 1) * BANK)
                eng.wait_ge(pg_sig, u + 1)
                eng.wait_ge(pproj_done, u + 1)
                v.tensor_tensor(sg2[:, u % 2, :], sg2[:, u % 2, :], pproj[:, t, cols_], ALU.mult).then_inc(ple_mul, 1)
                eng.wait_ge(ple_mul, u + 1)
                v.tensor_tensor(h[:, t, cols_], h[:, t, cols_], sg2[:, u % 2, :], ALU.add).then_inc(ple_done, 1)

            def last_norm(t):
                mean_square(3, t)
                row(3, t, pproj[:, t, :]).then_inc(orow_done, 1)

            choice_sum(0)
            ple_norm(0)
            row_evac(2, 0)
            choice_sum(1)
            ple_norm(1)
            for t in range(NT):
                ple(HALVES * t)
                if t + 1 < NT:
                    row_evac(2, t + 1)
                if t + 2 < NT:
                    choice_sum(t + 2)
                    ple_norm(t + 2)
                ple(HALVES * t + 1)
                if t:
                    last_norm(t - 1)
            last_norm(NT - 1)

        @block.gpsimd
        def _(eng):
            g = nc.gpsimd
            g.memset(ident[:, :], 0.0).then_inc(bd_zero, 1)
            eng.wait_ge(bd_zero, 1)
            g.memset(wab, 0.0)
            g.memset(wib, 0.0).then_inc(bd_zero, 1)
            g.memset(xr[:, 0:3], 0.0).then_inc(bd_zero, 1)
            g.affine_select(out=ident[:, :], in_=ident[:, :], compare_op=ALU.not_equal, fill=1.0, base=0,
                            pattern=[[-1, P]], channel_multiplier=1).then_inc(consts, 1)
            g.memset(ones[:, :], 1.0)
            g.memset(onesb[:, :], 1.0)
            g.memset(tri[:, :], 1.0)
            g.memset(cmask[:, :], 0.0)
            g.iota(slots[:, :, :], [[P, MAXB + 1], [1, P]], base=0, channel_multiplier=0, allow_small_or_imprecise_dtypes=True)
            g.iota(pid[:, :], [[0, 1]], base=0, channel_multiplier=1, allow_small_or_imprecise_dtypes=True)
            g.iota(tlo[:, :], [[0, 2], [P, 2]], base=0, channel_multiplier=1,
                   allow_small_or_imprecise_dtypes=True).then_inc(consts, 1)
            eng.wait_ge(consts, 2)
            g.affine_select(out=cmask[:, :], in_=cmask[:, :], compare_op=ALU.is_ge, fill=NEG, base=0,
                            pattern=[[-1, P]], channel_multiplier=1)
            g.affine_select(out=tri[:, :], in_=tri[:, :], compare_op=ALU.is_gt, fill=0.0, base=0,
                            pattern=[[1, P]], channel_multiplier=-1).then_inc(consts, 1)
            eng.wait_ge(mix_full, NT * HALVES)
            g.memset(xg, 0.0).then_inc(xg_zero, 1)

            def gather(e, s):
                eng.wait_ge(ix_done, 2 * e + 2)
                if not isinstance(e, int) or e >= 2:
                    eng.wait_ge(tx_full, HALVES * (e - 1))
                eng.sem_inc(pool_ready, 1)
                g.indirect_dma_start(xg[:, s % 2, :], None, hf_rows,
                                     bass.IndirectOffsetOnAxis(ap=ixg[:, s % 2:s % 2 + 1], axis=0),
                                     bounds_check=T - 1, oob_is_err=False).then_inc(gathered[s % 2], 16)

            def scatter(e, s):
                eng.wait_ge(y_evac_a, e + 1)
                eng.wait_ge(y_evac_v, e + 1)
                eng.sem_inc(pool_ready, 1)
                g.indirect_dma_start(routed, bass.IndirectOffsetOnAxis(ap=ixd[:, s:s + 1], axis=0),
                                     yb[:, s % 2, :], None,
                                     bounds_check=CHOICES - 1, oob_is_err=False).then_inc(scattered[s % 2], 16)

            eng.wait_ge(xg_zero, 1)
            for r in range(2):
                eng.wait_ge(hf_stored[r], 16 * NT // 2)
            gather(0, 0)
            gather(1, 1)
            gather(2, 2)

            def turn(e, s, first=False, left=U):
                if left > 3:
                    gather(e + 3, (s + 3) % U)
                if not first:
                    scatter(e - 1, (s - 1) % U)

            for s in range(U):
                turn(s, s, first=(s == 0))
            with eng.Fori(1, NE // U - 1) as i:
                for s in range(U):
                    turn(i * U + s, s)
            for e in range(NE - U, STEPS):
                turn(e, e % U, left=STEPS - e)
            scatter(STEPS - 1, (STEPS - 1) % U)

            def pair(i):
                for stage in (gather, scatter):
                    for j in range(2):
                        stage(i * 2 + (NE + j), j)

            def all_scattered(steps):
                for r in range(2):
                    eng.wait_ge(scattered[r], steps * 8)
                    eng.sem_inc(routed_done, 1)

            extra_steps(eng, pair, all_scattered, eng.nop)

            for t in range(NT):
                for k in range(3):
                    eng.wait_ge(plane_in[t % 2][k], 16 * (t // 2 + 1))
                    a, b = (planes[:, t % 2, 2 * k + i, :] for i in range(2))
                    g.tensor_tensor(a, a, b, ALU.add).then_inc(pair_added, 1)

        @block.tensor
        def _(eng):
            pe = nc.tensor
            eng.wait_ge(consts, 3)

            def row_T_(n, t, src):
                for j in range(HALVES):
                    b = (2 * t + j) % 4
                    if t >= 2:
                        eng.wait_ge((row_evac_a, row_evac_v)[j], NT * n + t - 1)
                    for c in range(4):
                        mm = pe.transpose(PS[:, b, c * P:(c + 1) * P],
                                          src.rearrange("p (q c) -> p c q", c=KC)[:, 4 * j + c, :], ident[:, :])
                    mm.then_inc(row_T, 1)

            for t in range(NT):
                eng.wait_ge(row_done, t + 1)
                row_T_(0, t, rowbuf[:, t % 2, :])
            eng.wait_ge(row_evac_a, NT)
            eng.wait_ge(row_evac_v, NT)

            def unit(n, pairs):
                if n >= 2:
                    eng.wait_ge(z_free, n - 1)
                for j, (a, b) in enumerate(pairs):
                    mm = pe.matmul(PS[:, n % 2, :], a, b, start=(j == 0), stop=(j == len(pairs) - 1))
                mm.then_inc(z_full, 1)

            def qk_T_(n):
                eng.wait_ge(rope_done, 2 * n + 2)
                if n >= 2:
                    eng.wait_ge(qk_evac, n - 1)
                for hh in range(H):
                    mm = pe.transpose(PS[:, 2 + n % 2, hh * P:(hh + 1) * P], qk[:, n % 2, hh * P:(hh + 1) * P], ident[:, :])
                mm.then_inc(qk_T, 1)

            for n in range(3 * NT):
                j, t = divmod(n, NT)
                if t == 0:
                    eng.wait_ge(win_in[j % 2], 16 * (j // 2 + 1))
                unit(n, [(hT[:, c, t * P:(t + 1) * P], win[:, j % 2, c, :]) for c in range(KC)])
                if 1 <= n <= 2 * NT:
                    qk_T_(n - 1)

            def z_unit(k):
                j = 3 + k // RC
                if k % RC == 0:
                    eng.wait_ge(win_in[j % 2], 16 * (j // 2 + 1))
                c0 = (k % RC) * P
                unit(ring_at[("Z", k)], [(win[:, j % 2, c, c0:c0 + P], hT[:, c, :]) for c in range(KC)])

            def scores_(s):
                i, hh = divmod(s, H)
                nk = (i + 1) * P
                if s >= 2:
                    eng.wait_ge(att_exp, 2 * (s - 1))
                for c in range(2):
                    a, b = c * HALF, (c + 1) * HALF
                    pe.matmul(PS[:, 2 + 2 * (s % 2) + c, 0:nk], qT[a:b, hh, i * P:(i + 1) * P], kT[a:b, hh, 0:nk],
                              start=True, stop=True).then_inc(att_s, 1)

            def w_T(s):
                eng.wait_ge(att_w, s + 1)
                if s >= 2:
                    eng.wait_ge(att_o, 2 * (s - 1))
                for kb in range(s // H + 1):
                    mm = pe.transpose(PS[:, 6 + s % 2, kb * P:(kb + 1) * P], wb[:, s % 2, kb * P:(kb + 1) * P], ident[:, :])
                mm.then_inc(att_t, 1)

            def pv(s):
                i, hh = divmod(s, H)
                eng.wait_ge(att_wt, s + 1)
                for kb in range(i + 1):
                    mm = pe.matmul(PS[:, 6 + s % 2, 0:DV], wT[:, s % 2, kb * P:(kb + 1) * P],
                                   vv[:, kb, hh * DV:(hh + 1) * DV], start=(kb == 0), stop=(kb == i))
                mm.then_inc(att_pv, 1)

            eng.wait_ge(qk_evac, 2 * NT)
            eng.wait_ge(bd_in, 64)
            for k in range(NSLOT):
                if k < 2 * RC:
                    z_unit(k)
                if 1 <= k <= RC:
                    eng.wait_ge(rec_conv, k)
                    unit(ring_at[("R", k - 1)], [(wab[:, k - 1, :], xc[:, (k - 1) % 2, :])])
                    unit(ring_at[("I", k - 1)], [(wib[:, k - 1, :], xc[:, (k - 1) % 2, :])])
                if k < 8:
                    scores_(2 * k)
                    scores_(2 * k + 1)
                if k >= 1:
                    for f in (w_T, pv):
                        f(2 * k - 2)
                        f(2 * k - 1)
            eng.wait_ge(z_free, len(ring))
            eng.wait_ge(rec_y, RC)
            for c in range(RC):
                mm = pe.matmul(PS[:, 0, :], ones[:, :], ysq[:, c, :], start=(c == 0), stop=(c == RC - 1))
            mm.then_inc(rec_ss, 1)
            eng.wait_ge(o_norm, 1)
            eng.wait_ge(att_exp, 2 * NS)
            for i in range(NT):
                for hh in range(H):
                    mm = pe.transpose(PS[:, 2 + i, hh * P:(hh + 1) * P], ob[:, H * i + hh, :], ident[:, :])
                mm.then_inc(o_T, 1)

            eng.wait_ge(y_ready, RC + NT)
            eng.wait_ge(win_in[1], 16 * 3)
            eng.wait_ge(win_in[0], 16 * 4)
            for t in range(NT):
                for n in range(HALVES):
                    for c in range(KC):
                        mm = pe.matmul(PS[:, HALVES * t + n, :], yT[:, c, t * P:(t + 1) * P], win[:, (5 + n) % 2, c, :],
                                       start=(c == 0), stop=(c == KC - 1))
                    mm.then_inc(mix_full, 1)

            eng.wait_ge(wr_in, 16)

            def router(t):
                eng.wait_ge(row_evac_a, NT + t + 1)
                eng.wait_ge(row_evac_v, NT + t + 1)
                eng.wait_ge(h1_done, 5)
                for c in range(KC):
                    mm = pe.matmul(PS[:, 4, t * NE:(t + 1) * NE], hT[:, c, t * P:(t + 1) * P], wr[:, c, :],
                                   start=(c == 0), stop=(c == KC - 1))
                mm.then_inc(rt_full, 1)

            for t in range(NT):
                eng.wait_ge(row_done, NT + t + 1)
                row_T_(1, t, rowbuf[:, t % 2, :])
                if t:
                    router(t - 1)
            router(NT - 1)

            def ranks():
                eng.wait_ge(mk_done, 1)
                for t in range(NT):
                    for i in range(t + 1):
                        mm = pe.matmul(PS[:, 5, t * NE:(t + 1) * NE], tri[:, :] if i == t else onesb[:, :], mkb[:, i, :],
                                       start=(i == 0), stop=(i == t))
                    mm.then_inc(rank_full, 1)
                for i in range(NT):
                    mm = pe.matmul(PS[:, 5, NT * NE:NT * NE + NE], onesb[:, :], mkb[:, i, :], start=(i == 0), stop=(i == NT - 1))
                mm.then_inc(rank_full, 1)

            eng.wait_ge(sw_in, 48)
            for t in range(NT + 1):
                if t < NT:
                    if t >= 2:
                        eng.wait_ge(sh_h, t - 1)
                    for c in range(KC):
                        mm = pe.matmul(PS[:, 6 + t % 2, :], hT[:, c, t * P:(t + 1) * P],
                                       wup[3][:, c].rearrange("p w f -> p (w f)"), start=(c == 0), stop=(c == KC - 1))
                    mm.then_inc(sh_up, 1)
                if t == 1:
                    ranks()
                if t:
                    eng.wait_ge(sh_h, t)
                    if t >= 3:
                        eng.wait_ge(sh_hT, t - 2)
                    for c in range(FC):
                        mm = pe.transpose(PS[:, 2 + (t - 1) % 2, c * P:(c + 1) * P],
                                          hb[:, (t - 1) % 2, :].rearrange("p (q c) -> p c q", c=FC)[:, c, :], ident[:, :])
                    mm.then_inc(sh_T, 1)
                    eng.wait_ge(sh_hT, t)
                    for n in range(HALVES):
                        if t >= 2:
                            eng.wait_ge(sh_add, HALVES * (t - 2) + n + 1)
                        for c in range(FC):
                            mm = pe.matmul(PS[:, n, :], hTe[:, (t - 1) % 2, c, :], wdn[3][:, c, n * BANK:(n + 1) * BANK],
                                           start=(c == 0), stop=(c == FC - 1))
                        mm.then_inc(sh_dn, 1)

            def index_sums(e, s, expert=None):
                expert = e if expert is None else expert
                eng.wait_ge(oh_done, e + 1)
                if not isinstance(e, int) or e >= 1:
                    eng.wait_ge(ix_done, 2 * e)
                for c in range(NT):
                    mm = pe.matmul(PS[:, 5, 0:6], ohb[:, s % 2, c, :],
                                   VV[:, c, bass.ds(expert, 1), :].rearrange("p a v -> p (a v)"), start=(c == 0), stop=(c == NT - 1))
                mm.then_inc(ix_full, 1)

            def gathered_T(e, s):
                eng.wait_ge(gathered[s % 2], 16 * (e // 2 + 1) if isinstance(e, int) else (e - s) * 8 + 16 * (s // 2 + 1))
                for j in range(HALVES):
                    if not isinstance(e, int) or e >= 1:
                        eng.wait_ge(tx_evac, HALVES * (e - 1) + j + 1)
                    for c in range(4):
                        mm = pe.transpose(PS[:, 2 + j, c * P:(c + 1) * P],
                                          xg[:, s % 2, :].rearrange("p (q c) -> p c q", c=KC)[:, 4 * j + c, :], ident[:, :])
                    mm.then_inc(tx_full, 1)

            def up(e, s, extra=False):
                eng.wait_ge(tx_evac, HALVES * (e + 1))
                eng.wait_ge(up_in[s], loads(e, s, 2, extra))
                if not isinstance(e, int) or e >= 2:
                    eng.wait_ge(h_done, e - 1)
                for c in range(KC):
                    mm = pe.matmul(PS[:, s % 2, :], xgT[:, s % 2, c, :], wup[s][:, c].rearrange("p w f -> p (w f)"),
                                   start=(c == 0), stop=(c == KC - 1))
                mm.then_inc(up_full, 1)

            def hidden_T(e, s):
                eng.wait_ge(h_done, e + 1)
                if not isinstance(e, int) or e >= 1:
                    eng.wait_ge(ht_evac, e)
                for c in range(FC):
                    mm = pe.transpose(PS[:, 4, c * P:(c + 1) * P],
                                      hb[:, s % 2, :].rearrange("p (q c) -> p c q", c=FC)[:, c, :], ident[:, :])
                mm.then_inc(ht_full, 1)

            def down(e, s, extra=False):
                eng.wait_ge(ht_evac, e + 1)
                eng.wait_ge(dn_in[s], loads(e, s, 1, extra))
                for n in range(HALVES):
                    if not isinstance(e, int) or e >= 1:
                        eng.wait_ge((y_evac_a, y_evac_v)[n], e)
                    for c in range(FC):
                        mm = pe.matmul(PS[:, 6 + n, :], hTe[:, s % 2, c, :], wdn[s][:, c, n * BANK:(n + 1) * BANK],
                                       start=(c == 0), stop=(c == FC - 1))
                    mm.then_inc(dn_full, 1)

            eng.wait_ge(xlist, 1)
            for a in range(2):
                mm = pe.matmul(PS[0:1, 5, a * P:(a + 1) * P], xcol[:, a:a + 1], ident[:, :], start=True, stop=True)
            mm.then_inc(xrow, 1)
            eng.wait_ge(routes, 1)
            eng.wait_ge(sh_add, HALVES * NT)
            eng.wait_ge(sh_h, NT)
            index_sums(0, 0)
            index_sums(1, 1)
            gathered_T(0, 0)
            index_sums(2, 2)

            def turn(e, s, first=False, left=U, listed=None):
                if left > 1:
                    gathered_T(e + 1, (s + 1) % U)
                if left > 3:
                    index_sums(e + 3, (s + 3) % U, listed[e + 3 - NE] if isinstance(e, int) and e + 3 >= NE else None)
                if not first:
                    hidden_T(e - 1, (s - 1) % U)
                up(e, s)
                if not first:
                    down(e - 1, (s - 1) % U)

            for s in range(U):
                turn(s, s, first=(s == 0))
            with eng.Fori(1, NE // U - 1) as i:
                for s in range(U):
                    turn(i * U + s, s)
            listed = [eng.value_load(xtab[0:1, 0, j:j + 1], min_val=0, max_val=NE - 1) for j in range(2)]
            for e in range(NE - U, STEPS):
                turn(e, e % U, left=STEPS - e, listed=listed)
            hidden_T(STEPS - 1, (STEPS - 1) % U)
            down(STEPS - 1, (STEPS - 1) % U)

            def pair(i):
                for j in range(2):
                    e = eng.value_load(xtab[0:1, 0, bass.ds(i * 2 + j, 1)], min_val=0, max_val=NE - 1)
                    index_sums(i * 2 + (NE + j), j, e)
                for j in range(2):
                    gathered_T(i * 2 + (NE + j), j)
                for j in range(2):
                    up(i * 2 + (NE + j), j, extra=True)
                for j in range(2):
                    hidden_T(i * 2 + (NE + j), j)
                    down(i * 2 + (NE + j), j, extra=True)

            extra_steps(eng, pair, lambda steps: eng.wait_ge(dn_full, steps * HALVES), lambda: eng.sem_inc(experts_done_t, 1))

            eng.wait_ge(experts_done_v, 1)
            eng.wait_ge(experts_done_a, 1)
            eng.wait_ge(pw_in, 32)
            for u in range(DPLE // P):
                for t in range(NT):
                    mm = pe.transpose(PS[:, u, t * P:(t + 1) * P],
                                      prow[:, t, :].rearrange("p (q c) -> p c q", c=DPLE // P)[:, u, :], ident[:, :])
                mm.then_inc(p_T, 1)
            eng.wait_ge(p_evac, 2)
            for u in range(NT * HALVES):
                t, n = divmod(u, HALVES)
                if u >= 2:
                    eng.wait_ge(pproj_done, u - 1)
                for c in range(DPLE // P):
                    mm = pe.matmul(PS[:, 6 + u % 2, :], pT[:, c, t * P:(t + 1) * P], wpp[:, c, n * BANK:(n + 1) * BANK],
                                   start=(c == 0), stop=(c == DPLE // P - 1))
                mm.then_inc(pp_full, 1)
            eng.wait_ge(wpg_in, 16)

            def ple_T(t):
                eng.wait_ge(row_done, 2 * NT + t + 1)
                row_T_(2, t, orow[:, t % 2, :])

            def ple_gate(u):
                t, n = divmod(u, HALVES)
                if n == 0:
                    eng.wait_ge(row_evac_a, 2 * NT + t + 1)
                    eng.wait_ge(row_evac_v, 2 * NT + t + 1)
                if u >= 2:
                    eng.wait_ge(pg_sig, u - 1)
                for c in range(KC):
                    mm = pe.matmul(PS[:, 4 + u % 2, :], hT[:, c, t * P:(t + 1) * P], wpg[:, c, n * BANK:(n + 1) * BANK],
                                   start=(c == 0), stop=(c == KC - 1))
                mm.then_inc(pg_full, 1)

            ple_T(0)
            for t in range(NT):
                ple_gate(HALVES * t)
                if t + 1 < NT:
                    ple_T(t + 1)
                ple_gate(HALVES * t + 1)


_INS = ["x", "p", "positions", "ln_mix", "w_in", "conv_w", "conv_b", "w_a", "b_a", "w_i", "b_i", "rg_lambda",
        "g_rec", "lq1", "lk1", "lq2", "lk2", "g_sub", "w_out", "ln_moe", "w_router", "e_bias", "w1", "w3", "w2",
        "ws1", "ws3", "ws2", "ln_ple", "w_ple_gate", "w_ple_proj", "ln_f"]


def kernel(**inputs):
    import numpy as _np
    import concourse.bacc as _bacc
    from concourse import mybir as _mybir
    from concourse.bass_utils import run_bass_kernel_spmd as _run

    nc = _bacc.Bacc("TRN2", target_bir_lowering=False, num_devices=1)
    arrays, args = {}, []
    for name in _INS:
        a = _np.ascontiguousarray(inputs[name])
        if name == "ln_f":
            a = a.reshape(1, D)
        arrays[f"in_{name}_dram"] = a
        args.append(nc.dram_tensor(f"in_{name}_dram", a.shape, _mybir.dt.from_np(a.dtype), kind="ExternalInput").ap())
    args.append(nc.dram_tensor("out_0_dram", (1, T, D), _mybir.dt.float32, kind="ExternalOutput").ap())
    build_layer(nc, *args)
    r = _run(nc, [arrays], core_ids=[0])
    return r.results[0]["out_0_dram"]
```

```python
from contextlib import ExitStack

import numpy as np
import concourse.bass as bass
from concourse import mybir

F32 = mybir.dt.float32
F32R = mybir.dt.float32r
BF16 = mybir.dt.bfloat16
U32 = mybir.dt.uint32
I32 = mybir.dt.int32
ALU = mybir.AluOpType
ACT = mybir.ActivationFunctionType
AX_X = mybir.AxisListType.X

P = 128
T = 512
NT = T // P
D = 1024
KC = D // P
BANK = 512
DR = 512
RC = DR // P
H = 4
HALF = 64
DV = 128
ROPE = 16
RH = ROPE // 2
NE = 64
TOPK = 8
NG = 8
GE = NE // NG
TOPG = 4
F = 256
FC = F // P
DPLE = 256
EPS = 1e-6
LAM_INIT = 0.2
ROUTE_SCALE = 2.5
RG_C = 8.0
NEG = -1.0e30
BIG = 1.0e30
NOWHERE = 8192
CHOICES = TOPK * T
MAXB = T // P
MAXX = 34
WSLOT = 2 * KC * F + FC * D
U = 4
STEPS = NE + 2
GELU_A = 0.044715
GELU_B = 0.7978845608028654


class Chain:

    def __init__(self, eng, sem, base=0):
        self.eng, self.sem, self.base, self.n = eng, sem, base, 0

    def mark(self, ins):
        self.n += 1
        ins.then_inc(self.sem, 1)

    def sync(self):
        self.eng.wait_ge(self.sem, self.base + self.n)

    def link(self, ins):
        self.mark(ins)
        self.sync()


def build_layer(nc, x, p, positions, ln_mix, w_in, conv_w, conv_b, w_a, b_a, w_i, b_i, rg_lambda,
                g_rec, lq1, lk1, lq2, lk2, g_sub, w_out, ln_moe, w_router, e_bias, w1, w3, w2,
                ws1, ws3, ws2, ln_ple, w_ple_gate, w_ple_proj, ln_f, out):
    ctx = ExitStack()
    with ctx:
        def sb(name, shape, dt=F32):
            return ctx.enter_context(nc.sbuf_tensor(name, shape, dt))

        def sem(name):
            return ctx.enter_context(nc.semaphore(name))

        hf_rows = nc.dram_tensor("hf_rows", (T, D), F32, kind="Internal").ap()
        routed = nc.dram_tensor("routed", (CHOICES, D), F32, kind="Internal").ap()

        PS = ctx.enter_context(nc.psum_tensor("PS", [P, 8, BANK], F32))
        h = sb("h", [P, NT, D])
        with ExitStack() as mixer_only:
            def early(name, shape, dt=F32):
                return mixer_only.enter_context(nc.sbuf_tensor(name, shape, dt))

            wraw = early("wraw", [P, 4, 2 * BANK])
            ah = early("ah", [P, KC, T], F32R)
            al = early("al", [P, KC, T], F32R)
            wh = early("wh", [P, 4, 2 * BANK], F32R)
            wl = early("wl", [P, 4, 2 * BANK], F32R)
            MX = early("MX", [P, 7428])
        hT = sb("hT", [P, KC, T])
        WB = sb("WB", [P, U * WSLOT])
        WK = sb("WK", [P, 16384])

        def region(base, at):
            def take(*shape):
                n = int(np.prod(shape))
                v = base[:, at[0]:at[0] + n]
                at[0] += n
                if len(shape) > 1:
                    names = " ".join(f"d{i}" for i in range(len(shape)))
                    v = v.rearrange(f"p ({names}) -> p {names}", **{f"d{i}": s for i, s in enumerate(shape) if i})
                return v
            return take

        wup = [WB[:, s * WSLOT:s * WSLOT + 2 * KC * F].rearrange("p (c w f) -> p c w f", w=2, f=F) for s in range(U)]
        wdn = [WB[:, s * WSLOT + 2 * KC * F:(s + 1) * WSLOT].rearrange("p (c n) -> p c n", n=D) for s in range(U)]

        pre = region(MX, [0])
        wab = pre(RC, P)
        wib = pre(RC, P)
        xr = pre(516)
        xc = pre(2, T)
        rg = pre(T)
        ig = pre(T)
        th = pre(T)
        aa = pre(T)
        gs = pre(T)
        gq = pre(T)
        gt = pre(T)
        qk = pre(2, BANK)
        rp = pre(4, 8, RH)
        ysq = MX[:, 2564:2564 + RC * T].rearrange("p (c t) -> p c t", c=RC)
        wk = region(WK, [0])
        qT = wk(H, T)
        kT = wk(H, T)
        ob = wk(4 * H, DV)
        yT = wk(RC, T)
        vv = wk(NT, BANK)
        pr = wk(2, 2, T)
        wb = wk(2, T)
        wT = wk(2, T)
        at_pr = 2 * H * T + 4 * H * DV + RC * T + NT * BANK
        rowbuf = WK[:, at_pr:at_pr + NT * D].rearrange("p (t n) -> p t n", n=D)
        lk = region(WK, [0])
        xg = lk(2, D)
        xgT = lk(2, KC, P)
        sgb = lk(2, F)
        hb = lk(2, F)
        hTe = lk(2, FC, P)
        yb = lk(2, D)
        onehot = lk(2, NT * P // 2)
        SL = lk(NT, NE)
        VVf = lk(NT * NE * 6 // 2)
        scores = lk(NT, NE)
        rt = region(WK, [12288])
        sel = rt(NT, NE)
        selm = rt(NT, NE)
        mk = rt(NT, NE)
        ww = rt(NT, NE)
        rr = rt(NT, NE)
        cr = rt(NT, NE)
        g8 = rt(NT, NG, 8)
        gsc = rt(NT, 16)
        gtop = rt(NT, 8)
        gthr = rt(NT, 8)
        grep = rt(NT, 16)
        gmask = rt(NT, NG)
        gpen = rt(NT, NG)
        top8 = rt(NT, 8)
        cnt = rt(NE)
        nxe = rt(MAXB - 1, NE)
        xpos = rt(MAXB - 1, NE)
        xeq = rt(MAXB - 1, NE)
        xev = rt(NE)
        xcol = rt(4)
        xsel = rt(MAXB - 1, NE)
        mkb = rt(NT * NE // 2).bitcast(BF16).rearrange("p (t e) -> p t e", e=NE)
        ohb = onehot.bitcast(BF16).rearrange("p r (c s) -> p r c s", s=P)
        VV = VVf.bitcast(BF16).rearrange("p (t e v) -> p t e v", t=NT, v=6)
        planes = WB[:, 0:2 * KC * D].rearrange("p (r j n) -> p r j n", r=2, n=D)
        wpg = WB[:, 2 * KC * D:3 * KC * D].rearrange("p (c n) -> p c n", n=D)
        pk = region(WK, [0])
        pproj = pk(NT, D)
        sg2 = pk(2, BANK)
        orow = pk(2, D)
        gain_f = pk(D)
        pT = pk(DPLE // P, T)
        pk2 = region(WK, [9472])
        prow = pk2(NT, DPLE)
        wpp = pk2(DPLE // P, D)
        wsd = pk2(FC, D)

        ident = sb("ident", [P, P])
        ones = sb("ones", [P, P])
        cmask = sb("cmask", [P, P])
        slots = sb("slots", [P, MAXB + 1, P])
        tri = sb("tri", [P, P], BF16)
        onesb = sb("onesb", [P, P], BF16)
        junk = WK[:, 15360:16384]
        ojunk = sb("ojunk", [P, DV])
        gain = sb("gain", [P, D])
        wr = sb("wr", [P, KC, NE])
        ebias = sb("ebias", [P, NE])
        posi = sb("posi", [P, NT], I32)
        posf = sb("posf", [P, NT])
        ang = sb("ang", [P, 2, NT, RH])
        kk = sb("kk", [P, 2, NT, RH])
        cs = sb("cs", [P, 2, NT, RH])
        cw = sb("cw", [P, 4, RC])
        cols = sb("cols", [P, 6, RC])
        spt = sb("spt", [P, 4, RC])
        lqk = sb("lqk", [P, 4, HALF])
        ljunk = sb("ljunk", [P, 2, HALF])
        lam = sb("lam", [P, 4])
        gsub = sb("gsub", [P, 1])
        ssq = sb("ssq", [P, 4, NT])
        rstd = sb("rstd", [P, 4, NT])
        oss = sb("oss", [P, 4 * H])
        ors = sb("ors", [P, 4 * H])
        rec_rstd = sb("rec_rstd", [P, NT])
        mx = sb("mx", [P, 2, 2])
        nmx = sb("nmx", [P, 2, 2])
        sums = sb("sums", [P, 2, 2])
        rec = sb("rec", [P, 2, 2])
        den = sb("den", [P, NT])
        tlo = sb("tlo", [P, NT])
        pid = sb("pid", [P, 1])
        warm = sb("warm", [P, 1])
        xtab = sb("xtab", [1, 2, P], I32)
        xnum = sb("xnum", [1, 1], I32)
        ixg = sb("ixg", [P, 2], U32)
        ixd = sb("ixd", [P, 4], U32)
        raw = sb("raw", [P, 4, 6])
        wgt = sb("wgt", [P, 4])
        CB, BA, BI, RL, GR, SP8 = range(6)

        x_in = [sem(f"x_in{t}") for t in range(NT)]
        gain_in = sem("gain_in")
        gain_f_in = sem("gain_f_in")
        small_in = sem("small_in")
        bd_in = sem("bd_in")
        raw_in = [sem(f"raw_in{q}") for q in range(4)]
        w_hi = sem("w_hi")
        w_lo_v = sem("w_lo_v")
        w_lo_g = sem("w_lo_g")
        w_read = sem("w_read")
        yh_done = sem("yh_done")
        row_lo = sem("row_lo")
        consts = sem("consts")
        bd_zero = sem("bd_zero")
        ssq_done = sem("ssq_done")
        ms_done = sem("ms_done")
        root_done = sem("root_done")
        sqrt_ready = sem("sqrt_ready")
        row_done = sem("row_done")
        row_T = sem("row_T")
        row_evac_a = sem("row_evac_a")
        row_evac_v = sem("row_evac_v")
        dve = sem("dve_steps")
        positions_in = sem("positions_in")
        rope_ready = sem("rope_ready")
        lam_v = sem("lam_v")
        lam_a = sem("lam_a")
        z_full = sem("z_full")
        z_free = sem("z_free")
        rope_done = sem("rope_done")
        qk_T = sem("qk_T")
        qk_evac = sem("qk_evac")
        att_s = sem("att_s")
        att_max = sem("att_max")
        att_exp = sem("att_exp")
        att_w = sem("att_w")
        att_t = sem("att_t")
        att_wt = sem("att_wt")
        att_pv = sem("att_pv")
        att_o = sem("att_o")
        rec_conv = sem("rec_conv")
        rec_la = sem("rec_la")
        rec_ta = sem("rec_ta")
        rec_q = sem("rec_q")
        rec_m = sem("rec_m")
        rec_h = sem("rec_h")
        gate_sq = sem("gate_sq")
        gate_t = sem("gate_t")
        gate_th = sem("gate_th")
        rec_y = sem("rec_y")
        rec_x = sem("rec_x")
        rec_sq = sem("rec_sq")
        rec_full = sem("rec_full")
        rec_added = sem("rec_added")
        rec_ss = sem("rec_ss")
        mixn_v = sem("mixn_v")
        mixn_a = sem("mixn_a")
        y_ready = sem("y_ready")
        o_norm = sem("o_norm")
        o_T = sem("o_T")
        mix_full = sem("mix_full")
        h1_done = sem("h1_done")
        hf_stored = [sem("hf_stored0"), sem("hf_stored1")]
        rt_full = sem("rt_full")
        rt_sig = sem("rt_sig")
        mk_done = sem("mk_done")
        rank_full = sem("rank_full")
        routes = sem("routes")
        xlist = sem("xlist")
        xrow = sem("xrow")
        wr_in = sem("wr_in")
        sw_in = sem("sw_in")
        sh_up = sem("sh_up")
        sh_sig = sem("sh_sig")
        sh_h = sem("sh_h")
        sh_T = sem("sh_T")
        sh_hT = sem("sh_hT")
        sh_dn = sem("sh_dn")
        sh_add = sem("sh_add")
        xg_zero = sem("xg_zero")
        up_in = [sem(f"up_in{s}") for s in range(U)]
        dn_in = [sem(f"dn_in{s}") for s in range(U)]
        pool_ready = sem("pool_ready")
        oh_done = sem("oh_done")
        ix_full = sem("ix_full")
        ix_done = sem("ix_done")
        dest_done = sem("dest_done")
        gathered = [sem("gathered0"), sem("gathered1")]
        tx_full = sem("tx_full")
        tx_evac = sem("tx_evac")
        up_full = sem("up_full")
        sg_done = sem("sg_done")
        ht_step = sem("ht_step")
        h_done = sem("h_done")
        ht_full = sem("ht_full")
        ht_evac = sem("ht_evac")
        dn_full = sem("dn_full")
        y_evac_a = sem("y_evac_a")
        y_evac_v = sem("y_evac_v")
        scattered = [sem("scattered0"), sem("scattered1")]
        experts_done_v = sem("experts_done_v")
        experts_done_a = sem("experts_done_a")
        experts_done_t = sem("experts_done_t")
        routed_done = sem("routed_done")
        wpg_in = sem("wpg_in")
        pw_in = sem("pw_in")
        plane_in = [[sem(f"plane_in{r}_{g}") for g in range(4)] for r in range(2)]
        pair_added = sem("pair_added")
        sums_done = sem("sums_done")
        pproj_done = sem("pproj_done")
        plane_used = sem("plane_used")
        p_T = sem("p_T")
        p_evac = sem("p_evac")
        pg_full = sem("pg_full")
        pg_sig = sem("pg_sig")
        pp_full = sem("pp_full")
        ple_mul = sem("ple_mul")
        ple_done = sem("ple_done")
        orow_done = sem("orow_done")
        stored = [sem("stored0"), sem("stored1")]

        block = ctx.enter_context(nc.Block())

        ring = [("qkv", n) for n in range(3 * NT)]
        for k in range(2 * RC):
            ring.append(("Z", k))
            if 1 <= k <= RC:
                ring += [("R", k - 1), ("I", k - 1)]
        ring_at = {u: n for n, u in enumerate(ring)}
        NSLOT = 2 * RC + 1
        NS = 4 * H
        ATT_STEPS = [(i, 2 * half + j) for i, half in ((1, 0), (0, 0), (1, 1), (2, 0), (2, 1), (3, 0), (3, 1), (0, 1)) for j in range(2)]
        HALVES = 2
        SH_BANK = (5, 6, 7, 6)
        PROJ_BEFORE = 7

        w_in_v = w_in[0].rearrange("(p c) n -> p c n", c=KC)
        w_out_v = w_out[0].rearrange("(c p) n -> p c n", p=P)
        x_v = x[0].rearrange("(t p) n -> t p n", p=P)
        out_v = out[0].rearrange("(t p) n -> t p n", p=P)
        p_v = p[0, 0].rearrange("(t p) n -> t p n", p=P)
        hf_v = hf_rows.rearrange("(t p) n -> t p n", p=P)
        routed_v = routed.rearrange("(j t p) n -> t p j n", j=TOPK, p=P)
        WIN_COLS = [2 * DR, 2 * DR + 512, 2 * DR + 1024, 0, DR]
        CHUNKS = 7

        def quarter(j, q):
            if j < 5:
                return w_in_v[:, 2 * q:2 * q + 2, WIN_COLS[j]:WIN_COLS[j] + BANK]
            return w_out_v[:, (j - 5) * RC + q, :]

        def quarter_read(eng, j, q):
            if j == 0:
                return
            if q < 3:
                eng.wait_ge(w_read, 3 * (j - 1) + q + 1)
            elif j <= 5:
                eng.wait_ge(z_full, WIN_UNITS[j - 1])
            else:
                eng.wait_ge(rec_full, NT * HALVES)

        WIN_UNITS = [NT, 2 * NT, 3 * NT, ring_at[("Z", RC - 1)] + 1, ring_at[("Z", 2 * RC - 1)] + 1]

        def expert_up(e):
            return (w1[0, bass.ds(e, 1)].rearrange("a (p c) f -> p (a c) f", c=KC),
                    w3[0, bass.ds(e, 1)].rearrange("a (p c) f -> p (a c) f", c=KC))

        def expert_dn(e):
            return w2[0, bass.ds(e, 1)].rearrange("a (p c) n -> p (a c) n", c=FC)

        def scatters_before(e, s):
            return 16 * (e // 2) if isinstance(e, int) else (e - s) * 8 + 16 * (s // 2)

        late = [(2, 0), (2, 1), (2, 2)] + [nt for t in range(3, NT) for nt in ((2, t), (3, t - 3))] + \
            [(3, t) for t in range(NT - 3, NT)]

        def norm_count(n, t):
            return NT * n + t if n < 2 else 2 * NT + late.index((n, t))

        def loads(e, s, dmas, extra):
            if isinstance(e, int):
                return 16 * dmas * (e // U + 1)
            if not extra:
                return (e - s) * (4 * dmas) + 16 * dmas
            return (e - s) * (8 * dmas) + 16 * dmas * (1 - NE // U)

        def extra_steps(eng, stages, finish, tail):
            pairs = eng.value_load(xnum[0:1, 0:1], min_val=0, max_val=MAXX // 2)
            with eng.If(pairs > 1):
                with eng.Fori(1, pairs) as i:
                    stages(i)
                finish(pairs * 2 + NE)
                tail()
            with eng.Else():
                finish(STEPS)
                tail()

        @block.sync
        def _(eng):
            for t in range(NT):
                eng.dma_start(h[:, t, :], x_v[t]).then_inc(x_in[t], 16)

            def load_chunk(j):
                for q in range(4):
                    if j:
                        eng.wait_ge((w_lo_g, w_lo_v)[q % 2], 2 * (j - 1) + q // 2 + 1)
                    dst = wraw[:, q, :].rearrange("p (c n) -> p c n", n=BANK) if j < 5 else wraw[:, q, :]
                    eng.dma_start(dst, quarter(j, q)).then_inc(raw_in[q], 16)

            load_chunk(0)

            def small(dst, src):
                with nc.allow_non_contiguous_dma(reason="small columns"):
                    eng.dma_start(dst, src).then_inc(small_in, 16)

            def rows(dst, src):
                eng.dma_start(dst, src.to_broadcast([P, src.shape[1]])).then_inc(small_in, 16)

            with nc.allow_non_contiguous_dma(reason="a number for each token"):
                eng.dma_start(posi[:, :], positions[0].rearrange("(t p) -> p t", p=P)).then_inc(positions_in, 16)
            for j, v in enumerate((lq1, lk1, lq2, lk2)):
                rows(lqk[:, j, :], v)
            small(cw[:, :, :], conv_w[0].rearrange("w (c p) -> p w c", p=P))
            small(cols[:, CB, :], conv_b[0].rearrange("(c p) -> p c", p=P))
            small(cols[:, BA, :], b_a[0].rearrange("(c b) j -> (b j) c", b=2))
            small(cols[:, BI, :], b_i[0].rearrange("(c b) j -> (b j) c", b=2))
            small(cols[:, RL, :], rg_lambda[0].rearrange("(c p) -> p c", p=P))
            small(cols[:, GR, :], g_rec[0].rearrange("(c p) -> p c", p=P))
            small(gsub[:, :], g_sub[0].rearrange("(d a) -> d a", a=1))
            rows(ebias[:, :], e_bias)
            eng.wait_ge(bd_zero, 2)
            for b in range(2):
                for dst, src in ((wab, w_a), (wib, w_i)):
                    eng.dma_start(dst[b * HALF:(b + 1) * HALF, :, b * HALF:(b + 1) * HALF],
                                  src[0].rearrange("(c b) i j -> b i c j", b=2)[b]).then_inc(bd_in, 16)
            eng.dma_start(wr[:, :, :], w_router[0].rearrange("(p c) e -> p c e", c=KC)).then_inc(wr_in, 16)


            def load_up(e, s):
                for j, src in enumerate(expert_up(e)):
                    eng.dma_start(wup[s][:, :, j, :], src).then_inc(up_in[s], 16)

            def load_dn(e, s):
                eng.dma_start(wdn[s], expert_dn(e)).then_inc(dn_in[s], 16)

            for j in range(1, CHUNKS):
                load_chunk(j)
            def store_row(t):
                eng.wait_ge(row_done, NT + t + 1)
                eng.dma_start(hf_v[t], rowbuf[:, t, :]).then_inc(hf_stored[t % 2], 16)
            eng.wait_ge(rec_ss, 1)
            eng.dma_start(wup[3][:, :, 0, :], ws1[0].rearrange("(p c) f -> p c f", c=KC)).then_inc(sw_in, 16)
            eng.dma_start(wup[3][:, :, 1, :], ws3[0].rearrange("(p c) f -> p c f", c=KC)).then_inc(sw_in, 16)
            for t in range(NT):
                store_row(t)
            eng.wait_ge(mix_full, NT * HALVES)
            for s in range(3):
                load_up(s, s)
                load_dn(s, s)
            eng.wait_ge(sh_up, NT)
            eng.wait_ge(gathered[1], 16)
            load_up(3, 3)
            load_dn(3, 3)

            def refill_up(e, s, step):
                up_src = expert_up(e)
                up_read = step - (U - 1) if isinstance(step, int) else eng.snap(step - (U - 1))
                eng.wait_ge(up_full, up_read)
                for j, src in enumerate(up_src):
                    eng.dma_start(wup[s][:, :, j, :], src).then_inc(up_in[s], 16)

            def refill_dn(e, s, step):
                dn_src = expert_dn(e)
                dn_read = (step - (U - 1)) * HALVES if isinstance(step, int) else eng.snap((step - (U - 1)) * HALVES)
                eng.wait_ge(dn_full, dn_read)
                eng.dma_start(wdn[s], dn_src).then_inc(dn_in[s], 16)

            refill_up(U, 0, U)
            with eng.Fori(1, NE // U - 1) as i:
                for s in range(U):
                    e = eng.snap(i * U + s)
                    e_next = eng.snap(e + 1)
                    refill_up(e_next, (s + 1) % U, e_next)
                    refill_dn(e, s, e)
            eng.wait_ge(routes, 1)
            expert_of = list(range(NE)) + [eng.value_load(xtab[0:1, 0, j:j + 1], min_val=0, max_val=NE - 1) for j in range(2)]
            for e in range(NE - U, STEPS):
                if e + 1 < STEPS:
                    refill_up(expert_of[e + 1], (e + 1) % U, e + 1)
                refill_dn(expert_of[e], e % U, e)
            eng.dma_start(wpp, w_ple_proj[0].rearrange("(p c) n -> p c n", c=DPLE // P)).then_inc(pw_in, 16)
            eng.dma_start(prow, p_v.rearrange("t p n -> p t n")).then_inc(pw_in, 16)
            eng.dma_start(wsd, ws2[0].rearrange("(p c) n -> p c n", c=FC)).then_inc(pw_in, 16)
            eng.wait_ge(dn_full, HALVES * NE)
            eng.dma_start(wpg, w_ple_gate[0].rearrange("(p c) n -> p c n", c=KC)).then_inc(wpg_in, 16)
            pairs = eng.value_load(xnum[0:1, 0:1], min_val=0, max_val=MAXX // 2)
            with eng.If(pairs > 1):
                with eng.Fori(1, pairs) as i:
                    for j in range(2):
                        e = eng.value_load(xtab[0:1, 0, bass.ds(i * 2 + j, 1)], min_val=0, max_val=NE - 1)
                        up_src, dn_src = expert_up(e), expert_dn(e)
                        up_read = eng.snap(i * 2 + (NE + j - 1))
                        dn_read = eng.snap(up_read * HALVES)
                        eng.wait_ge(up_full, up_read)
                        for w, src in enumerate(up_src):
                            eng.dma_start(wup[j][:, :, w, :], src).then_inc(up_in[j], 16)
                        eng.wait_ge(dn_full, dn_read)
                        eng.dma_start(wdn[j], dn_src).then_inc(dn_in[j], 16)
            with eng.Else():
                eng.nop()

            eng.wait_ge(experts_done_t, 1)
            eng.wait_ge(routed_done, 2)
            for t in range(NT):
                if t >= 2:
                    eng.wait_ge(plane_used, t - 1)
                for g in range(4):
                    eng.dma_start(planes[:, t % 2, 2 * g:2 * g + 2], routed_v[t][:, 2 * g:2 * g + 2]).then_inc(plane_in[t % 2][g], 16)
            for t in range(NT):
                eng.wait_ge(orow_done, t + 1)
                eng.dma_start(out_v[t], pproj[:, t, :]).then_inc(stored[t % 2], 16)
            for r in range(2):
                eng.wait_ge(stored[r], 16 * NT // 2)

        @block.scalar
        def _(eng):
            act = nc.scalar

            def load_gain(src):
                eng.dma_start(gain[:, :], src.to_broadcast([P, D])).then_inc(gain_in, 16)

            load_gain(ln_mix)
            def squares(n, t):
                if n or t:
                    eng.wait_ge(ssq_done, norm_count(n, t))
                act.activation(junk, h[:, t, :], ACT.Square, accum_out=ssq[:, n, t:t + 1]).then_inc(ssq_done, 1)

            tables = []

            def sqrt_table():
                if tables:
                    eng.wait_ge(sqrt_ready, len(tables))
                act.activation(warm[:, :], ident[:, 0:1], ACT.Sqrt).then_inc(sqrt_ready, 1)
                tables.append(len(tables))

            def root(n, t):
                eng.wait_ge(ms_done, norm_count(n, t) + 1)
                act.activation(rstd[:, n, t:t + 1], rstd[:, n, t:t + 1], ACT.Sqrt).then_inc(root_done, 1)

            def split_hi(j, q):
                eng.wait_ge(raw_in[q], 16 * (j + 1))
                quarter_read(eng, j, q)
                act.activation(wh[:, q, :], wraw[:, q, :], ACT.Copy).then_inc(w_hi, 1)

            def row_evac(n, t):
                eng.wait_ge(row_T, HALVES * (NT * n + t) + 1)
                act.activation((hT if n else ah)[:, 0:4, t * P:(t + 1) * P],
                               PS[:, (2 * t) % 4, :].rearrange("p (c n) -> p c n", n=P), ACT.Copy).then_inc(row_evac_a, 1)

            eng.wait_ge(consts, 1)
            sqrt_table()
            for t in range(NT):
                eng.wait_ge(x_in[t], 16)
                squares(0, t)
                root(0, t)
                if t:
                    row_evac(0, t - 1)
            split_hi(0, 0)
            row_evac(0, NT - 1)
            for q in range(1, 4):
                split_hi(0, q)
            eng.wait_ge(rope_ready, 1)
            act.activation(cs[:, :, :, :], ang[:, :, :, :], ACT.Sin).then_inc(rope_ready, 1)
            eng.wait_ge(lam_v, 3)
            act.activation(lam[:, 2:4], lam[:, 0:2], ACT.Exp).then_inc(lam_a, 1)
            act.activation(spt[:, 1, :], spt[:, 0, :], ACT.Exp).then_inc(lam_a, 1)

            for n in range(3 * NT):
                if n % NT == NT - 1:
                    for q in range(4):
                        split_hi(n // NT + 1, q)
                eng.wait_ge(z_full, n + 1)
                if n < 2 * NT:
                    if n >= 2:
                        eng.wait_ge(qk_T, n - 1)
                    dst = qk[:, n % 2, :]
                else:
                    dst = vv[:, n - 2 * NT, :]
                act.activation(dst, PS[:, n % 2, :], ACT.Copy).then_inc(z_free, 1)

            def evac_z(k):
                n = ring_at[("Z", k)]
                eng.wait_ge(z_full, n + 1)
                if k < RC:
                    if k == 0:
                        eng.wait_ge(bd_zero, 3)
                    else:
                        eng.wait_ge(rec_conv, k)
                    act.activation(xr[:, 3:3 + T], PS[:, n % 2, :], ACT.Copy).then_inc(z_free, 1)
                else:
                    if k > RC:
                        eng.wait_ge(rec_y, k - RC)
                    act.activation(gs, PS[:, n % 2, :], ACT.Copy).then_inc(z_free, 1)
                    eng.wait_ge(z_free, n + 1)
                    act.activation(gq, gs, ACT.Square).then_inc(gate_sq, 1)

            def gates(c):
                for what, dst, bias in (("R", rg, BA), ("I", ig, BI)):
                    n = ring_at[(what, c)]
                    eng.wait_ge(z_full, n + 1)
                    if c:
                        eng.wait_ge(rec_h, c)
                    act.activation(dst, PS[:, n % 2, :], ACT.Sigmoid, bias=cols[:, bias, c:c + 1]).then_inc(z_free, 1)

            def exps(s):
                i = ATT_STEPS[s][0]
                nk = (i + 1) * P
                eng.wait_ge(att_max, s + 1)
                if s >= 2:
                    eng.wait_ge(att_w, s - 1)
                for c in range(2):
                    act.activation(pr[:, s % 2, c, 0:nk], PS[:, 2 + 2 * (s % 2) + c, 0:nk], ACT.Exp,
                                   bias=nmx[:, s % 2, c:c + 1], scale=HALF ** -0.5,
                                   accum_out=sums[:, s % 2, c:c + 1]).then_inc(att_exp, 1)

            def evac_wT(s):
                nk = (ATT_STEPS[s][0] + 1) * P
                eng.wait_ge(att_t, s + 1)
                if s >= 2:
                    eng.wait_ge(att_pv, s - 1)
                act.activation(wT[:, s % 2, 0:nk], PS[:, 6 + s % 2, 0:nk], ACT.Copy).then_inc(att_wt, 1)

            def evac_o(s):
                eng.wait_ge(att_pv, s + 1)
                i, hh = ATT_STEPS[s]
                act.activation(ob[:, H * i + hh, :], PS[:, 6 + s % 2, 0:DV], ACT.Copy).then_inc(att_o, 1)
                if s:
                    eng.wait_ge(att_o, 2 * s)
                act.activation(ojunk[:, :], PS[:, 6 + s % 2, 0:DV], ACT.Square,
                               accum_out=oss[:, H * i + hh:H * i + hh + 1]).then_inc(att_o, 1)

            eng.wait_ge(ssq_done, NT)
            for k in range(NSLOT + 1):
                if k == NSLOT:
                    eng.wait_ge(mixn_v, 1)
                    act.activation(rec_rstd[:, :], rec_rstd[:, :], ACT.Sqrt).then_inc(mixn_a, 1)
                if RC < k <= 2 * RC:
                    eng.wait_ge(gate_t, k - RC)
                    act.activation(gq, gt, ACT.Tanh, scale=GELU_B).then_inc(gate_th, 1)
                if k in (RC - 1, 2 * RC - 1):
                    for q in range(4):
                        split_hi(4 + k // RC, q)
                if k < 2 * RC:
                    evac_z(k)
                if k == 2 * RC:
                    for c in range(RC):
                        eng.wait_ge(rec_y, c + 1)
                        eng.wait_ge(z_full, len(ring))
                        act.activation(ah[:, c, :], yT[:, c, :], ACT.Copy, scale=cols[:, GR, c:c + 1]).then_inc(yh_done, 1)
                if k >= 2:
                    evac_o(2 * k - 4)
                    evac_o(2 * k - 3)
                if 1 <= k <= RC:
                    gates(k - 1)
                if k < 8:
                    exps(2 * k)
                    exps(2 * k + 1)
                if 1 <= k <= RC:
                    c = k - 1
                    eng.wait_ge(rec_la, c + 1)
                    act.activation(th, rg, ACT.Tanh).then_inc(rec_ta, 1)
                    act.activation(aa, rg, ACT.Exp, scale=-1.0).then_inc(rec_ta, 1)
                    eng.wait_ge(rec_ta, 3 * c + 2)
                    act.activation(rg, rg, ACT.Exp, scale=-2.0).then_inc(rec_ta, 1)
                if 1 <= k <= 2 * RC:
                    evac_wT(2 * k - 2)
                    evac_wT(2 * k - 1)
                if 1 <= k <= RC:
                    eng.wait_ge(rec_q, k)
                    act.activation(th, th, ACT.Sqrt).then_inc(rec_m, 1)
            eng.wait_ge(mixn_v, 2)
            act.activation(ors[:, :], ors[:, :], ACT.Sqrt).then_inc(mixn_a, 1)
            for q in range(4):
                split_hi(6, q)

            eng.wait_ge(row_done, NT)
            load_gain(ln_moe)
            for t in range(NT):
                eng.wait_ge(h1_done, HALVES * (t + 1))
                squares(1, t)
                root(1, t)
                if t:
                    row_evac(1, t - 1)
            row_evac(1, NT - 1)
            eng.wait_ge(row_done, 2 * NT)
            load_gain(ln_ple)
            eng.wait_ge(rt_full, NT)
            act.activation(scores, PS[:, 4, 0:NT * NE].rearrange("p (t e) -> p t e", e=NE), ACT.Sigmoid).then_inc(rt_sig, 1)

            for t in range(NT + 1):
                if t < NT:
                    eng.wait_ge(sh_up, t + 1)
                    if t >= 2:
                        eng.wait_ge(sh_h, t - 1)
                    act.activation(sgb[:, t % 2, :], PS[:, SH_BANK[t], 0:F], ACT.Sigmoid).then_inc(sh_sig, 1)
                if t:
                    eng.wait_ge(sh_T, t)
                    act.activation(hT[:, 0:FC, (t - 1) * P:t * P], PS[:, 2 + (t - 1) % 2, 0:F].rearrange("p (c n) -> p c n", n=P),
                                   ACT.Copy).then_inc(sh_hT, 1)

            def tx(e, s):
                for j in range(HALVES):
                    eng.wait_ge(tx_full, HALVES * e + j + 1)
                    if not isinstance(e, int) or e >= 2:
                        eng.wait_ge(up_full, e - 1)
                    act.activation(xgT[:, s % 2, 4 * j:4 * j + 4, :],
                                   PS[:, 2 + j, :].rearrange("p (c n) -> p c n", n=P), ACT.Copy).then_inc(tx_evac, 1)

            def sig(e, s):
                eng.wait_ge(up_full, e + 1)
                if not isinstance(e, int) or e >= 2:
                    eng.wait_ge(h_done, e - 1)
                act.activation(sgb[:, s % 2, :], PS[:, s % 2, 0:F], ACT.Sigmoid).then_inc(sg_done, 1)

            def hidden_evac(e, s):
                eng.wait_ge(ht_full, e + 1)
                if not isinstance(e, int) or e >= 2:
                    eng.wait_ge(dn_full, HALVES * (e - 1))
                act.activation(hTe[:, s % 2], PS[:, 4, 0:F].rearrange("p (c n) -> p c n", n=P), ACT.Copy).then_inc(ht_evac, 1)

            def down_evac(e, s):
                eng.wait_ge(dn_full, HALVES * e + 1)
                if not isinstance(e, int) or e >= 2:
                    eng.wait_ge(scattered[s % 2], scatters_before(e, s))
                eng.wait_ge(dest_done, 2 * e + 2)
                act.activation(yb[:, s % 2, 0:BANK], PS[:, 6, :], ACT.Copy, scale=wgt[:, s:s + 1]).then_inc(y_evac_a, 1)

            def turn(e, s, first=False, last=False):
                if not last:
                    tx(e + 1, (s + 1) % U)
                if not first:
                    hidden_evac(e - 1, (s - 1) % U)
                sig(e, s)
                if not first:
                    down_evac(e - 1, (s - 1) % U)

            eng.wait_ge(sh_h, NT)
            tx(0, 0)
            for s in range(U):
                turn(s, s, first=(s == 0))
            with eng.Fori(1, NE // U - 1) as i:
                for s in range(U):
                    turn(i * U + s, s)
            for s in range(U):
                turn(NE - U + s, s)
            for e in range(NE, STEPS):
                turn(e, e % U, last=(e == STEPS - 1))
            hidden_evac(STEPS - 1, (STEPS - 1) % U)
            down_evac(STEPS - 1, (STEPS - 1) % U)

            def pair(i):
                for stages in ((tx,), (sig,), (hidden_evac, down_evac)):
                    for j in range(2):
                        for stage in stages:
                            stage(i * 2 + (NE + j), j)

            extra_steps(eng, pair, lambda steps: eng.wait_ge(y_evac_a, steps), lambda: eng.sem_inc(experts_done_a, 1))

            eng.wait_ge(experts_done_t, 1)
            eng.wait_ge(experts_done_v, 1)
            eng.wait_ge(routed_done, 2)
            eng.dma_start(gain_f, ln_f.to_broadcast([P, D])).then_inc(gain_f_in, 16)
            def proj_evac(u):
                t, n = divmod(u, HALVES)
                eng.wait_ge(pp_full, u + 1)
                act.activation(pproj[:, t, n * BANK:(n + 1) * BANK], PS[:, 6 + u % 2, :], ACT.Copy).then_inc(pproj_done, 1)

            for u in range(PROJ_BEFORE - 2):
                proj_evac(u)

            def gate(u):
                eng.wait_ge(pg_full, u + 1)
                if u >= 2:
                    eng.wait_ge(ple_done, u - 1)
                act.activation(sg2[:, u % 2, :], PS[:, 4 + u % 2, :], ACT.Sigmoid).then_inc(pg_sig, 1)

            def last_norm(t):
                eng.wait_ge(ple_done, HALVES * (t + 1))
                squares(3, t)
                root(3, t)

            sqrt_table()
            eng.wait_ge(sums_done, 1)
            squares(2, 0)
            root(2, 0)
            for u in range(PROJ_BEFORE - 2, PROJ_BEFORE):
                proj_evac(u)
            row_evac(2, 0)
            for u in range(PROJ_BEFORE, NT * HALVES):
                proj_evac(u)
            eng.wait_ge(sums_done, 2)
            squares(2, 1)
            root(2, 1)
            for t in range(NT):
                gate(HALVES * t)
                if t + 1 < NT:
                    row_evac(2, t + 1)
                if t + 2 < NT:
                    eng.wait_ge(sums_done, t + 3)
                    squares(2, t + 2)
                    root(2, t + 2)
                gate(HALVES * t + 1)
                if t:
                    last_norm(t - 1)
            sqrt_table()
            last_norm(NT - 1)

        @block.vector
        def _(eng):
            v = nc.vector
            ch = Chain(eng, dve)

            def mean_square(n, t):
                eng.wait_ge(ssq_done, norm_count(n, t) + 1)
                v.tensor_scalar(rstd[:, n, t:t + 1], ssq[:, n, t:t + 1], 1.0 / D, EPS, ALU.mult, ALU.add).then_inc(ms_done, 1)

            def row(n, t, dst):
                eng.wait_ge(root_done, norm_count(n, t) + 1)
                ch.link(v.reciprocal(rstd[:, n, t:t + 1], rstd[:, n, t:t + 1]))
                if n == 3:
                    eng.wait_ge(gain_f_in, 16)
                else:
                    eng.wait_ge(gain_in, 16 * (n + 1))
                return v.scalar_tensor_tensor(out=dst, in0=h[:, t, :], scalar=rstd[:, n, t:t + 1],
                                              in1=gain_f if n == 3 else gain[:, :], op0=ALU.mult, op1=ALU.mult)

            def split_lo(j):
                for q in (1, 3):
                    eng.wait_ge(w_hi, 4 * j + q + 1)
                    v.tensor_tensor(wl[:, q, :], wraw[:, q, :], wh[:, q, :], ALU.subtract).then_inc(w_lo_v, 1)

            def x_evac(t):
                tile = slice(t * P, (t + 1) * P)
                PSa, PSb = (PS[:, (2 * t + j) % 4, :].rearrange("p (c n) -> p c n", n=P) for j in range(2))
                eng.wait_ge(row_T, HALVES * t + 2)
                ch.link(v.tensor_copy(ah[:, 4:8, tile], PSb))
                v.tensor_tensor(al[:, 4:8, tile], PSb, ah[:, 4:8, tile], ALU.subtract).then_inc(row_evac_v, 1)
                eng.wait_ge(row_evac_a, t + 1)
                v.tensor_tensor(al[:, 0:4, tile], PSa, ah[:, 0:4, tile], ALU.subtract).then_inc(row_lo, 1)

            def row_evac(n, t):
                eng.wait_ge(row_T, HALVES * (NT * n + t) + 2)
                v.tensor_copy(hT[:, 4:8, t * P:(t + 1) * P],
                              PS[:, (2 * t + 1) % 4, :].rearrange("p (c n) -> p c n", n=P)).then_inc(row_evac_v, 1)

            for t in range(NT):
                mean_square(0, t)
                row(0, t, rowbuf[:, t, :]).then_inc(row_done, 1)
                if t:
                    x_evac(t - 1)
            x_evac(NT - 1)
            split_lo(0)

            inv = [float(np.float32(500000.0) ** np.float32(-2 * j / ROPE)) for j in range(RH)]
            eng.wait_ge(positions_in, 16)
            ch.link(v.tensor_copy(posf[:, :], posi[:, :]))
            for j in range(RH):
                ch.mark(v.tensor_scalar(ang[:, 0, :, j], posf[:, :], inv[j], None, ALU.mult))
            ch.sync()
            ch.mark(v.tensor_scalar(kk[:, 0], ang[:, 0], float(1 / (2 * np.pi)), 12582912.0, ALU.mult, ALU.add))
            ch.link(v.tensor_scalar(ang[:, 1], ang[:, 0], float(1 / (2 * np.pi)), 0.25, ALU.mult, ALU.add))
            ch.link(v.tensor_scalar(kk[:, 1], ang[:, 1], 12582912.0, None, ALU.add))
            ch.link(v.tensor_scalar(kk[:, :], kk[:, :], 12582912.0, None, ALU.subtract))
            ch.link(v.tensor_copy(ang[:, 1], ang[:, 0]))
            c1, c2 = 6.28125, float(np.float32(2 * np.pi - 6.28125))
            for c in (c1, c2):
                ch.link(v.scalar_tensor_tensor(out=ang[:, :, :, :].rearrange("p a t j -> p (a t j)"),
                                               in0=kk[:, :, :, :].rearrange("p a t j -> p (a t j)"), scalar=-c,
                                               in1=ang[:, :, :, :].rearrange("p a t j -> p (a t j)"), op0=ALU.mult, op1=ALU.add))
            ch.link(v.tensor_scalar(ang[:, 1], ang[:, 1], float(np.pi / 2), None, ALU.add))
            v.tensor_scalar(ang[:, :], ang[:, :], 3.1415925, -3.1415925, ALU.min, ALU.max).then_inc(rope_ready, 1)

            eng.wait_ge(small_in, 16 * 12)
            for j in range(2):
                v.tensor_tensor_reduce(ljunk[:, j, :], lqk[:, 2 * j, :], lqk[:, 2 * j + 1, :], 1.0, 0.0, ALU.mult, ALU.add,
                                       lam[:, j:j + 1]).then_inc(lam_v, 1)
            L = cols[:, RL, :]
            ch.link(v.tensor_scalar(spt[:, 1, :], L, -1.0, None, ALU.mult))
            ch.link(v.tensor_tensor(spt[:, 0, :], L, spt[:, 1, :], ALU.min))
            ch.link(v.tensor_scalar(cols[:, SP8, :], spt[:, 1, :], 0.0, None, ALU.max))
            eng.sem_inc(lam_v, 1)
            eng.wait_ge(lam_a, 2)
            ch.link(v.tensor_tensor(lam[:, 0:1], lam[:, 3:4], lam[:, 2:3], ALU.subtract))
            ch.link(v.tensor_scalar(lam[:, 0:1], lam[:, 0:1], LAM_INIT, None, ALU.subtract))
            y0, s0, s2, acc = spt[:, 1, :], spt[:, 0, :], spt[:, 2, :], spt[:, 3, :]
            ch.link(v.tensor_scalar(s0, y0, 2.0, None, ALU.add))
            ch.link(v.reciprocal(s0, s0))
            ch.link(v.tensor_tensor(s0, s0, y0, ALU.mult))
            ch.link(v.tensor_tensor(s2, s0, s0, ALU.mult))
            ch.link(v.tensor_scalar(acc, s2, 1.0 / 17, 1.0 / 15, ALU.mult, ALU.add))
            for d in (13, 11, 9, 7, 5, 3, 1):
                ch.link(v.tensor_tensor(acc, acc, s2, ALU.mult))
                ch.link(v.tensor_scalar(acc, acc, 1.0 / d, None, ALU.add))
            ch.link(v.tensor_tensor(acc, acc, s0, ALU.mult))
            ch.link(v.scalar_tensor_tensor(out=cols[:, SP8, :], in0=acc, scalar=2.0, in1=cols[:, SP8, :],
                                           op0=ALU.mult, op1=ALU.add))
            ch.link(v.tensor_scalar(cols[:, SP8, :], cols[:, SP8, :], RG_C, None, ALU.mult))
            ch.link(v.tensor_scalar(gsub[:, :], gsub[:, :], 1.0 - LAM_INIT, None, ALU.mult))

            def rope(n):
                t = n % NT
                eng.wait_ge(z_free, n + 1)
                g = qk[:, n % 2, :].rearrange("p (g d) -> p g d", d=HALF)
                x1, x2 = g[:, :, 0:RH], g[:, :, RH:ROPE]
                sn = cs[:, 0, t, :].unsqueeze(1).to_broadcast([P, 8, RH])
                cn = cs[:, 1, t, :].unsqueeze(1).to_broadcast([P, 8, RH])
                if n:
                    eng.wait_ge(rope_done, 2 * n)
                ch.mark(v.tensor_tensor(rp[:, 0], x1, cn, ALU.mult))
                ch.mark(v.tensor_tensor(rp[:, 1], x2, sn, ALU.mult))
                ch.mark(v.tensor_tensor(rp[:, 2], x2, cn, ALU.mult))
                ch.link(v.tensor_tensor(rp[:, 3], x1, sn, ALU.mult))
                v.tensor_tensor(x1, rp[:, 0], rp[:, 1], ALU.subtract).then_inc(rope_done, 1)
                v.tensor_tensor(x2, rp[:, 2], rp[:, 3], ALU.add).then_inc(rope_done, 1)

            def evac_qk(n):
                t = n % NT
                eng.wait_ge(qk_T, n + 1)
                dst = qT if n < NT else kT
                v.tensor_copy(dst[:, :, t * P:(t + 1) * P],
                              PS[:, 2 + n % 2, :].rearrange("p (h n) -> p h n", n=P)).then_inc(qk_evac, 1)

            eng.wait_ge(rope_ready, 2)
            for n in range(2 * NT + 1):
                if n % NT == NT - 1:
                    split_lo(n // NT + 1)
                if n < 2 * NT:
                    rope(n)
                if n:
                    evac_qk(n - 1)
            split_lo(3)

            def conv(k):
                eng.wait_ge(z_free, ring_at[("Z", k)] + 1)
                if k >= 2:
                    eng.wait_ge(rec_x, k - 1)
                o = xc[:, k % 2, :]
                ch.link(v.tensor_scalar(o, xr[:, 0:T], cw[:, 0, k:k + 1], cols[:, CB, k:k + 1], ALU.mult, ALU.add))
                for j in (1, 2):
                    ch.link(v.scalar_tensor_tensor(out=o, in0=xr[:, j:j + T], scalar=cw[:, j, k:k + 1], in1=o,
                                                   op0=ALU.mult, op1=ALU.add))
                v.scalar_tensor_tensor(out=o, in0=xr[:, 3:3 + T], scalar=cw[:, 3, k:k + 1], in1=o,
                                       op0=ALU.mult, op1=ALU.add).then_inc(rec_conv, 1)

            def smax(s):
                i = ATT_STEPS[s][0]
                nk = (i + 1) * P
                b = 2 + 2 * (s % 2)
                eng.wait_ge(att_s, 2 * s + 2)
                diag = PS[:, b:b + 2, i * P:nk]
                ch.link(v.tensor_tensor(diag, diag, cmask[:, :].unsqueeze(1).to_broadcast([P, 2, P]), ALU.add))
                ch.link(v.tensor_reduce(mx[:, s % 2, :], PS[:, b:b + 2, 0:nk], AX_X, ALU.max))
                if s >= 2:
                    eng.wait_ge(att_exp, 2 * (s - 1))
                v.tensor_scalar(nmx[:, s % 2, :], mx[:, s % 2, :], -HALF ** -0.5, None, ALU.mult).then_inc(att_max, 1)

            def combine(s):
                nk = (ATT_STEPS[s][0] + 1) * P
                eng.wait_ge(att_exp, 2 * (s + 1))
                ch.link(v.reciprocal(rec[:, s % 2, :], sums[:, s % 2, :]))
                ch.link(v.tensor_tensor(rec[:, s % 2, 1:2], rec[:, s % 2, 1:2], lam[:, 0:1], ALU.mult))
                if s >= 2:
                    eng.wait_ge(att_t, s - 1)
                w = wb[:, s % 2, 0:nk]
                ch.link(v.tensor_scalar(w, pr[:, s % 2, 0, 0:nk], rec[:, s % 2, 0:1], None, ALU.mult))
                v.scalar_tensor_tensor(out=w, in0=pr[:, s % 2, 1, 0:nk], scalar=rec[:, s % 2, 1:2], in1=w,
                                       op0=ALU.mult, op1=ALU.add).then_inc(att_w, 1)

            def gated(c):
                eng.wait_ge(gate_th, c + 1)
                ch.link(v.scalar_tensor_tensor(out=gq, in0=gq, scalar=1.0, in1=gs, op0=ALU.add, op1=ALU.mult))
                eng.wait_ge(rec_h, RC)
                v.scalar_tensor_tensor(out=yT[:, c, :], in0=gq, scalar=0.5, in1=yT[:, c, :],
                                       op0=ALU.mult, op1=ALU.mult).then_inc(rec_y, 1)

            def gained(c):
                eng.wait_ge(yh_done, c + 1)
                v.scalar_tensor_tensor(out=al[:, c, :], in0=yT[:, c, :], scalar=cols[:, GR, c:c + 1], in1=ah[:, c, :],
                                       op0=ALU.mult, op1=ALU.subtract).then_inc(y_ready, 1)

            for k in range(NSLOT):
                if RC < k <= 2 * RC:
                    gated(k - 1 - RC)
                if k in (RC - 1, 2 * RC - 1):
                    split_lo(4 + k // RC)
                if k < RC:
                    conv(k)
                if k < 8:
                    smax(2 * k)
                    smax(2 * k + 1)
                if 1 <= k <= RC:
                    c = k - 1
                    eng.wait_ge(z_free, ring_at[("I", c)] + 1)
                    v.tensor_scalar(rg, rg, cols[:, SP8, c:c + 1], None, ALU.mult).then_inc(rec_la, 1)
                if k < 8:
                    combine(2 * k)
                    combine(2 * k + 1)
                if k == 2 * RC:
                    for c in range(RC):
                        gained(c)
                if 1 <= k <= RC:
                    c = k - 1
                    eng.wait_ge(rec_ta, 3 * k)
                    v.scalar_tensor_tensor(out=th, in0=rg, scalar=1.0, in1=th, op0=ALU.add, op1=ALU.mult).then_inc(rec_q, 1)
                    eng.wait_ge(rec_x, k)
                    eng.wait_ge(rec_m, k)
                    ch.link(v.tensor_tensor(ig, ig, th, ALU.mult))
                    v.tensor_tensor_scan(yT[:, c, :], aa, ig, 0.0, ALU.mult, ALU.add).then_inc(rec_h, 1)
                if RC <= k < 2 * RC:
                    c = k - RC
                    eng.wait_ge(gate_sq, c + 1)
                    ch.link(v.tensor_scalar(gt, gq, GELU_A, 1.0, ALU.mult, ALU.add))
                    v.tensor_tensor(gt, gt, gs, ALU.mult).then_inc(gate_t, 1)
            eng.wait_ge(rec_ss, 1)
            v.tensor_scalar(rec_rstd[:, :], PS[:, 4, 0:NT], 1.0 / DR, EPS, ALU.mult, ALU.add).then_inc(mixn_v, 1)
            eng.wait_ge(mixn_a, 1)
            ch.link(v.reciprocal(rec_rstd[:, :], rec_rstd[:, :]))

            def rec_residual(u):
                t, n = divmod(u, HALVES)
                eng.wait_ge(rec_full, u + 1)
                hh = h[:, t, n * BANK:(n + 1) * BANK]
                v.scalar_tensor_tensor(out=hh, in0=PS[:, u % 4, :], scalar=rec_rstd[:, t:t + 1], in1=hh,
                                       op0=ALU.mult, op1=ALU.add).then_inc(rec_added, 1)

            rec_residual(0)
            rec_residual(1)
            eng.wait_ge(att_o, 2 * NS)
            v.tensor_scalar(ors[:, :], oss[:, :], 1.0 / DV, EPS, ALU.mult, ALU.add).then_inc(mixn_v, 1)
            eng.wait_ge(mixn_a, 2)
            ch.link(v.reciprocal(ors[:, :], ors[:, :]))
            v.tensor_tensor(ob, ob, ors[:, :].unsqueeze(2).to_broadcast([P, NS, DV]), ALU.mult).then_inc(o_norm, 1)
            for u in range(2, 6):
                rec_residual(u)
            for i in range(NT):
                eng.wait_ge(o_T, i + 1)
                o, oh = PS[:, 4 + i, :].rearrange("p (h n) -> p h n", n=P), ah[:, RC:2 * RC, i * P:(i + 1) * P]
                ch.link(v.tensor_scalar(oh, o, gsub[:, :], None, ALU.mult))
                v.scalar_tensor_tensor(out=al[:, RC:2 * RC, i * P:(i + 1) * P], in0=o, scalar=gsub[:, :], in1=oh,
                                       op0=ALU.mult, op1=ALU.subtract).then_inc(y_ready, 1)
            rec_residual(6)
            split_lo(6)
            rec_residual(7)

            for t in range(NT):
                for n in range(HALVES):
                    u = HALVES * t + n
                    eng.wait_ge(mix_full, u + 1)
                    eng.wait_ge(rec_added, NT * HALVES)
                    hh = h[:, t, n * BANK:(n + 1) * BANK]
                    v.tensor_tensor(hh, hh, PS[:, u, :], ALU.add).then_inc(h1_done, 1)
                mean_square(1, t)
                row(1, t, rowbuf[:, t, :]).then_inc(row_done, 1)
                if t:
                    row_evac(1, t - 1)
            row_evac(1, NT - 1)

            def sh_hidden(t):
                eng.wait_ge(sh_sig, t + 1)
                ch.link(v.tensor_tensor(sgb[:, t % 2, :], sgb[:, t % 2, :], PS[:, SH_BANK[t], 0:F], ALU.mult))
                if t >= 2:
                    eng.wait_ge(sh_T, t - 1)
                v.tensor_tensor(hb[:, t % 2, :], sgb[:, t % 2, :], PS[:, SH_BANK[t], F:2 * F], ALU.mult).then_inc(sh_h, 1)

            def sh_residual(t):
                for n in range(HALVES):
                    eng.wait_ge(sh_dn, HALVES * t + n + 1)
                    hh = h[:, t, n * BANK:(n + 1) * BANK]
                    v.tensor_tensor(hh, hh, PS[:, 2 + (HALVES * t + n) % 4, :], ALU.add).then_inc(sh_add, 1)

            def one_hot(e, s, expert=None, block=0):
                expert = e if expert is None else expert
                if not isinstance(e, int) or e >= 2:
                    eng.wait_ge(ix_full, e - 1)
                v.tensor_tensor(ohb[:, s % 2], slots[:, bass.ds(block, 1), :].to_broadcast([P, NT, P]),
                                SL[:, :, bass.ds(expert, 1)].to_broadcast([P, NT, P]), ALU.is_equal).then_inc(oh_done, 1)

            def indices(e, s, extra=False):
                eng.wait_ge(ix_full, e + 1)
                b = PS[:, 5, 0:6]
                if not isinstance(e, int) or e >= 2:
                    eng.wait_ge(tx_full, HALVES * (e - 1))
                v.tensor_scalar(ixg[:, s % 2:s % 2 + 1], b[:, 1:2], b[:, 0:1], float(NOWHERE), ALU.add, ALU.add).then_inc(ix_done, 1)
                if extra:
                    eng.wait_ge(dest_done, 2 * e - 2)
                elif not isinstance(e, int) or e >= U:
                    eng.wait_ge(dest_done, 2 * e - 2 * (U - 1))
                v.tensor_copy(raw[:, s, :], b).then_inc(ix_done, 1)

            def dest(e, s, extra=False):
                eng.wait_ge(ix_done, 2 * e + 2)
                if extra:
                    eng.wait_ge(y_evac_a, e - 1)
                    eng.wait_ge(y_evac_v, e - 1)
                    eng.wait_ge(scattered[s % 2], scatters_before(e, s))
                elif not isinstance(e, int) or e >= U:
                    eng.wait_ge(y_evac_a, e - (U - 1))
                    eng.wait_ge(y_evac_v, e - (U - 1))
                    eng.wait_ge(scattered[s % 2], scatters_before(e, s) - 16)
                r = raw[:, s, :]
                v.tensor_scalar(ixd[:, s:s + 1], r[:, 2:3], r[:, 0:1], float(NOWHERE), ALU.add, ALU.add).then_inc(dest_done, 1)
                v.tensor_reduce(wgt[:, s:s + 1], r[:, 3:6], AX_X, ALU.add).then_inc(dest_done, 1)

            def act_mul(e, s):
                eng.wait_ge(sg_done, e + 1)
                if not isinstance(e, int) or e >= 2:
                    eng.wait_ge(ht_full, e - 1)
                v.tensor_tensor(hb[:, s % 2, :], sgb[:, s % 2, :], PS[:, s % 2, 0:F], ALU.mult).then_inc(ht_step, 1)
                eng.wait_ge(ht_step, e + 1)
                v.tensor_tensor(hb[:, s % 2, :], hb[:, s % 2, :], PS[:, s % 2, F:2 * F], ALU.mult).then_inc(h_done, 1)

            def down_evac(e, s):
                eng.wait_ge(dn_full, HALVES * e + 2)
                eng.wait_ge(dest_done, 2 * e + 2)
                if not isinstance(e, int) or e >= 2:
                    eng.wait_ge(scattered[s % 2], scatters_before(e, s))
                v.tensor_scalar(yb[:, s % 2, BANK:D], PS[:, 7, :], wgt[:, s:s + 1], None, ALU.mult).then_inc(y_evac_v, 1)

            for r in range(2):
                eng.wait_ge(hf_stored[r], 16 * NT // 2)
            ch.mark(v.memset(gsc[:, :, :], NEG))
            ch.mark(v.memset(gthr[:, :, :], NEG))
            eng.wait_ge(rt_sig, 1)
            ch.link(v.tensor_tensor(sel, scores, ebias[:, :].unsqueeze(1).to_broadcast([P, NT, NE]), ALU.add))
            for t in range(NT):
                for g in range(NG):
                    ch.mark(v.max(g8[:, t, g, :], sel[:, t, g * GE:(g + 1) * GE]))
            ch.sync()
            ch.link(v.tensor_tensor(gsc[:, :, 0:NG], g8[:, :, :, 0], g8[:, :, :, 1], ALU.add))
            for t in range(NT):
                ch.mark(v.max(gtop[:, t, :], gsc[:, t, :]))
            ch.sync()
            ch.link(v.tensor_copy(gthr[:, :, 0:TOPG], gtop[:, :, 0:TOPG]))
            for t in range(NT):
                ch.mark(v.match_replace(grep[:, t, :], gthr[:, t, :], gsc[:, t, :], BIG))
            ch.sync()
            ch.link(v.tensor_scalar(gmask[:, :, :], grep[:, :, 0:NG], BIG / 10, None, ALU.is_ge))
            ch.link(v.tensor_scalar(gpen[:, :, :], gmask[:, :, :], BIG, BIG, ALU.mult, ALU.subtract))
            selg = sel.rearrange("p t (g e) -> p (t g) e", e=GE)
            selmg = selm.rearrange("p t (g e) -> p (t g) e", e=GE)
            ch.link(v.tensor_tensor(selmg, selg, gmask[:, :, :].rearrange("p t g -> p (t g)").unsqueeze(2).to_broadcast([P, NT * NG, GE]), ALU.mult))
            ch.link(v.tensor_tensor(selmg, selmg, gpen[:, :, :].rearrange("p t g -> p (t g)").unsqueeze(2).to_broadcast([P, NT * NG, GE]), ALU.add))
            for t in range(NT):
                ch.mark(v.max(top8[:, t, :], selm[:, t, :]))
            ch.sync()
            for t in range(NT):
                ch.mark(v.match_replace(mk[:, t, :], top8[:, t, :], selm[:, t, :], BIG))
            ch.sync()
            ch.link(v.tensor_scalar(mk, mk, BIG / 10, None, ALU.is_ge))
            v.tensor_copy(mkb, mk).then_inc(mk_done, 1)
            sh_hidden(0)
            ch.link(v.tensor_tensor(ww, mk, scores, ALU.mult))
            ch.link(v.tensor_reduce(den[:, :], ww, AX_X, ALU.add))
            ch.link(v.reciprocal(den[:, :], den[:, :]))
            ch.link(v.tensor_tensor(ww, ww, den[:, :].unsqueeze(2).to_broadcast([P, NT, NE]), ALU.mult))
            ch.link(v.tensor_scalar(ww, ww, ROUTE_SCALE, None, ALU.mult))
            ch.link(v.tensor_copy(VV[:, :, :, 3], ww))
            ch.link(v.tensor_tensor(rr, ww, VV[:, :, :, 3], ALU.subtract))
            ch.link(v.tensor_copy(VV[:, :, :, 4], rr))
            ch.link(v.tensor_tensor(VV[:, :, :, 5], rr, VV[:, :, :, 4], ALU.subtract))
            sh_hidden(1)
            for t in range(NT):
                ch.mark(v.tensor_tensor_scan(cr[:, t, :], ones[:, 0:NE], mk[:, t, :], 0.0, ALU.mult, ALU.add))
            ch.sync()
            ch.link(v.tensor_tensor(cr, cr, mk, ALU.subtract))
            eng.wait_ge(consts, 3)
            for t in range(NT):
                hi = float(256 * (t // 2) - NOWHERE)
                ch.mark(v.tensor_scalar(VV[:, t, :, 0], ones[:, 0:NE], tlo[:, t:t + 1], None, ALU.mult))
                ch.mark(v.memset(VV[:, t, :, 1], hi))
                ch.mark(v.tensor_scalar(VV[:, t, :, 2], cr[:, t, :], float(T), hi, ALU.mult, ALU.add))
            eng.wait_ge(rank_full, NT + 1)
            ch.link(v.scalar_tensor_tensor(out=SL.rearrange("p t e -> p (t e)"), in0=PS[:, 5, 0:NT * NE], scalar=1.0,
                                           in1=mk.rearrange("p t e -> p (t e)"), op0=ALU.add, op1=ALU.mult))
            ch.link(v.tensor_scalar(SL, SL, -1.0, None, ALU.add))
            ch.link(v.tensor_copy(cnt, PS[:, 5, NT * NE:NT * NE + NE]))
            one_hot(0, 0)
            one_hot(1, 1)
            sh_hidden(2)
            indices(0, 0)
            one_hot(2, 2)
            indices(1, 1)
            sh_hidden(3)
            one_hot(3, 3)
            indices(2, 2)
            for b in range(1, MAXB):
                ch.mark(v.tensor_scalar(nxe[:, b - 1, :], cnt, b * P + 0.5, None, ALU.is_ge))
            ch.sync()
            ch.link(v.tensor_tensor(cnt, nxe[:, 0, :], nxe[:, 1, :], ALU.add))
            ch.link(v.tensor_tensor(cnt, cnt, nxe[:, 2, :], ALU.add))
            ch.link(v.tensor_tensor_scan(xev, ones[:, 0:NE], cnt, 0.0, ALU.mult, ALU.add))
            ch.link(v.tensor_tensor(cnt, xev, cnt, ALU.subtract))
            ch.mark(v.tensor_scalar(xcol[:, 2:3], xev[:, NE - 1:NE], 0.5, 0.25, ALU.mult, ALU.add))
            for b in range(1, MAXB):
                ch.mark(v.tensor_scalar(xpos[:, b - 1, :], cnt, float(b - 1), None, ALU.add))
            ch.sync()
            ch.link(v.tensor_scalar(xeq, xpos, pid[:, :], None, ALU.is_equal))
            ch.link(v.tensor_tensor(xeq, xeq, nxe, ALU.mult))
            ch.link(v.tensor_tensor(xsel, xeq, slots[:, 0, 0:NE].unsqueeze(1).to_broadcast([P, MAXB - 1, NE]), ALU.mult))
            ch.link(v.tensor_reduce(xcol[:, 0:1], xsel.rearrange("p b e -> p (b e)"), AX_X, ALU.add))
            for b in range(1, MAXB):
                ch.mark(v.tensor_scalar(xsel[:, b - 1, :], xeq[:, b - 1, :], float(b - MAXB), None, ALU.mult))
            ch.sync()
            ch.link(v.tensor_reduce(xcol[:, 1:2], xsel.rearrange("p b e -> p (b e)"), AX_X, ALU.add))
            v.tensor_scalar(xcol[:, 1:2], xcol[:, 1:2], float(MAXB), None, ALU.add).then_inc(xlist, 1)
            ch.link(v.tensor_copy(xnum[:, :], xcol[0:1, 2:3]))

            def turn(e, s, first=False, left=U + 1, listed=None):
                if left > 4:
                    if isinstance(e, int) and e + 4 >= NE:
                        one_hot(e + 4, s, *listed[e + 4 - NE])
                    else:
                        one_hot(e + 4, s)
                if left > 3:
                    indices(e + 3, (s + 3) % U)
                act_mul(e, s)
                if not first:
                    down_evac(e - 1, (s - 1) % U)
                dest(e, s)

            for s in range(U - 1):
                turn(s, s, first=(s == 0))
            eng.wait_ge(xrow, 1)
            v.tensor_copy(xtab[:, :, :], PS[0:1, 5, 0:2 * P].rearrange("p (a x) -> p a x", a=2)).then_inc(routes, 1)
            ch.sync()
            turn(U - 1, U - 1)
            with eng.Fori(1, NE // U - 1) as i:
                for s in range(U):
                    turn(i * U + s, s)
            listed = [[eng.value_load(xtab[0:1, a, j:j + 1], min_val=0, max_val=(NE - 1, MAXB)[a]) for a in range(2)]
                      for j in range(2)]
            for e in range(NE - U, STEPS):
                turn(e, e % U, left=STEPS - e, listed=listed)
            down_evac(STEPS - 1, (STEPS - 1) % U)

            def pair(i):
                for j in range(2):
                    e = eng.value_load(xtab[0:1, 0, bass.ds(i * 2 + j, 1)], min_val=0, max_val=NE - 1)
                    b = eng.value_load(xtab[0:1, 1, bass.ds(i * 2 + j, 1)], min_val=0, max_val=MAXB)
                    one_hot(i * 2 + (NE + j), j, e, b)
                for j in range(2):
                    indices(i * 2 + (NE + j), j, extra=True)
                for j in range(2):
                    act_mul(i * 2 + (NE + j), j)
                for j in range(2):
                    dest(i * 2 + (NE + j), j, extra=True)
                    down_evac(i * 2 + (NE + j), j)

            extra_steps(eng, pair, lambda steps: eng.wait_ge(y_evac_v, steps), lambda: eng.sem_inc(experts_done_v, 1))

            for u in range(DPLE // P):
                eng.wait_ge(p_T, u + 1)
                v.tensor_copy(pT[:, u, :], PS[:, u, :]).then_inc(p_evac, 1)
            for t in range(NT):
                sh_residual(t)

            def choice_sum(t):
                for j in (0, 2, 4, 6, 7):
                    if j < 6:
                        eng.wait_ge(pair_added, 3 * t + j // 2 + 1)
                    elif j == 6:
                        eng.wait_ge(plane_in[t % 2][3], 16 * (t // 2 + 1))
                    ins = v.tensor_tensor(h[:, t, :], h[:, t, :], planes[:, t % 2, j, :], ALU.add)
                    if j < TOPK - 1:
                        ch.link(ins)
                    else:
                        ins.then_inc(plane_used, 1)
                eng.wait_ge(plane_used, t + 1)
                eng.sem_inc(sums_done, 1)

            def ple_norm(t):
                mean_square(2, t)
                if t >= 2:
                    eng.wait_ge(row_T, HALVES * (2 * NT + t - 1))
                row(2, t, orow[:, t % 2, :]).then_inc(row_done, 1)

            def ple(u):
                t, n = divmod(u, HALVES)
                cols_ = slice(n * BANK, (n + 1) * BANK)
                eng.wait_ge(pg_sig, u + 1)
                eng.wait_ge(pproj_done, u + 1)
                v.tensor_tensor(sg2[:, u % 2, :], sg2[:, u % 2, :], pproj[:, t, cols_], ALU.mult).then_inc(ple_mul, 1)
                eng.wait_ge(ple_mul, u + 1)
                v.tensor_tensor(h[:, t, cols_], h[:, t, cols_], sg2[:, u % 2, :], ALU.add).then_inc(ple_done, 1)

            def last_norm(t):
                mean_square(3, t)
                row(3, t, pproj[:, t, :]).then_inc(orow_done, 1)

            choice_sum(0)
            ple_norm(0)
            row_evac(2, 0)
            choice_sum(1)
            ple_norm(1)
            for t in range(NT):
                ple(HALVES * t)
                if t + 1 < NT:
                    row_evac(2, t + 1)
                if t + 2 < NT:
                    choice_sum(t + 2)
                    ple_norm(t + 2)
                ple(HALVES * t + 1)
                if t:
                    last_norm(t - 1)
            last_norm(NT - 1)

        @block.gpsimd
        def _(eng):
            g = nc.gpsimd
            g.memset(ident[:, :], 0.0).then_inc(bd_zero, 1)
            eng.wait_ge(bd_zero, 1)
            g.memset(wab, 0.0)
            g.memset(wib, 0.0).then_inc(bd_zero, 1)
            g.memset(xr[:, 0:3], 0.0).then_inc(bd_zero, 1)
            g.affine_select(out=ident[:, :], in_=ident[:, :], compare_op=ALU.not_equal, fill=1.0, base=0,
                            pattern=[[-1, P]], channel_multiplier=1).then_inc(consts, 1)
            g.memset(ones[:, :], 1.0)
            g.memset(onesb[:, :], 1.0)
            g.memset(tri[:, :], 1.0)
            g.memset(cmask[:, :], 0.0)
            g.iota(slots[:, :, :], [[P, MAXB + 1], [1, P]], base=0, channel_multiplier=0, allow_small_or_imprecise_dtypes=True)
            g.iota(pid[:, :], [[0, 1]], base=0, channel_multiplier=1, allow_small_or_imprecise_dtypes=True)
            g.iota(tlo[:, :], [[0, 2], [P, 2]], base=0, channel_multiplier=1,
                   allow_small_or_imprecise_dtypes=True).then_inc(consts, 1)
            eng.wait_ge(consts, 2)
            g.affine_select(out=cmask[:, :], in_=cmask[:, :], compare_op=ALU.is_ge, fill=NEG, base=0,
                            pattern=[[-1, P]], channel_multiplier=1)
            g.affine_select(out=tri[:, :], in_=tri[:, :], compare_op=ALU.is_gt, fill=0.0, base=0,
                            pattern=[[1, P]], channel_multiplier=-1).then_inc(consts, 1)
            def split_lo(j):
                for q in (0, 2):
                    eng.wait_ge(w_hi, 4 * j + q + 1)
                    g.tensor_tensor(wl[:, q, :], wraw[:, q, :], wh[:, q, :], ALU.subtract).then_inc(w_lo_g, 1)

            for j in range(4):
                split_lo(j)
            for c in range(RC):
                if c == RC - 2:
                    split_lo(4)
                eng.wait_ge(z_free, ring_at[("I", c)] + 1)
                g.tensor_tensor(ig, ig, xc[:, c % 2, :], ALU.mult).then_inc(rec_x, 1)
            for c in range(RC):
                if c == RC - 1:
                    split_lo(5)
                eng.wait_ge(rec_y, c + 1)
                g.tensor_tensor(ysq[:, c, :], yT[:, c, :], yT[:, c, :], ALU.mult).then_inc(rec_sq, 1)
            split_lo(6)
            eng.wait_ge(mix_full, NT * HALVES)
            g.memset(xg, 0.0).then_inc(xg_zero, 1)

            def gather(e, s):
                eng.wait_ge(ix_done, 2 * e + 2)
                if not isinstance(e, int) or e >= 2:
                    eng.wait_ge(tx_full, HALVES * (e - 1))
                eng.sem_inc(pool_ready, 1)
                g.indirect_dma_start(xg[:, s % 2, :], None, hf_rows,
                                     bass.IndirectOffsetOnAxis(ap=ixg[:, s % 2:s % 2 + 1], axis=0),
                                     bounds_check=T - 1, oob_is_err=False).then_inc(gathered[s % 2], 16)

            def scatter(e, s):
                eng.wait_ge(y_evac_a, e + 1)
                eng.wait_ge(y_evac_v, e + 1)
                eng.sem_inc(pool_ready, 1)
                g.indirect_dma_start(routed, bass.IndirectOffsetOnAxis(ap=ixd[:, s:s + 1], axis=0),
                                     yb[:, s % 2, :], None,
                                     bounds_check=CHOICES - 1, oob_is_err=False).then_inc(scattered[s % 2], 16)

            eng.wait_ge(xg_zero, 1)
            for r in range(2):
                eng.wait_ge(hf_stored[r], 16 * NT // 2)
            gather(0, 0)
            gather(1, 1)
            gather(2, 2)

            def turn(e, s, first=False, left=U):
                if left > 3:
                    gather(e + 3, (s + 3) % U)
                if not first:
                    scatter(e - 1, (s - 1) % U)

            for s in range(U):
                turn(s, s, first=(s == 0))
            with eng.Fori(1, NE // U - 1) as i:
                for s in range(U):
                    turn(i * U + s, s)
            for e in range(NE - U, STEPS):
                turn(e, e % U, left=STEPS - e)
            scatter(STEPS - 1, (STEPS - 1) % U)

            def pair(i):
                for stage in (gather, scatter):
                    for j in range(2):
                        stage(i * 2 + (NE + j), j)

            def all_scattered(steps):
                for r in range(2):
                    eng.wait_ge(scattered[r], steps * 8)
                    eng.sem_inc(routed_done, 1)

            extra_steps(eng, pair, all_scattered, eng.nop)

            for t in range(NT):
                for k in range(3):
                    eng.wait_ge(plane_in[t % 2][k], 16 * (t // 2 + 1))
                    a, b = (planes[:, t % 2, 2 * k + i, :] for i in range(2))
                    g.tensor_tensor(a, a, b, ALU.add).then_inc(pair_added, 1)

        @block.tensor
        def _(eng):
            pe = nc.tensor
            eng.wait_ge(consts, 3)

            def row_T_(n, t, src):
                for j in range(HALVES):
                    b = (2 * t + j) % 4
                    if t >= 2:
                        eng.wait_ge((row_evac_a, row_evac_v)[j], NT * n + t - 1)
                    for c in range(4):
                        mm = pe.transpose(PS[:, b, c * P:(c + 1) * P],
                                          src.rearrange("p (q c) -> p c q", c=KC)[:, 4 * j + c, :], ident[:, :])
                    mm.then_inc(row_T, 1)

            for t in range(NT):
                eng.wait_ge(row_done, t + 1)
                row_T_(0, t, rowbuf[:, t, :])
            eng.wait_ge(row_evac_v, NT)
            eng.wait_ge(row_lo, NT)

            def split_products(bank, j, pairs, first, last):
                for q in range(4):
                    if first:
                        eng.wait_ge((w_lo_g, w_lo_v)[q % 2], 2 * j + q // 2 + 1)
                    for n, ((ahi, alo), (bhi, blo)) in enumerate(pairs[q]):
                        end = q == 3 and n == len(pairs[q]) - 1
                        pe.matmul(PS[:, bank, :], ahi, blo, start=(q == 0 and n == 0), stop=False)
                        pe.matmul(PS[:, bank, :], ahi, bhi, start=False, stop=False)
                        mm = pe.matmul(PS[:, bank, :], alo, bhi, start=False, stop=end)
                    if last and q < 3:
                        mm.then_inc(w_read, 1)
                return mm

            def unit(n, pairs):
                if n >= 2:
                    eng.wait_ge(z_free, n - 1)
                for j, (a, b) in enumerate(pairs):
                    mm = pe.matmul(PS[:, n % 2, :], a, b, start=(j == 0), stop=(j == len(pairs) - 1))
                mm.then_inc(z_full, 1)

            def qk_T_(n):
                eng.wait_ge(rope_done, 2 * n + 2)
                if n >= 2:
                    eng.wait_ge(qk_evac, n - 1)
                for hh in range(H):
                    mm = pe.transpose(PS[:, 2 + n % 2, hh * P:(hh + 1) * P], qk[:, n % 2, hh * P:(hh + 1) * P], ident[:, :])
                mm.then_inc(qk_T, 1)

            for n in range(3 * NT):
                j, t = divmod(n, NT)
                if n >= 2:
                    eng.wait_ge(z_free, n - 1)
                split_products(n % 2, j, [[(tuple(a[:, c, t * P:(t + 1) * P] for a in (ah, al)),
                                            tuple(w[:, q, (c % 2) * BANK:(c % 2 + 1) * BANK] for w in (wh, wl)))
                                           for c in (2 * q, 2 * q + 1)] for q in range(4)],
                               t == 0, t == NT - 1).then_inc(z_full, 1)
                if 1 <= n <= 2 * NT:
                    qk_T_(n - 1)

            def z_unit(k):
                n = ring_at[("Z", k)]
                c0 = (k % RC) * P
                eng.wait_ge(z_free, n - 1)
                split_products(n % 2, 3 + k // RC, [[(tuple(w[:, q, (c % 2) * BANK + c0:(c % 2) * BANK + c0 + P] for w in (wh, wl)),
                                                      tuple(a[:, c, :] for a in (ah, al)))
                                                     for c in (2 * q, 2 * q + 1)] for q in range(4)],
                               k % RC == 0, k % RC == RC - 1).then_inc(z_full, 1)

            def scores_(s):
                i, hh = ATT_STEPS[s]
                nk = (i + 1) * P
                if s >= 2:
                    eng.wait_ge(att_exp, 2 * (s - 1))
                for c in range(2):
                    a, b = c * HALF, (c + 1) * HALF
                    pe.matmul(PS[:, 2 + 2 * (s % 2) + c, 0:nk], qT[a:b, hh, i * P:(i + 1) * P], kT[a:b, hh, 0:nk],
                              start=True, stop=True).then_inc(att_s, 1)

            def w_T(s):
                eng.wait_ge(att_w, s + 1)
                if s >= 2:
                    eng.wait_ge(att_o, 2 * (s - 1))
                for kb in range(ATT_STEPS[s][0] + 1):
                    mm = pe.transpose(PS[:, 6 + s % 2, kb * P:(kb + 1) * P], wb[:, s % 2, kb * P:(kb + 1) * P], ident[:, :])
                mm.then_inc(att_t, 1)

            def pv(s):
                i, hh = ATT_STEPS[s]
                eng.wait_ge(att_wt, s + 1)
                for kb in range(i + 1):
                    mm = pe.matmul(PS[:, 6 + s % 2, 0:DV], wT[:, s % 2, kb * P:(kb + 1) * P],
                                   vv[:, kb, hh * DV:(hh + 1) * DV], start=(kb == 0), stop=(kb == i))
                mm.then_inc(att_pv, 1)

            eng.wait_ge(qk_evac, 2 * NT)
            eng.wait_ge(bd_in, 64)
            for k in range(NSLOT):
                if k < 2 * RC:
                    z_unit(k)
                if k >= 2:
                    pv(2 * k - 4)
                    pv(2 * k - 3)
                if 1 <= k <= RC:
                    eng.wait_ge(rec_conv, k)
                    unit(ring_at[("R", k - 1)], [(wab[:, k - 1, :], xc[:, (k - 1) % 2, :])])
                    unit(ring_at[("I", k - 1)], [(wib[:, k - 1, :], xc[:, (k - 1) % 2, :])])
                if k < 8:
                    scores_(2 * k)
                    scores_(2 * k + 1)
                if k >= 1:
                    w_T(2 * k - 2)
                    w_T(2 * k - 1)
            def mix_half(sem_, bank, u, j):
                t, n = divmod(u, HALVES)
                split_products(bank, j, [[(tuple(a[:, (j - 5) * RC + q, t * P:(t + 1) * P] for a in (ah, al)),
                                           tuple(w[:, q, n * BANK:(n + 1) * BANK] for w in (wh, wl)))] for q in range(4)],
                               u == 0, j == 5 and u == NT * HALVES - 1).then_inc(sem_, 1)

            def rec_half(u):
                if u >= 4:
                    eng.wait_ge(rec_added, u - 3)
                mix_half(rec_full, u % 4, u, 5)

            eng.wait_ge(z_free, len(ring))
            eng.wait_ge(att_exp, 2 * NS)
            eng.wait_ge(rec_sq, RC)
            for t in range(NT):
                for c in range(RC):
                    mm = pe.matmul(PS[:, 4, t:t + 1], ysq[:, c, t * P:(t + 1) * P], ones[:, 0:1],
                                   start=(c == 0), stop=(c == RC - 1))
            mm.then_inc(rec_ss, 1)
            eng.wait_ge(y_ready, RC)
            rec_half(0)
            pv(NS - 2)
            pv(NS - 1)
            for u in range(1, 6):
                rec_half(u)
            eng.wait_ge(o_norm, 1)
            for i in range(NT):
                for hh in range(H):
                    mm = pe.transpose(PS[:, 4 + i, hh * P:(hh + 1) * P], ob[:, H * i + hh, :], ident[:, :])
                mm.then_inc(o_T, 1)
            rec_half(6)
            rec_half(7)
            eng.wait_ge(y_ready, RC + NT)
            for u in range(NT * HALVES):
                if u < 4:
                    eng.wait_ge(rec_added, 4 + u + 1)
                mix_half(mix_full, u, u, 6)

            eng.wait_ge(wr_in, 16)

            def router(t):
                eng.wait_ge(row_evac_a, NT + t + 1)
                eng.wait_ge(row_evac_v, NT + t + 1)
                eng.wait_ge(h1_done, 5)
                for c in range(KC):
                    mm = pe.matmul(PS[:, 4, t * NE:(t + 1) * NE], hT[:, c, t * P:(t + 1) * P], wr[:, c, :],
                                   start=(c == 0), stop=(c == KC - 1))
                mm.then_inc(rt_full, 1)

            def sh_up_part(t, chunks):
                for c in chunks:
                    mm = pe.matmul(PS[:, SH_BANK[t], :], hT[:, c, t * P:(t + 1) * P],
                                   wup[3][:, c].rearrange("p w f -> p (w f)"), start=(c == 0), stop=(c == KC - 1))
                if KC - 1 in chunks:
                    mm.then_inc(sh_up, 1)

            def rows_T(t):
                eng.wait_ge(row_done, NT + t + 1)
                row_T_(1, t, rowbuf[:, t, :])

            rows_T(0)
            rows_T(1)
            router(0)
            eng.wait_ge(sw_in, 32)
            eng.wait_ge(h1_done, 6)
            sh_up_part(0, range(KC))
            rows_T(2)
            router(1)
            rows_T(3)
            router(2)
            eng.wait_ge(h1_done, 7)
            sh_up_part(1, range(KC // 2))
            router(3)
            sh_up_part(1, range(KC // 2, KC))
            eng.wait_ge(h1_done, 8)
            sh_up_part(2, range(KC))

            def ranks():
                eng.wait_ge(mk_done, 1)
                eng.wait_ge(sh_h, 1)
                for t in range(NT):
                    for i in range(t + 1):
                        mm = pe.matmul(PS[:, 5, t * NE:(t + 1) * NE], tri[:, :] if i == t else onesb[:, :], mkb[:, i, :],
                                       start=(i == 0), stop=(i == t))
                    mm.then_inc(rank_full, 1)
                for i in range(NT):
                    mm = pe.matmul(PS[:, 5, NT * NE:NT * NE + NE], onesb[:, :], mkb[:, i, :], start=(i == 0), stop=(i == NT - 1))
                mm.then_inc(rank_full, 1)

            def index_sums(e, s, expert=None):
                expert = e if expert is None else expert
                eng.wait_ge(oh_done, e + 1)
                if not isinstance(e, int) or e >= 1:
                    eng.wait_ge(ix_done, 2 * e)
                for c in range(NT):
                    mm = pe.matmul(PS[:, 5, 0:6], ohb[:, s % 2, c, :],
                                   VV[:, c, bass.ds(expert, 1), :].rearrange("p a v -> p (a v)"), start=(c == 0), stop=(c == NT - 1))
                mm.then_inc(ix_full, 1)

            def sh_hidden_T(t):
                eng.wait_ge(sh_h, t + 1)
                if t >= 2:
                    eng.wait_ge(sh_hT, t - 1)
                for c in range(FC):
                    mm = pe.transpose(PS[:, 2 + t % 2, c * P:(c + 1) * P],
                                      hb[:, t % 2, :].rearrange("p (q c) -> p c q", c=FC)[:, c, :], ident[:, :])
                mm.then_inc(sh_T, 1)

            ranks()
            sh_hidden_T(0)
            eng.wait_ge(sh_h, 2)
            sh_up_part(3, range(KC // 2))
            index_sums(0, 0)
            sh_hidden_T(1)
            sh_up_part(3, range(KC // 2, KC))
            index_sums(1, 1)
            sh_hidden_T(2)
            sh_hidden_T(3)

            def gathered_T(e, s):
                eng.wait_ge(gathered[s % 2], 16 * (e // 2 + 1) if isinstance(e, int) else (e - s) * 8 + 16 * (s // 2 + 1))
                for j in range(HALVES):
                    if not isinstance(e, int) or e >= 1:
                        eng.wait_ge(tx_evac, HALVES * (e - 1) + j + 1)
                    for c in range(4):
                        mm = pe.transpose(PS[:, 2 + j, c * P:(c + 1) * P],
                                          xg[:, s % 2, :].rearrange("p (q c) -> p c q", c=KC)[:, 4 * j + c, :], ident[:, :])
                    mm.then_inc(tx_full, 1)

            def up(e, s, extra=False):
                eng.wait_ge(tx_evac, HALVES * (e + 1))
                eng.wait_ge(up_in[s], loads(e, s, 2, extra))
                if not isinstance(e, int) or e >= 2:
                    eng.wait_ge(h_done, e - 1)
                for c in range(KC):
                    mm = pe.matmul(PS[:, s % 2, :], xgT[:, s % 2, c, :], wup[s][:, c].rearrange("p w f -> p (w f)"),
                                   start=(c == 0), stop=(c == KC - 1))
                mm.then_inc(up_full, 1)

            def hidden_T(e, s):
                eng.wait_ge(h_done, e + 1)
                if not isinstance(e, int) or e >= 1:
                    eng.wait_ge(ht_evac, e)
                for c in range(FC):
                    mm = pe.transpose(PS[:, 4, c * P:(c + 1) * P],
                                      hb[:, s % 2, :].rearrange("p (q c) -> p c q", c=FC)[:, c, :], ident[:, :])
                mm.then_inc(ht_full, 1)

            def down(e, s, extra=False):
                eng.wait_ge(ht_evac, e + 1)
                eng.wait_ge(dn_in[s], loads(e, s, 1, extra))
                for n in range(HALVES):
                    if not isinstance(e, int) or e >= 1:
                        eng.wait_ge((y_evac_a, y_evac_v)[n], e)
                    for c in range(FC):
                        mm = pe.matmul(PS[:, 6 + n, :], hTe[:, s % 2, c, :], wdn[s][:, c, n * BANK:(n + 1) * BANK],
                                       start=(c == 0), stop=(c == FC - 1))
                    mm.then_inc(dn_full, 1)

            eng.wait_ge(sh_hT, NT)
            gathered_T(0, 0)
            index_sums(2, 2)

            def turn(e, s, first=False, left=U, listed=None):
                if left > 1:
                    gathered_T(e + 1, (s + 1) % U)
                if left > 3:
                    index_sums(e + 3, (s + 3) % U, listed[e + 3 - NE] if isinstance(e, int) and e + 3 >= NE else None)
                if not first:
                    hidden_T(e - 1, (s - 1) % U)
                up(e, s)
                if not first:
                    down(e - 1, (s - 1) % U)

            for s in range(U - 1):
                turn(s, s, first=(s == 0))
            eng.wait_ge(xlist, 1)
            eng.wait_ge(ix_done, 2 * (U + 2))
            for a in range(2):
                mm = pe.matmul(PS[0:1, 5, a * P:(a + 1) * P], xcol[:, a:a + 1], ident[:, :], start=True, stop=True)
            mm.then_inc(xrow, 1)
            eng.wait_ge(routes, 1)
            turn(U - 1, U - 1)
            with eng.Fori(1, NE // U - 1) as i:
                for s in range(U):
                    turn(i * U + s, s)
            listed = [eng.value_load(xtab[0:1, 0, j:j + 1], min_val=0, max_val=NE - 1) for j in range(2)]
            for e in range(NE - U, STEPS):
                turn(e, e % U, left=STEPS - e, listed=listed)
            hidden_T(STEPS - 1, (STEPS - 1) % U)
            down(STEPS - 1, (STEPS - 1) % U)

            def pair(i):
                for j in range(2):
                    e = eng.value_load(xtab[0:1, 0, bass.ds(i * 2 + j, 1)], min_val=0, max_val=NE - 1)
                    index_sums(i * 2 + (NE + j), j, e)
                for j in range(2):
                    gathered_T(i * 2 + (NE + j), j)
                for j in range(2):
                    up(i * 2 + (NE + j), j, extra=True)
                for j in range(2):
                    hidden_T(i * 2 + (NE + j), j)
                    down(i * 2 + (NE + j), j, extra=True)

            extra_steps(eng, pair, lambda steps: eng.wait_ge(dn_full, steps * HALVES), lambda: eng.sem_inc(experts_done_t, 1))

            eng.wait_ge(experts_done_v, 1)
            eng.wait_ge(experts_done_a, 1)
            eng.wait_ge(pw_in, 48)
            for u in range(DPLE // P):
                for t in range(NT):
                    mm = pe.transpose(PS[:, u, t * P:(t + 1) * P],
                                      prow[:, t, :].rearrange("p (q c) -> p c q", c=DPLE // P)[:, u, :], ident[:, :])
                mm.then_inc(p_T, 1)
            for u in range(NT * HALVES):
                t, n = divmod(u, HALVES)
                if u >= 4:
                    eng.wait_ge(sh_add, u - 3)
                for c in range(FC):
                    mm = pe.matmul(PS[:, 2 + u % 4, :], hT[:, c, t * P:(t + 1) * P], wsd[:, c, n * BANK:(n + 1) * BANK],
                                   start=(c == 0), stop=(c == FC - 1))
                mm.then_inc(sh_dn, 1)

            def ple_proj(u):
                t, n = divmod(u, HALVES)
                if u >= 2:
                    eng.wait_ge(pproj_done, u - 1)
                for c in range(DPLE // P):
                    mm = pe.matmul(PS[:, 6 + u % 2, :], pT[:, c, t * P:(t + 1) * P], wpp[:, c, n * BANK:(n + 1) * BANK],
                                   start=(c == 0), stop=(c == DPLE // P - 1))
                mm.then_inc(pp_full, 1)

            eng.wait_ge(p_evac, 2)
            for u in range(PROJ_BEFORE):
                ple_proj(u)
            eng.wait_ge(wpg_in, 16)

            def ple_T(t):
                eng.wait_ge(row_done, 2 * NT + t + 1)
                row_T_(2, t, orow[:, t % 2, :])

            def ple_gate(u):
                t, n = divmod(u, HALVES)
                if n == 0:
                    eng.wait_ge(row_evac_a, 2 * NT + t + 1)
                    eng.wait_ge(row_evac_v, 2 * NT + t + 1)
                if u >= 2:
                    eng.wait_ge(pg_sig, u - 1)
                for c in range(KC):
                    mm = pe.matmul(PS[:, 4 + u % 2, :], hT[:, c, t * P:(t + 1) * P], wpg[:, c, n * BANK:(n + 1) * BANK],
                                   start=(c == 0), stop=(c == KC - 1))
                mm.then_inc(pg_full, 1)

            eng.wait_ge(sh_add, NT * HALVES)
            ple_T(0)
            for u in range(PROJ_BEFORE, NT * HALVES):
                ple_proj(u)
            for t in range(NT):
                ple_gate(HALVES * t)
                if t + 1 < NT:
                    ple_T(t + 1)
                ple_gate(HALVES * t + 1)


_INS = ["x", "p", "positions", "ln_mix", "w_in", "conv_w", "conv_b", "w_a", "b_a", "w_i", "b_i", "rg_lambda",
        "g_rec", "lq1", "lk1", "lq2", "lk2", "g_sub", "w_out", "ln_moe", "w_router", "e_bias", "w1", "w3", "w2",
        "ws1", "ws3", "ws2", "ln_ple", "w_ple_gate", "w_ple_proj", "ln_f"]


def kernel(**inputs):
    import numpy as _np
    import concourse.bacc as _bacc
    from concourse import mybir as _mybir
    from concourse.bass_utils import run_bass_kernel_spmd as _run

    nc = _bacc.Bacc("TRN2", target_bir_lowering=False, num_devices=1)
    arrays, args = {}, []
    for name in _INS:
        a = _np.ascontiguousarray(inputs[name])
        if name == "ln_f":
            a = a.reshape(1, D)
        arrays[f"in_{name}_dram"] = a
        args.append(nc.dram_tensor(f"in_{name}_dram", a.shape, _mybir.dt.from_np(a.dtype), kind="ExternalInput").ap())
    args.append(nc.dram_tensor("out_0_dram", (1, T, D), _mybir.dt.float32, kind="ExternalOutput").ap())
    build_layer(nc, *args)
    r = _run(nc, [arrays], core_ids=[0])
    return r.results[0]["out_0_dram"]
```
